# Optimizing a Trainium2 kernel written in Bass

```python
import math
import jax
import jax.numpy as jnp
from jax import lax
import numpy as np
import jax, jax.numpy as jnp

D_MODEL = 1024
BATCH = 1
SEQ = 512
DEPTH = 2

N_MIXERS = 2
POOL_WINDOWS = (2, 4, 8, 16)
N_POOL_GROUPS = len(POOL_WINDOWS)
POOL_GROUP_DIM = D_MODEL // N_POOL_GROUPS
HEAD_DIM = 64
N_HEADS = D_MODEL // HEAD_DIM
DIL_CONFIGS = ((128, 1), (512, 4), (2048, 16))
N_DIL_GROUPS = len(DIL_CONFIGS)
ATTN_WIDTH = N_HEADS * HEAD_DIM
QKV_WIDTH = N_DIL_GROUPS * 3 * ATTN_WIDTH
D_FF = 2816
MACARON_WEIGHT = 0.5
ALPHA = (2.0 * DEPTH) ** 0.25
BETA = (8.0 * DEPTH) ** -0.25
LN_EPS = 1e-5
MASK_VALUE = -1e30


def _alibi_slopes():
    n = N_DIL_GROUPS * N_HEADS
    s = 2.0 ** (-8.0 * np.arange(1, n + 1) / n)
    return s.reshape(N_DIL_GROUPS, N_HEADS).astype(np.float32)

def _layer_norm(x, g, b):
    x32 = x.astype(jnp.float32)
    mu = jnp.mean(x32, axis=-1, keepdims=True)
    var = jnp.mean(jnp.square(x32 - mu), axis=-1, keepdims=True)
    y = (x32 - mu) * lax.rsqrt(var + LN_EPS)
    return (y * g.astype(jnp.float32) + b.astype(jnp.float32)).astype(x.dtype)

def _swiglu(x, w_gate, w_up, w_down):
    return (jax.nn.silu(x @ w_gate) * (x @ w_up)) @ w_down

def _pool_mixer(x, w_in, w_group, scale, w_out):
    B, S, _ = x.shape
    u = (x @ w_in).reshape(B, S, N_POOL_GROUPS, POOL_GROUP_DIM).astype(jnp.float32)
    csum = jnp.concatenate([jnp.zeros_like(u[:, :1]), jnp.cumsum(u, axis=1)], axis=1)
    half = jnp.asarray([w // 2 for w in POOL_WINDOWS], dtype=jnp.int32)
    t = jnp.arange(S, dtype=jnp.int32)[:, None]
    lo = jnp.clip(t - half[None, :], 0, S)
    hi = jnp.clip(t + half[None, :], 0, S)
    gidx = jnp.arange(N_POOL_GROUPS)[None, :]
    win_sum = csum[:, hi, gidx] - csum[:, lo, gidx]
    mean = win_sum / (hi - lo).astype(jnp.float32)[None, :, :, None]
    mixed = (mean - u).astype(x.dtype)
    y = jnp.einsum('bsgc,gce->bsge', mixed, w_group).reshape(B, S, D_MODEL) * scale
    return y @ w_out

def _dilated_group(q, k, v, window, dilation, slopes):
    B, S, H, E = q.shape
    d = dilation
    L = S // d
    R = window // (2 * d)
    W = R
    nb = -(-L // W)
    Lp = nb * W

    def to_sub(a):
        return a.reshape(B, L, d, H, E).transpose(0, 2, 3, 1, 4)

    qs = jnp.pad(to_sub(q), ((0, 0),) * 3 + ((0, Lp - L), (0, 0))).reshape(B, d, H, nb, W, E)

    def windows(a):
        ap = jnp.pad(to_sub(a), ((0, 0),) * 3 + ((W, W + Lp - L), (0, 0)))
        ap = ap.reshape(B, d, H, nb + 2, W, E)
        return jnp.concatenate([ap[:, :, :, :-2], ap[:, :, :, 1:-1], ap[:, :, :, 2:]], axis=4)

    kw = windows(k)
    vw = windows(v)
    a_idx = jnp.arange(W)
    c_idx = jnp.arange(3 * W)
    n_idx = jnp.arange(nb)
    rel = c_idx[None, :] - W - a_idx[:, None]
    j = (n_idx[:, None, None] - 1) * W + c_idx[None, None, :]
    valid = (jnp.abs(rel)[None] <= R) & (j >= 0) & (j < L)
    dist = (d * jnp.abs(rel)).astype(jnp.float32)
    bias = -slopes[:, None, None] * dist[None]
    scores = jnp.einsum('bdhnqe,bdhnke->bdhnqk', qs.astype(jnp.float32),
                        kw.astype(jnp.float32)) * (E ** -0.5) + bias[:, None]
    scores = jnp.where(valid, scores, MASK_VALUE)
    lse = jax.nn.logsumexp(scores, axis=-1)
    p = jnp.exp(scores - lse[..., None])
    o = jnp.einsum('bdhnqk,bdhnke->bdhnqe', p, vw.astype(jnp.float32))
    o = o.reshape(B, d, H, Lp, E)[:, :, :, :L].transpose(0, 3, 1, 2, 4).reshape(B, S, H, E)
    lse = lse.reshape(B, d, H, Lp)[..., :L].transpose(0, 3, 1, 2).reshape(B, S, H)
    return o, lse

def _dilated_attention_mixer(x, w_qkv, w_out):
    B, S, _ = x.shape
    qkv = (x @ w_qkv).reshape(B, S, N_DIL_GROUPS, 3, N_HEADS, HEAD_DIM)
    slopes = jnp.asarray(_alibi_slopes())
    outs, lses = [], []
    for g, (window, dil) in enumerate(DIL_CONFIGS):
        o, l = _dilated_group(qkv[:, :, g, 0], qkv[:, :, g, 1], qkv[:, :, g, 2],
                              window, dil, slopes[g])
        outs.append(o)
        lses.append(l)
    wts = jax.nn.softmax(jnp.stack(lses), axis=0)
    o = jnp.sum(wts[..., None] * jnp.stack(outs), axis=0)
    return o.reshape(B, S, ATTN_WIDTH).astype(x.dtype) @ w_out

def first_inputs(seed: int = 0) -> dict:
    key = jax.random.key(seed)
    ks = jax.random.split(key, 16)
    n_pool = (DEPTH + 1) // 2
    n_attn = DEPTH // 2
    f32 = jnp.float32

    def nrm(k, shape, scale):
        return jax.random.normal(k, shape, f32) * scale

    return {
        "x": jax.random.normal(ks[0], (BATCH, SEQ, D_MODEL), f32),
        "ffn1_w_gate": nrm(ks[1], (DEPTH, D_MODEL, D_FF), D_MODEL ** -0.5),
        "ffn1_w_up": nrm(ks[2], (DEPTH, D_MODEL, D_FF), D_MODEL ** -0.5),
        "ffn1_w_down": nrm(ks[3], (DEPTH, D_FF, D_MODEL), BETA * D_FF ** -0.5),
        "ffn2_w_gate": nrm(ks[4], (DEPTH, D_MODEL, D_FF), D_MODEL ** -0.5),
        "ffn2_w_up": nrm(ks[5], (DEPTH, D_MODEL, D_FF), D_MODEL ** -0.5),
        "ffn2_w_down": nrm(ks[6], (DEPTH, D_FF, D_MODEL), BETA * D_FF ** -0.5),
        "ln_gain": 1.0 + nrm(ks[7], (DEPTH, 3, D_MODEL), 0.02),
        "ln_bias": nrm(ks[8], (DEPTH, 3, D_MODEL), 0.02),
        "pool_w_in": nrm(ks[9], (n_pool, D_MODEL, D_MODEL), D_MODEL ** -0.5),
        "pool_w_group": nrm(ks[10], (n_pool, N_POOL_GROUPS, POOL_GROUP_DIM, POOL_GROUP_DIM),
                            POOL_GROUP_DIM ** -0.5),
        "pool_scale": 1.0 + nrm(ks[11], (n_pool, D_MODEL), 0.1),
        "pool_w_out": nrm(ks[12], (n_pool, D_MODEL, D_MODEL), BETA * D_MODEL ** -0.5),
        "attn_w_qkv": nrm(ks[13], (n_attn, D_MODEL, QKV_WIDTH), D_MODEL ** -0.5),
        "attn_w_out": nrm(ks[14], (n_attn, ATTN_WIDTH, D_MODEL), BETA * ATTN_WIDTH ** -0.5),
    }

def first_block(x, ffn1_w_gate, ffn1_w_up, ffn1_w_down, ffn2_w_gate, ffn2_w_up, ffn2_w_down,
              ln_gain, ln_bias, pool_w_in, pool_w_group, pool_scale, pool_w_out,
              attn_w_qkv, attn_w_out):
    for i in range(DEPTH):
        h = _swiglu(x, ffn1_w_gate[i], ffn1_w_up[i], ffn1_w_down[i])
        x = _layer_norm(ALPHA * x + MACARON_WEIGHT * h, ln_gain[i, 0], ln_bias[i, 0])
        if i % N_MIXERS == 0:
            p = i // N_MIXERS
            m = _pool_mixer(x, pool_w_in[p], pool_w_group[p], pool_scale[p], pool_w_out[p])
        else:
            a = i // N_MIXERS
            m = _dilated_attention_mixer(x, attn_w_qkv[a], attn_w_out[a])
        x = _layer_norm(ALPHA * x + m, ln_gain[i, 1], ln_bias[i, 1])
        h = _swiglu(x, ffn2_w_gate[i], ffn2_w_up[i], ffn2_w_down[i])
        x = _layer_norm(ALPHA * x + MACARON_WEIGHT * h, ln_gain[i, 2], ln_bias[i, 2])
    return x


N_A = DEPTH // 2
N_B = DEPTH - N_A
N_META = 16
A_EXPAND = 128
A_HEADS = D_MODEL // A_EXPAND
A_DV = D_MODEL // A_HEADS
A_CHUNK = 64
B_HEADS = 16
B_HDIM = D_MODEL // B_HEADS
Q_BLOCK = 128
FG_BIAS_INIT = 2.0
D_FF_2 = ((8 * D_MODEL // 3 + 63) // 64) * 64
CONV_W = 3
EPS = 1e-6


def rmsnorm(x, g):
    xf = x.astype(jnp.float32)
    y = xf * lax.rsqrt(jnp.mean(xf * xf, axis=-1, keepdims=True) + EPS)
    return (y * g.astype(jnp.float32)).astype(x.dtype)

def causal_dwconv(u, w):
    C = u.shape[-1]
    return lax.conv_general_dilated(
        u, w[:, None, :].astype(u.dtype), window_strides=(1,),
        padding=[(CONV_W - 1, 0)], dimension_numbers=("NWC", "WIO", "NWC"),
        feature_group_count=C)

def conv_ffn(x, w_up, conv_w, w_down):
    u = causal_dwconv(x @ w_up, conv_w)
    gate, val = jnp.split(u, 2, axis=-1)
    return (jax.nn.silu(gate) * val) @ w_down

def gla_chunks(q, k, v, logf, s0):
    b = jnp.cumsum(logf, axis=3)
    b_last = b[..., -1:, :]
    q_in = q * jnp.exp(b)
    k_in = k * jnp.exp(-b)
    k_out = k * jnp.exp(b_last - b)
    C = q.shape[3]
    causal = jnp.tril(jnp.ones((C, C), dtype=bool))
    attn = jnp.where(causal, jnp.einsum("bhnck,bhnsk->bhncs", q_in, k_in), 0.0)
    o_intra = jnp.einsum("bhncs,bhnsv->bhncv", attn, v)
    dS = jnp.einsum("bhnck,bhncv->bhnkv", k_out, v)
    decay = jnp.exp(b_last[..., 0, :])

    def step(S, inp):
        d, ds = inp
        return d[..., :, None] * S + ds, S

    S_fin, S_in = lax.scan(step, s0, (jnp.moveaxis(decay, 2, 0), jnp.moveaxis(dS, 2, 0)))
    S_in = jnp.moveaxis(S_in, 0, 2)
    o_inter = jnp.einsum("bhnck,bhnkv->bhncv", q_in, S_in)
    return o_intra + o_inter, S_fin

def hgrn2_mixer(x, w_in, lb, head_gain, w_out):
    Bsz, T, _ = x.shape
    q, f_pre, i, g = jnp.split(x @ w_in, 4, axis=-1)
    f = lb + (1.0 - lb) * jax.nn.sigmoid(f_pre.astype(jnp.float32))
    logf = jnp.log(f)
    k = 1.0 - f

    def heads(t):
        return t.astype(jnp.float32).reshape(Bsz, T, A_HEADS, -1).transpose(0, 2, 1, 3)

    qh, kh, vh, lh = heads(q), heads(k), heads(i), heads(logf)

    def meta_part(t):
        return t[:, :, :N_META][:, :, None]

    def real_part(t):
        return t[:, :, N_META:].reshape(Bsz, A_HEADS, -1, A_CHUNK, t.shape[-1])

    s0 = jnp.zeros((Bsz, A_HEADS, A_EXPAND, A_DV), jnp.float32)
    o_meta, s_meta = gla_chunks(meta_part(qh), meta_part(kh), meta_part(vh), meta_part(lh), s0)
    o_real, _ = gla_chunks(real_part(qh), real_part(kh), real_part(vh), real_part(lh), s_meta)
    o = jnp.concatenate([o_meta.reshape(Bsz, A_HEADS, N_META, A_DV),
                         o_real.reshape(Bsz, A_HEADS, T - N_META, A_DV)], axis=2)
    o = o.transpose(0, 2, 1, 3)
    o = o * lax.rsqrt(jnp.mean(o * o, axis=-1, keepdims=True) + EPS)
    o = o * head_gain.astype(jnp.float32).reshape(A_HEADS, A_DV)
    o = o.reshape(Bsz, T, D_MODEL).astype(x.dtype) * jax.nn.silu(g)
    return o @ w_out

def shared_kv(h, kv_norm, kv_w, fg_b):
    Bsz, T, _ = h.shape
    proj = rmsnorm(h, kv_norm) @ kv_w
    k = proj[..., :D_MODEL].reshape(Bsz, T, B_HEADS, B_HDIM).transpose(0, 2, 1, 3)
    v = proj[..., D_MODEL:2 * D_MODEL].reshape(Bsz, T, B_HEADS, B_HDIM).transpose(0, 2, 1, 3)
    zf = proj[..., 2 * D_MODEL:].astype(jnp.float32) + fg_b.astype(jnp.float32)
    c = jnp.cumsum(jax.nn.log_sigmoid(zf), axis=1).transpose(0, 2, 1)
    return k, v, c

def fox_mixer(x, w_q, w_out, k, v, c):
    Bsz, T, _ = x.shape
    q = (x @ w_q).reshape(Bsz, T, B_HEADS, B_HDIM).transpose(0, 2, 1, 3)
    scale = 1.0 / np.sqrt(B_HDIM).astype(np.float32)
    bounds = [(0, N_META)] + [(N_META + n * Q_BLOCK, N_META + (n + 1) * Q_BLOCK)
                              for n in range((T - N_META) // Q_BLOCK)]
    outs = []
    for s, e in bounds:
        logits = jnp.einsum("bhqd,bhkd->bhqk", q[:, :, s:e], k[:, :, :e]).astype(jnp.float32) * scale
        logits = logits + (c[:, :, s:e, None] - c[:, :, None, :e])
        mask = jnp.arange(s, e)[:, None] >= jnp.arange(e)[None, :]
        p = jax.nn.softmax(jnp.where(mask, logits, -1e30), axis=-1)
        outs.append(jnp.einsum("bhqk,bhkd->bhqd", p.astype(v.dtype), v[:, :, :e]))
    o = jnp.concatenate(outs, axis=2).transpose(0, 2, 1, 3).reshape(Bsz, T, D_MODEL)
    return o @ w_out

def second_inputs(seed: int = 0) -> dict:
    key = jax.random.key(seed)
    ks = jax.random.split(key, 16)
    D = D_MODEL

    def nrm(k, shape, scale):
        return jax.random.normal(k, shape, jnp.float32) * scale

    return {
        "x": nrm(ks[0], (BATCH, SEQ, D), 1.0),
        "meta_tokens": nrm(ks[1], (N_META, D), 1.0),
        "norm_gains": 1.0 + nrm(ks[2], (DEPTH, 4, D), 0.05),
        "a_w_in": nrm(ks[3], (N_A, D, 4 * D), D ** -0.5),
        "a_lb_logits": nrm(ks[4], (N_A + 1, D), 0.1),
        "a_head_norm": 1.0 + nrm(ks[5], (N_A, D), 0.05),
        "a_w_out": nrm(ks[6], (N_A, D, D), D ** -0.5),
        "kv_norm": 1.0 + nrm(ks[7], (D,), 0.05),
        "kv_w": nrm(ks[8], (D, 2 * D + B_HEADS), D ** -0.5),
        "fg_b": FG_BIAS_INIT + nrm(ks[9], (B_HEADS,), 0.1),
        "b_w_q": nrm(ks[10], (N_B, D, D), D ** -0.5),
        "b_w_out": nrm(ks[11], (N_B, D, D), D ** -0.5),
        "ffn_w_up": nrm(ks[12], (DEPTH, D, 2 * D_FF_2), D ** -0.5),
        "ffn_conv": nrm(ks[13], (DEPTH, CONV_W, 2 * D_FF_2), CONV_W ** -0.5),
        "ffn_w_down": nrm(ks[14], (DEPTH, D_FF_2, D), D_FF_2 ** -0.5),
    }

def second_block(x, meta_tokens, norm_gains, a_w_in, a_lb_logits, a_head_norm, a_w_out,
              kv_norm, kv_w, fg_b, b_w_q, b_w_out, ffn_w_up, ffn_conv, ffn_w_down):
    Bsz = x.shape[0]
    meta = jnp.broadcast_to(meta_tokens[None].astype(x.dtype), (Bsz, N_META, D_MODEL))
    h = jnp.concatenate([meta, x], axis=1)
    lb_all = jnp.cumsum(jax.nn.softmax(a_lb_logits.astype(jnp.float32), axis=0), axis=0)
    k_sh = v_sh = c_sh = None
    for l in range(DEPTH):
        g = norm_gains[l]
        hn = rmsnorm(h, g[0])
        if l < N_A:
            mix = hgrn2_mixer(hn, a_w_in[l], lb_all[l], a_head_norm[l], a_w_out[l])
        else:
            if l == N_A:
                k_sh, v_sh, c_sh = shared_kv(h, kv_norm, kv_w, fg_b)
            j = l - N_A
            mix = fox_mixer(hn, b_w_q[j], b_w_out[j], k_sh, v_sh, c_sh)
        h = h + rmsnorm(mix, g[1])
        ff = conv_ffn(rmsnorm(h, g[2]), ffn_w_up[l], ffn_conv[l], ffn_w_down[l])
        h = h + rmsnorm(ff, g[3])
    return h[:, N_META:]


def setup_inputs(seed=0):
    out = dict(first_inputs(seed))
    for name, value in second_inputs(seed + 1).items():
        if name != "x":
            out[name + "_2"] = value
    return out


def reference(
    x, ffn1_w_gate, ffn1_w_up, ffn1_w_down, ffn2_w_gate, ffn2_w_up, ffn2_w_down, ln_gain,
    ln_bias, pool_w_in, pool_w_group, pool_scale, pool_w_out, attn_w_qkv, attn_w_out,
    meta_tokens_2, norm_gains_2, a_w_in_2, a_lb_logits_2, a_head_norm_2, a_w_out_2, kv_norm_2,
    kv_w_2, fg_b_2, b_w_q_2, b_w_out_2, ffn_w_up_2, ffn_conv_2, ffn_w_down_2,
):
    x = first_block(
        x, ffn1_w_gate, ffn1_w_up, ffn1_w_down, ffn2_w_gate, ffn2_w_up, ffn2_w_down, ln_gain,
        ln_bias, pool_w_in, pool_w_group, pool_scale, pool_w_out, attn_w_qkv, attn_w_out,
    )
    return second_block(
        x, meta_tokens_2, norm_gains_2, a_w_in_2, a_lb_logits_2, a_head_norm_2, a_w_out_2,
        kv_norm_2, kv_w_2, fg_b_2, b_w_q_2, b_w_out_2, ffn_w_up_2, ffn_conv_2, ffn_w_down_2,
    )


_drawn_inputs = setup_inputs


def setup_inputs(seed=0):
    import zlib

    import numpy as np

    out = dict(_drawn_inputs(seed))
    spreads = {}
    factors = {}
    for name, (base, spread) in spreads.items():
        noise = np.random.default_rng([zlib.crc32(name.encode()), seed]).standard_normal(out[name].shape)
        drawn = base * np.exp(spread * noise) if base else spread * noise
        out[name] = jnp.asarray(drawn.astype(out[name].dtype))
    for name, factor in factors.items():
        out[name] = (out[name] * factor).astype(out[name].dtype)
    return out
```

```python
from contextlib import ExitStack

import numpy as np

import concourse.bass as bass
from concourse import mybir

F32 = mybir.dt.float32
F32R = mybir.dt.float32r
ACT = mybir.ActivationFunctionType
ALU = mybir.AluOpType
AX_X = mybir.AxisListType.X

P = 128
D = 1024
KD = D // P
S = 512
META = 16
T = S + META
FF = 2816
KF = FF // P
FF2 = 2752
RING = 4
AHEAD = 2
ALPHA = 4.0 ** 0.25
LN_EPS = 1e-5
EPS = 1e-6
POOL_WINDOWS = (2, 4, 8, 16)
PAD = 8
K_CHUNKS = (8, 8, 6)
HEADS = 16
HD = 64
DIL = ((64, 1), (64, 4), (64, 16))
R4 = 4
NI = S // R4
MASKED = -1e30
CH = 64
FG = 32
FOX_JOBS = tuple((0, b) for b in range(5)) + tuple((1, b) for b in (0, 1, 2, 4, 3))
FOX_AT = {-(-16 * (m + 1) // len(FOX_JOBS)): m for m in range(len(FOX_JOBS))}
NCH = S // CH


def param_columns():
    out = {}
    at = 0
    sizes = [(f"ln_{what}{l}{j}", KD) for l in range(2) for j in range(3) for what in ("gain", "bias")]
    sizes += [("pool_scale", KD)]
    sizes += [(f"norm{l}{j}", KD) for l in range(2) for j in range(4)]
    sizes += [(f"conv{l}{part}{tap}", KF) for l in range(2) for part in "gv" for tap in range(3)]
    sizes += [("lb0", KD), ("lb1", KD), ("head_norm", KD), ("kv_norm", KD), ("fg_b", 1)]
    for name, n in sizes:
        out[name] = at
        at += n
    return out, at


PARAM, N_PARAM = param_columns()

C_ID = 0
C_MEAN = C_ID + P
C_POOL = C_MEAN + P
C_NEAR = C_POOL + 4 * S
N_NEAR = S + R4 - 1
C_FAR = C_NEAR + N_NEAR
C_SLOPE = C_FAR + 2 * NI
C_CHUNK = C_SLOPE + HEADS
C_KEEP = C_CHUNK + T
C_CAUSAL = C_KEEP + S
N_CONST = C_CAUSAL + P


def constants():
    c = np.zeros((P, N_CONST), np.float32)
    c[:, C_ID:C_ID + P] = np.eye(P)
    c[:, C_MEAN:C_MEAN + P] = 1.0 / D
    t = np.arange(S)
    for g, w in enumerate(POOL_WINDOWS):
        count = np.minimum(t + w // 2, S) - np.maximum(t - w // 2, 0)
        c[:, C_POOL + g * S:C_POOL + (g + 1) * S] = 1.0 / count
    i = np.arange(P)[:, None]
    dist = np.abs(4 * i - (np.arange(N_NEAR)[None, :] - (R4 - 1)))
    c[:, C_NEAR:C_NEAR + N_NEAR] = np.where(dist <= DIL[0][0], -dist, MASKED)
    steps = np.abs(i - np.arange(NI)[None, :])
    n = 3 * HEADS
    slopes = 2.0 ** (-8.0 * np.arange(1, n + 1) / n)
    near = np.where(steps <= DIL[1][0], -4.0 * steps, MASKED)
    same = np.where(steps % 4 == 0, -4.0 * steps, MASKED)
    c[:, C_FAR:C_FAR + NI] = near * (slopes[HEADS] / slopes[0])
    c[:, C_FAR + NI:C_FAR + 2 * NI] = same * (slopes[2 * HEADS] / slopes[0])
    c[:, C_SLOPE:C_SLOPE + HEADS] = slopes[:HEADS]
    c[:, C_CHUNK:C_CHUNK + T] = 1.0
    c[:, [C_CHUNK] + [C_CHUNK + META + CH * j for j in range(S // CH)]] = 0.0
    q = np.arange(P)[None, :]
    keep = (i // CH == q // CH) & (i <= q)
    c[:, C_KEEP:C_KEEP + S] = np.tile(np.where(keep, np.finfo(np.float32).max, 0.0), (1, S // P))
    c[:, C_CAUSAL:C_CAUSAL + P] = np.where(i >= q, 0.0, MASKED)
    return c


def plan():
    stages = []
    at = dict(u0=0, t0=0, n0=0, g0=0, h0=0, p0=0, x0=0, r0=0, c0=0, j0=0, v0=0, a0=0, s0=0, y0=0)

    def add(kind, counts={}, **more):
        stages.append(dict(kind=kind, **at, **more))
        for key, n in counts.items():
            at[key + "0"] += n

    def norm1(l, j):
        scaled = (l, j) != (1, 2)
        add("layer_norm", dict(n=1, x=KD * scaled, r=KD * scaled), l=l, j=j, scaled=scaled)

    def renorm(after, *outs):
        n_x = sum(to == "x" for _, to in outs)
        add("renorm", dict(v=bool(after) + bool(outs), a=KD * bool(after), s=KD * bool(outs), y=KD * len(outs),
                           x=KD * n_x, h=KD * (len(outs) - n_x)), after=after, outs=outs)

    def project2(units=KD, chunks=(KD,)):
        add("project2", dict(u=units, t=KD, j=1), chunks=chunks)

    def ffn2(l):
        add("glu2", dict(u=2 * KF, t=2 * KF, c=KF, h=KF), l=l)
        project2(3 * KD, K_CHUNKS)

    def ffn1(l, j):
        add("glu", dict(u=2 * KF, t=2 * KF, g=KF, h=KF))
        add("project", dict(u=3 * KD, t=KD, p=KD), source="h", src0=0, chunks=K_CHUNKS, coef=0.5)
        norm1(l, j)

    add("load", dict(x=KD, r=KD))
    ffn1(0, 0)
    add("pool_in", dict(u=KD, t=KD, h=KD))
    add("pool_group", dict(u=2, t=KD, h=KD))
    add("project", dict(u=KD, t=KD, p=KD), source="h", src0=KD, chunks=(KD,), coef=1.0)
    norm1(0, 1)
    ffn1(0, 2)
    ffn1(1, 0)
    add("values1", dict(u=3 * KD, t=3 * KD))
    add("attend1", dict(u=6 * KD, t=6 * KD, x=KD))
    add("project", dict(u=KD, t=KD, p=KD), source="x", src0=0, chunks=(KD,), coef=1.0)
    norm1(1, 1)
    ffn1(1, 2)
    renorm(None, ("norm00", "x"))
    add("hgrn", dict(u=4 * KD, t=4 * KD, h=KD))
    project2()
    renorm("norm01", ("norm02", "x"))
    ffn2(0)
    renorm("norm03", ("kv_norm", "x"), ("norm10", "h"))
    add("fox_values", dict(u=1 + KD, t=1 + KD))
    add("fox", dict(u=2 * KD, t=2 * KD, h=KD))
    project2()
    renorm("norm11", ("norm12", "x"))
    ffn2(1)
    renorm("norm13")
    add("end")
    return stages, at["u0"]


STAGES, UNITS = plan()


def weight_stream(w):
    def tiles(m):
        k, n = m.shape
        return m.reshape(k // P, P, n // P, P).transpose(2, 1, 0, 3)

    units = np.zeros((UNITS, P, KD, P), np.float32)
    at = 0

    def put(u):
        nonlocal at
        units[at, :, :u.shape[1]] = u
        at += 1

    def ffn(gate, up, down):
        g, v, d = tiles(gate), tiles(up), tiles(down)
        for f in range(KF):
            put(g[f])
            put(v[f])
        for n in range(KD):
            k = 0
            for kn in K_CHUNKS:
                put(d[n][:, k:k + kn])
                k += kn

    def every(m):
        for u in tiles(m):
            put(u)

    def ffn1(l, which):
        ffn(w[f"ffn{which}_w_gate"][l], w[f"ffn{which}_w_up"][l], w[f"ffn{which}_w_down"][l])

    ffn1(0, 1)
    every(w["pool_w_in"][0])
    for v in range(2):
        two = [tiles(w["pool_w_group"][0][2 * v + g]) for g in range(2)]
        put(np.concatenate([two[g][e] for g in range(2) for e in range(2)], axis=1))
    every(w["pool_w_out"][0])
    ffn1(0, 2)
    ffn1(1, 1)
    qkv = tiles(w["attn_w_qkv"][0]).reshape(3, 3, KD, P, KD, P)
    for g in range(3):
        for n in range(KD):
            put(qkv[g, 2, n])
    for n in range(KD):
        for g in range(3):
            put(qkv[g, 0, n])
            put(qkv[g, 1, n])
    every(w["attn_w_out"][0])
    ffn1(1, 2)
    parts = tiles(w["a_w_in_2"][0]).reshape(4, KD, P, KD, P)
    for n in range(KD):
        for part in range(4):
            put(parts[part, n])
    every(w["a_w_out_2"][0])

    def ffn2(l):
        both, down = w["ffn_w_up_2"][l], w["ffn_w_down_2"][l]
        wide = [np.zeros((D, FF), np.float32) for _ in range(2)]
        wide[0][:, :FF2], wide[1][:, :FF2] = both[:, :FF2], both[:, FF2:]
        tall = np.zeros((FF, D), np.float32)
        tall[:FF2] = down
        ffn(wide[0], wide[1], tall)

    ffn2(0)
    kv, gates = w["kv_w_2"], np.zeros((D, P), np.float32)
    gates[:, :HEADS] = gates[:, FG:FG + HEADS] = kv[:, 2 * D:]
    put(tiles(gates)[0])
    every(kv[:, D:2 * D])
    k_tiles, q_tiles = tiles(kv[:, :D]), tiles(w["b_w_q_2"][0])
    for n in range(KD):
        put(k_tiles[n])
        put(q_tiles[n])
    every(w["b_w_out_2"][0])
    ffn2(1)
    assert at == UNITS
    return units


def build(nc, wstream, xT, metaT, params, consts, out):
    with ExitStack() as ctx:
        top = [0]

        def at(name, shape, dt=F32, offset=None):
            size = -(-int(np.prod(shape[1:])) * 4 // 64) * 64
            if offset is None:
                offset = top[0]
                top[0] += size
            assert base + offset + size <= nc.sbuf_usable_end, (name, offset, size)
            return nc.alloc_sbuf_tensor_at(name, shape, dt, offset=base + offset)

        def sem(name):
            return ctx.enter_context(nc.semaphore(name))

        base = -(-nc.sbuf_base // 64) * 64

        raw = at("raw", [P, RING, KD, P])
        w_hi = at("w_hi", [P, RING, KD, P], F32R)
        w_lo = at("w_lo", [P, RING, KD, P], F32R)
        res = at("res", [P, KD, T])
        x_hi = at("x_hi", [P, KD, T], F32R)
        x_lo_at = top[0]
        x_lo = at("x_lo", [P, KD, T], F32R)
        par = at("par", [P, N_PARAM])
        ident = at("ident", [P, P])
        mean_w = at("mean_w", [P, P])
        slopes = at("slopes", [P, HEADS])
        stat = at("stat", [P, 8])
        mixer0 = top[0]
        sums = at("sums", [P, 2, T])
        rstd = at("rstd", [P, T])
        pair = at("pair", [P, 2, T])
        upad2 = at("upad2", [P, 2, T + 2])
        hidden0 = top[0]
        h_hi = at("h_hi", [P, KF, T], F32R)
        h_lo = at("h_lo", [P, KF, T], F32R)
        top[0] = hidden0 + 2 * KD * T * 4
        invc = at("invc", [P, 4, S])
        upad = at("upad", [P, 2, PAD + S + PAD])
        assert top[0] <= hidden0 + KF * T * 4
        top[0] = hidden0 + (KF + 2 * KD) * T * 4
        win = at("win", [P, 2, PAD + S + PAD])
        top[0] = mixer0
        val = at("val", [P, R4, 3 * D])
        att = at("att", [P, KD, S])
        qk = at("qk", [P, 2, 6, S])
        prob = at("prob", [P, S + 2 * NI])
        probT = at("probT", [P, S + 2 * NI])
        near = at("near", [P, N_NEAR])
        far = at("far", [P, 2 * NI])
        o_tok = at("o_tok", [P, 2, P])
        vT = at("vT", [P, 2, S], offset=mixer0 + (R4 * 3 * D + KD * S + 2 * 6 * S) * 4)
        mix = at("mix", [P, KD, T], offset=x_lo_at)
        h_mix = at("h_mix", [P, KD, T], offset=hidden0 + KF * T * 4)
        top[0] = hidden0 + KD * T * 4
        g_q = at("g_q", [P, T])
        g_k = at("g_k", [P, T])
        g_b = at("g_b", [P, T])
        g_c = at("g_c", [P, T])
        g_eb = at("g_eb", [P, T])
        g_qin = at("g_qin", [P, T])
        g_kin = at("g_kin", [P, T])
        g_kout = at("g_kout", [P, T])
        g_v = at("g_v", [P, T])
        g_gate = at("g_gate", [P, 2, T])
        g_o = at("g_o", [P, T])
        g_rs = at("g_rs", [P, T])
        assert top[0] <= hidden0 + KF * T * 4
        top[0] = hidden0 + (KF + KD) * T * 4
        g_chunk = at("g_chunk", [P, T])
        g_keep = at("g_keep", [P, 2, S])
        g_kt = at("g_kt", [P, 4, P])
        g_vt = at("g_vt", [P, 4, P])
        g_mt = at("g_mt", [META, 2, P])
        g_at = at("g_at", [P, 4, P])
        g_atm = at("g_atm", [META, META])
        g_state = at("g_state", [P, NCH, P])
        g_lb = at("g_lb", [P, 4, KD])
        top[0] = hidden0 + KD * T * 4
        f_o = at("f_o", [P, KD, T])
        f_qk = at("f_qk", [P, 2, 2, T])
        f_b = at("f_b", [P, 2, T])
        assert top[0] <= hidden0 + KF * T * 4
        top[0] = hidden0 + (KF + KD) * T * 4
        f_val = at("f_val", [P, 4, D])
        f_vmeta = at("f_vmeta", [META, D])
        f_a = at("f_a", [P, T])
        f_c = at("f_c", [P, T])
        f_mask = at("f_mask", [P, P])
        f_otok = at("f_otok", [P, 5, P])
        f_probT = at("f_probT", [P, 2, 5, P], offset=mixer0)
        f_prob = pair
        ps = ctx.enter_context(nc.psum_tensor("ps", [P, 8, 512], F32))

        s_load = [sem(f"s_load{i}") for i in range(RING)]
        s_init = sem("s_init")
        s_tab = sem("s_tab")
        s_hi = sem("s_hi")
        s_lo = sem("s_lo")
        s_unit = sem("s_unit")
        s_evac = sem("s_evac")
        s_silu = sem("s_silu")
        s_hhi = sem("s_hhi")
        s_hlo = sem("s_hlo")
        s_sq = sem("s_sq")
        s_sum = sem("s_sum")
        s_stat = sem("s_stat")
        s_var = sem("s_var")
        s_cen = sem("s_cen")
        s_nrm = sem("s_nrm")
        s_aff = sem("s_aff")
        s_xhi = sem("s_xhi")
        s_xlo = sem("s_xlo")
        s_res = sem("s_res")
        s_pad = sem("s_pad")
        s_win = sem("s_win")
        s_vtr = sem("s_vtr")
        s_val = sem("s_val")
        s_score = sem("s_score")
        s_bias = sem("s_bias")
        s_max = sem("s_max")
        s_exp = sem("s_exp")
        s_pT = sem("s_pT")
        s_pTe = sem("s_pTe")
        s_pv = sem("s_pv")
        s_rec = sem("s_rec")
        s_on = sem("s_on")
        s_oT = sem("s_oT")
        s_oe = sem("s_oe")
        s_mixed = sem("s_mixed")
        s_sum2 = sem("s_sum2")
        s_rst = sem("s_rst")
        s_rv = sem("s_rv")
        s_mx = sem("s_mx")
        s_add = sem("s_add")
        s_sqr = sem("s_sqr")
        s_sqp = sem("s_sqp")
        s_y = sem("s_y")
        s_u = sem("s_u")
        s_zero = sem("s_zero")
        s_cv = sem("s_cv")
        s_gate = sem("s_gate")
        s_h = sem("s_h")
        G = {name: sem("s_g_" + name) for name in (
            "tab", "neg", "lb", "sig", "f", "k", "ln", "c", "eb", "enb", "d", "ed", "qin", "kin", "kout", "turn", "kt",
            "vt", "mt", "score", "clip", "at", "ds", "state", "o", "oe", "sq", "ms", "eps", "lnr", "rs", "og", "oh")}
        FX = {name: sem("s_f_" + name) for name in (
            "tab", "one", "c", "vtr", "val", "b", "score", "max", "exp", "pT", "pTe", "rec", "pv", "on", "oT", "oe")}
        s_out = sem("s_out")

        def two_banks(tok):
            return tok == T

        def psv(slot, tok=S):
            if two_banks(tok):
                return ps[:, 2 * slot:2 * slot + 2, 0:T // 2]
            return ps[:, 2 * slot, 0:S]

        def sbv(ap, tok=S):
            if two_banks(tok):
                return ap.rearrange("p (a b) -> p a b", a=2)
            return ap[:, META:T]

        def halves(tok):
            return [(0, 0, T // 2), (1, T // 2, T // 2)] if two_banks(tok) else [(0, META, S)]

        def par_of(name, k):
            return par[:, PARAM[name] + k:PARAM[name] + k + 1]

        def by_residue(ap):
            return ap.rearrange("p (r i) -> p i r", r=R4)

        def in_order(ap):
            return ap.rearrange("p (i r) -> p i r", r=R4)

        def past(eng, s, n):
            if not (isinstance(n, int) and n < 1):
                eng.wait_ge(s, n)

        def each(eng, st, count, body):
            if st["u0"] + len(st["chunks"]) * KD == UNITS:
                for i in range(count):
                    body(i)
            else:
                with eng.Fori(0, count) as i:
                    body(i)

        NJ = len(FOX_JOBS)

        def back(p, m, lag):
            if isinstance(p, int) and NJ * p + m < lag:
                return None
            return (p, m - lag) if m >= lag else (p - 1, m - lag + NJ)

        def fox_block(b):
            return (META + P * (b - 1), META + P * b) if b else (0, META)

        def out_count(p, m):
            return p * 5 + max(m - 4, 0)

        def by_bank(lo, hi):
            return [(c, min(hi, e) - c, b) for b, c, e in ((0, lo, 512), (1, max(lo, 512), hi)) if c < min(hi, e)]

        block = ctx.enter_context(nc.Block())

        @block.sync
        def _(sp):
            for dst, src in ((par[:, :], params), (ident[:, :], consts[:, C_ID:C_ID + P]),
                             (mean_w[:, :], consts[:, C_MEAN:C_MEAN + P]),
                             (slopes[:, :], consts[:, C_SLOPE:C_SLOPE + HEADS]),
                             (res[:, :, META:T], xT.rearrange("(k p) t -> p k t", p=P)),
                             (res[:, :, 0:META], metaT.rearrange("(k p) t -> p k t", p=P))):
                sp.dma_start(dst, src).then_inc(s_init, 16)
            for u in range(RING):
                sp.dma_start(raw[:, u], wstream[u]).then_inc(s_load[u], 16)
            whole = UNITS // RING
            with sp.Fori(1, whole) as i:
                for j in range(RING):
                    sp.wait_ge(s_lo, i * RING + (j - RING + 1))
                    sp.dma_start(raw[:, j], wstream[bass.ds(i * RING + j, 1)].rearrange("a p k n -> (a p) k n"))\
                        .then_inc(s_load[j], 16)
            for u in range(whole * RING, UNITS):
                sp.wait_ge(s_lo, u - RING + 1)
                sp.dma_start(raw[:, u % RING], wstream[u]).then_inc(s_load[u % RING], 16)
            sp.wait_ge(s_add, STAGES[-1]["a0"])
            sp.dma_start(out.rearrange("(k p) t -> p k t", p=P), res[:, :, META:T]).then_inc(s_out, 16)
            sp.wait_ge(s_out, 16)

        @block.tensor
        def _(pe):
            x_src = (x_hi, x_lo)
            h_src = (h_hi, h_lo)

            def products(bank, slot, wt, src, k, c0, n, first, last):
                hi, lo = src
                for q, (w, x) in enumerate(((w_hi, hi), (w_lo, hi), (w_hi, lo))):
                    m = pe.matmul(ps[:, bank, 0:n], w[:, slot, wt, :], x[:, k, c0:c0 + n],
                                  start=first and q == 0, stop=last and q == 2)
                return m

            def unit(u, slot, tile_slot, tok, src, k0, kn, first=True, last=True, x0=None, between=None):
                pe.wait_ge(s_lo, u + 1)
                for k in range(kn):
                    if x0 is not None:
                        pe.wait_ge(s_xlo, x0 + k + 1)
                    for a, c0, n in halves(tok):
                        m = products(2 * tile_slot + a, slot, k, src, k0 + k, c0, n,
                                     first and k == 0, last and k == kn - 1)
                    if k == kn - 1:
                        m.then_inc(s_unit, 1)
                    if between is not None:
                        between(k)

            def glu(st):
                tok = T if st["kind"] == "glu2" else S

                def body(i):
                    for j in range(4):
                        u, t = st["u0"] + 4 * i + j, st["t0"] + 4 * i + j
                        if not (isinstance(i, int) and t < RING):
                            pe.wait_ge(s_evac, t - RING + 1)
                        unit(u, (st["u0"] + j) % RING, (st["t0"] + j) % RING, tok, x_src, 0, KD,
                             x0=st["x0"] - KD if isinstance(i, int) and j == 0 else None)
                body(0)
                with pe.Fori(1, 2 * KF // 4) as i:
                    body(i)

            def project(st):
                chunks, per, tok = st["chunks"], 4, T if st["kind"] == "project2" else S
                from_x = st.get("source") == "x"
                if not from_x:
                    pe.wait_ge(s_hlo, st["h0"])
                else:
                    pe.wait_ge(s_xlo, st["x0"])
                with pe.Fori(0, KD // per) as i:
                    for n in range(per):
                        t = st["t0"] + per * i + n
                        pe.wait_ge(s_evac, t - RING + 1)
                        k0 = st.get("src0", 0)
                        for c, kn in enumerate(chunks):
                            v = len(chunks) * n + c
                            unit(st["u0"] + len(chunks) * per * i + v, (st["u0"] + v) % RING, (st["t0"] + n) % RING,
                                 tok, x_src if from_x else h_src, k0, kn, c == 0, c == len(chunks) - 1)
                            k0 += kn

            def layer_norm(st):
                for q in range(2):
                    pe.wait_ge(s_sum, (2 * KD + 1) * (st["n0"] + 1) - 1 + q)
                    pe.matmul(ps[:, 5 + 2 * q, 0:S], mean_w[:, :], sums[:, q, META:T], start=True, stop=True)\
                        .then_inc(s_stat, 1)

            def pool_in(st):
                for n in range(KD):
                    u, t = st["u0"] + n, st["t0"] + n
                    pe.wait_ge(s_evac, t - RING + 1)
                    unit(u, u % RING, t % RING, S, x_src, 0, KD, x0=st["x0"] - KD if n == 0 else None)

            def pool_group(st):
                for v in range(2):
                    u = st["u0"] + v
                    pe.wait_ge(s_lo, u + 1)
                    for w in range(KD):
                        n, k = 4 * v + w // 2, 4 * v + 2 * (w // 4) + w % 2
                        t = st["t0"] + n
                        if k % 2 == 0:
                            pe.wait_ge(s_evac, t - RING + 1)
                        pe.wait_ge(s_hlo, st["h0"] - KD + k + 1)
                        m = products(2 * (t % RING), u % RING, w, h_src, k, META, S, k % 2 == 0, k % 2 == 1)
                    m.then_inc(s_unit, 1)

            def values1(st):
                def turn(v, j):
                    pe.wait_ge(s_evac, st["t0"] + v + 1)
                    if not (isinstance(v, int) and v < 2):
                        pe.wait_ge(s_val, v - 1)
                    for r in range(R4):
                        m = pe.transpose(ps[:, 1 + 2 * (j % 2), r * P:(r + 1) * P],
                                         vT[:, j % 2, r * P:(r + 1) * P], ident[:, :])
                    m.then_inc(s_vtr, 1)

                def body(i):
                    for j in range(4):
                        u, t = st["u0"] + 4 * i + j, st["t0"] + 4 * i + j
                        pe.wait_ge(s_evac, t - RING + 1)
                        unit(u, (st["u0"] + j) % RING, (st["t0"] + j) % RING, S, x_src, 0, KD,
                             x0=st["x0"] - KD if isinstance(i, int) and j == 0 else None)
                        if not (isinstance(i, int) and j == 0):
                            turn(4 * i + j - 1, (j - 1) % 4)
                body(0)
                with pe.Fori(1, 3 * KD // 4) as i:
                    body(i)
                turn(3 * KD - 1, 3)

            def attend1(st):
                def head(half):
                    return slice(HD * half, HD * half + HD)

                def scores(a, m, buf, p):
                    r, hs = m // 2, head(m % 2)
                    if m == 0:
                        pe.wait_ge(s_evac, st["t0"] + 6 * p + 6)
                    if not (isinstance(a, int) and a < 1):
                        pe.wait_ge(s_bias, a)
                    q = [qk[hs, buf, 2 * g, r * NI:(r + 1) * NI] for g in range(3)]
                    pe.matmul(ps[:, 1, 0:S], q[0], qk[hs, buf, 1, :], start=True, stop=True)
                    for g in (1, 2):
                        mm = pe.matmul(ps[:, 3, (g - 1) * NI:g * NI], q[g],
                                       qk[hs, buf, 2 * g + 1, r * NI:(r + 1) * NI], start=True, stop=True)
                    mm.then_inc(s_score, 1)

                def turn(a):
                    pe.wait_ge(s_exp, a + 1)
                    if not (isinstance(a, int) and a < 1):
                        pe.wait_ge(s_pTe, a)
                    for b in range(6):
                        mm = pe.transpose(ps[:, 4 + b // 4, (b % 4) * P:(b % 4 + 1) * P],
                                          prob[:, b * P:(b + 1) * P], ident[:, :])
                    mm.then_inc(s_pT, 1)

                def weigh(a, m, p):
                    r, half = m // 2, m % 2
                    pe.wait_ge(s_pTe, a + 1)
                    if not (isinstance(a, int) and a < 1):
                        pe.wait_ge(s_on, a)
                    for b in range(6):
                        g, tile = (0, b) if b < 4 else (b - 3, r)
                        v = val[:, tile, bass.ds(g * D + P * p + HD * half, HD)]
                        mm = pe.matmul(ps[:, 6, half * HD:(half + 1) * HD], probT[:, b * P:(b + 1) * P], v,
                                       start=b == 0, stop=b == 5)
                    mm.then_inc(s_pv, 1)

                def turn_out(c, r):
                    pe.wait_ge(s_on, 2 * c + 2)
                    if not (isinstance(c, int) and c < 1):
                        pe.wait_ge(s_oe, c)
                    pe.transpose(ps[:, 7, 0:P], o_tok[:, r % 2, :], ident[:, :]).then_inc(s_oT, 1)

                def job(p, m, buf, only_from=0):
                    a = 8 * p + m
                    if only_from < 1:
                        scores(a, m, buf, p)
                    if only_from < 2 and not (isinstance(a, int) and a < 1):
                        turn(a - 1)
                    if only_from < 3 and not (isinstance(a, int) and a < 2):
                        weigh(a - 2, (m - 2) % 8, p if m >= 2 else p - 1)
                    if m % 2 == 0 and not (isinstance(a, int) and a < 4):
                        turn_out(4 * p + m // 2 - 2, (m // 2 - 2) % R4)

                def pair_step(p, q, buf, jobs):
                    count = [0]
                    for j in range(6):
                        u, t = st["u0"] + 6 * p + j, st["t0"] + 6 * p + j
                        pe.wait_ge(s_evac, t - 1)

                        def between(k):
                            if k % 2:
                                count[0] += 1
                                if count[0] % 3 == 0 and jobs:
                                    job(p - 1, count[0] // 3 - 1, 1 - buf)
                        unit(u, (st["u0"] + 6 * q + j) % RING, (st["t0"] + j) % 2, S, x_src, 0, KD, between=between)

                pe.wait_ge(s_val, 3 * KD)
                pair_step(0, 0, 0, False)
                pair_step(1, 1, 1, True)
                pair_step(2, 2, 0, True)
                with pe.Fori(1, KD // 2 - 1) as i:
                    pair_step(2 * i + 1, 1, 1, True)
                    pair_step(2 * i + 2, 2, 0, True)
                pair_step(KD - 1, KD - 1, 1, True)
                for m in range(8):
                    job(KD - 1, m, 1)
                for m in range(3):
                    job(KD, m, 0, only_from=m + 1)

            def renorm(st):
                def into_stat(rows, first, last):
                    for a, c0, n in halves(T):
                        m = pe.matmul(ps[:, 6 + a, 0:n], mean_w[:, :], rows[:, c0:c0 + n], start=first, stop=last)
                    return m
                if st["after"]:
                    pe.wait_ge(s_evac, st["t0"])
                    pe.wait_ge(s_sum2, (KD + 1) * st["j0"])
                    into_stat(sums[:, 1, :], True, True).then_inc(s_rst, 1)
                if st["outs"]:
                    for k in range(KD):
                        pe.wait_ge(s_sqr, st["s0"] + k + 1)
                        into_stat(pair[:, k % 2, :], k == 0, k == KD - 1).then_inc(s_sqp, 1)

            def hgrn(st):
                real = slice(META, T)

                def cols(b):
                    return slice(META + P * b, META + P * b + P)

                def turn_and_score(n):
                    pe.wait_ge(G["kout"], n + 1)
                    past(pe, G["kt"], n)
                    past(pe, G["vt"], n)
                    past(pe, G["mt"], n)
                    if not (isinstance(n, int) and n < 1):
                        pe.wait_ge(G["state"], NCH * n)
                        pe.wait_ge(G["eps"], n)
                        pe.wait_ge(G["oe"], 2 * n)
                    for b in range(4):
                        pe.transpose(ps[:, 4, P * b:P * b + P], g_kout[:, cols(b)], ident[:, :])
                    for b in range(4):
                        pe.transpose(ps[:, 5, P * b:P * b + P], g_v[:, cols(b)], ident[:, :])
                    pe.transpose(ps[0:META, 6, 0:P], g_kout[:, 0:META], ident[:, :])
                    pe.transpose(ps[0:META, 6, P:2 * P], g_v[:, 0:META], ident[:, :]).then_inc(G["turn"], 1)
                    for b in range(4):
                        pe.matmul(ps[:, 7, P * b:P * b + P], g_kin[:, cols(b)], g_qin[:, cols(b)],
                                  start=True, stop=True)
                    pe.matmul(ps[0:META, 6, 2 * P:2 * P + META], g_kin[:, 0:META], g_qin[:, 0:META],
                              start=True, stop=True).then_inc(G["score"], 1)

                def state_steps(n):
                    pe.wait_ge(G["kt"], n + 1)
                    pe.wait_ge(G["vt"], n + 1)
                    pe.wait_ge(G["mt"], n + 1)
                    pe.wait_ge(G["at"], n + 1)
                    pe.matmul(ps[:, 6, 0:P], g_mt[:, 0, :], g_mt[:, 1, :], start=True, stop=True)
                    for j in range(NCH - 1):
                        rows = slice(CH * (j % 2), CH * (j % 2) + CH)
                        m = pe.matmul(ps[:, 4 + j % 2, P * (j // 2):P * (j // 2) + P], g_kt[rows, j // 2, :],
                                      g_vt[rows, j // 2, :], start=True, stop=True)
                    m.then_inc(G["ds"], 1)

                def outputs(n):
                    pe.wait_ge(G["state"], NCH * (n + 1))
                    pe.matmul(ps[:, 6, 0:META], g_mt[:, 1, :], g_atm[:, :], start=True, stop=True)
                    for b in range(4):
                        pe.matmul(ps[:, 7, P * b:P * b + P], g_vt[:, b, :], g_at[:, b, :], start=True, stop=False)
                        for j in (2 * b, 2 * b + 1):
                            m = pe.matmul(ps[:, 7, CH * j:CH * j + CH], g_state[:, j, :],
                                          g_qin[:, META + CH * j:META + CH * j + CH], start=False, stop=j == 2 * b + 1)
                    m.then_inc(G["o"], 1)

                def mean_square(n):
                    pe.wait_ge(G["sq"], n + 1)
                    for a, c0, w in halves(T):
                        m = pe.matmul(ps[:, 4 + a, 0:w], mean_w[:, :], pair[:, 0, c0:c0 + w], start=True, stop=True)
                    m.then_inc(G["ms"], 1)

                def step(n, odd, before, before2):
                    for j in range(4):
                        u, t = st["u0"] + 4 * n + j, st["t0"] + 4 * n + j
                        pe.wait_ge(s_evac, t - 1)
                        unit(u, (st["u0"] + j) % RING, (st["t0"] + j) % 2, T, x_src, 0, KD,
                             x0=st["x0"] - KD if isinstance(n, int) and n == 0 and j == 0 else None)
                        if j == 0 and before2:
                            mean_square(n - 2)
                        if j >= 1 and before:
                            (turn_and_score, state_steps, outputs)[j - 1](n - 1)

                step(0, 0, False, False)
                step(1, 1, True, False)
                step(2, 0, True, True)
                step(3, 1, True, True)
                with pe.Fori(2, KD // 2) as i:
                    step(2 * i, 0, True, True)
                    step(2 * i + 1, 1, True, True)
                mean_square(KD - 2)
                turn_and_score(KD - 1)
                state_steps(KD - 1)
                outputs(KD - 1)
                mean_square(KD - 1)

            def fox_values(st):
                def turn(v):
                    pe.wait_ge(s_evac, st["t0"] + v + 2)
                    if v >= 2:
                        pe.wait_ge(FX["val"], v - 1)
                    for b in range(4):
                        pe.transpose(ps[:, 4 + v % 2, P * b:P * b + P],
                                     pair[:, v % 2, META + P * b:META + P * b + P], ident[:, :])
                    pe.transpose(ps[0:META, 6 + v % 2, 0:P], pair[:, v % 2, 0:META], ident[:, :])\
                        .then_inc(FX["vtr"], 1)

                for n in range(1 + KD):
                    u, t = st["u0"] + n, st["t0"] + n
                    pe.wait_ge(s_evac, t - 1)
                    unit(u, u % RING, t % 2, T, x_src, 0, KD, x0=st["x0"] - KD if n == 0 else None)
                    if n >= 2:
                        turn(n - 2)
                turn(KD - 1)

            def fox(st):
                def head(half):
                    return slice(HD * half, HD * half + HD)

                def scores(p, m, buf):
                    half, b = FOX_JOBS[m]
                    q0, nk = fox_block(b)
                    own = P if b else META
                    a, hs, bank = NJ * p + m, head(half), 6 if m % 2 else 2
                    if m == 0:
                        pe.wait_ge(s_evac, st["t0"] + 2 * p + 2)
                    if m % 5 == 0:
                        pe.wait_ge(FX["b"], 2 * p + half + 1)
                    if back(p, m, 2):
                        pe.wait_ge(FX["exp"], a - 1)
                    def at_bank(rows, c, n, k):
                        return ps[0:rows, bank + k, c - 512 * k:c - 512 * k + n]
                    for c, n, k in by_bank(0, nk):
                        pe.matmul(at_bank(P, c, n, k), f_a[:, q0:q0 + P], f_b[:, half, c:c + n],
                                  start=True, stop=False)
                    for c, n, k in by_bank(nk - own, nk):
                        pe.matmul(at_bank(own, c, n, k), ident[0:own, 0:own],
                                  f_mask[0:own, c - nk + own:c - nk + own + n], start=False, stop=False)
                    for c, n, k in by_bank(0, nk):
                        mm = pe.matmul(at_bank(P, c, n, k), f_qk[hs, buf, 1, q0:q0 + P], f_qk[hs, buf, 0, c:c + n],
                                       start=False, stop=True)
                    mm.then_inc(FX["score"], 1)

                def turn(p, m):
                    pe.wait_ge(FX["exp"], NJ * p + m + 1)
                    past(pe, FX["pTe"], NJ * p + m)
                    mm = pe.transpose(ps[0:META, 5, 0:P], f_prob[:, m % 2, 0:META], ident[:, :])
                    for j in range(FOX_JOBS[m][1]):
                        mm = pe.transpose(ps[:, 4, P * j:P * j + P],
                                          f_prob[:, m % 2, META + P * j:META + P * j + P], ident[:, :])
                    mm.then_inc(FX["pT"], 1)

                def turn_out(p, m):
                    pe.transpose(ps[:, 7, P:2 * P], f_otok[:, FOX_JOBS[m][1], :], ident[:, :]).then_inc(FX["oT"], 1)

                def weigh(p, m):
                    half, b = FOX_JOBS[m]
                    cols = bass.ds(P * p + HD * half, HD)
                    mm = pe.matmul(ps[:, 7, 0:HD], f_probT[0:META, m % 2, 0, :], f_vmeta[:, cols],
                                   start=True, stop=b == 0)
                    for j in range(b):
                        mm = pe.matmul(ps[:, 7, 0:HD], f_probT[:, m % 2, 1 + j, :], f_val[:, j, cols],
                                       start=False, stop=j == b - 1)
                    mm.then_inc(FX["pv"], 1)

                def job(p, m, buf, only_from=0):
                    if only_from < 1:
                        scores(p, m, buf)
                    if only_from < 3 and back(p, m, 2):
                        pe.wait_ge(FX["pTe"], NJ * p + m - 1)
                    if back(p, m, 3):
                        pe.wait_ge(FX["on"], NJ * p + m - 2)
                    if back(p, m, 4):
                        past(pe, FX["oe"], out_count(*back(p, m, 4)))
                    if only_from < 2 and back(p, m, 1):
                        turn(*back(p, m, 1))
                    if back(p, m, 3) and FOX_JOBS[(m - 3) % NJ][0]:
                        turn_out(*back(p, m, 3))
                    if only_from < 3 and back(p, m, 2):
                        weigh(*back(p, m, 2))

                def pair_step(p, q, buf, jobs):
                    for j in range(2):
                        u, t = st["u0"] + 2 * p + j, st["t0"] + 2 * p + j
                        pe.wait_ge(s_evac, t)

                        def between(k):
                            c = KD * j + k + 1
                            if jobs and c in FOX_AT:
                                job(p - 1, FOX_AT[c], 1 - buf)
                        unit(u, (st["u0"] + 2 * q + j) % RING, 0, T, (x_src, h_src)[j], 0, KD, between=between)

                pe.wait_ge(FX["val"], KD)
                pe.wait_ge(FX["tab"], 16)
                pe.wait_ge(s_hlo, st["h0"])
                pair_step(0, 0, 0, False)
                pair_step(1, 1, 1, True)
                pair_step(2, 2, 0, True)
                with pe.Fori(1, KD // 2 - 1) as i:
                    pair_step(2 * i + 1, 1, 1, True)
                    pair_step(2 * i + 2, 2, 0, True)
                pair_step(KD - 1, KD - 1, 1, True)
                for m in range(NJ):
                    job(KD - 1, m, 1)
                for m in range(3):
                    job(KD, m, 0, only_from=m + 1)

            run = dict(glu=glu, project=project, layer_norm=layer_norm, pool_in=pool_in, pool_group=pool_group,
                       values1=values1, attend1=attend1, glu2=glu, project2=project, renorm=renorm, hgrn=hgrn,
                       fox_values=fox_values, fox=fox)
            for st in STAGES:
                if st["kind"] in run:
                    run[st["kind"]](st)

        @block.scalar
        def _(act):
            def split(u, slot):
                if isinstance(u, int) and u >= UNITS:
                    return
                act.wait_ge(s_load[slot], (u // RING + 1) * 16 if isinstance(u, int) else (u - slot) * 4 + 16)
                if not (isinstance(u, int) and u < RING):
                    act.wait_ge(s_unit, u - RING + 1)
                act.activation(w_hi[:, slot], raw[:, slot], ACT.Copy).then_inc(s_hi, 1)

            def split_ahead(st, i, per, j):
                split(st["u0"] + per * i + j + AHEAD, (st["u0"] + j + AHEAD) % RING)

            def load(st):
                act.wait_ge(s_init, 6 * 16)
                split(0, 0)
                split(1, 1)
                for k in range(KD):
                    act.activation(x_hi[:, k, META:T], res[:, k, META:T], ACT.Copy).then_inc(s_xhi, 1)

            def glu(st):
                def body(i):
                    for f in range(2):
                        h = st["h0"] + 2 * i + f
                        g = st["g0"] + 2 * i + f
                        slot = (st["t0"] + 2 * f) % RING
                        split_ahead(st, i, 4, 2 * f)
                        act.wait_ge(s_unit, st["u0"] + 4 * i + 2 * f + 1)
                        if not (isinstance(h, int) and h < 2):
                            act.wait_ge(s_hlo, h - 1)
                        act.activation(pair[:, f, META:T], psv(slot), ACT.Silu).then_inc(s_silu, 1)
                        split_ahead(st, i, 4, 2 * f + 1)
                        act.wait_ge(s_evac, st["t0"] + 4 * i + 2 * f + 2)
                        k = 2 * i + f
                        act.activation(h_hi[:, bass.ds(k, 1), META:T].rearrange("p a t -> p (a t)"),
                                       pair[:, f, META:T], ACT.Copy).then_inc(s_hhi, 1)
                body(0)
                with act.Fori(1, KF // 2) as i:
                    body(i)

            def project(st):
                chunks, per = st["chunks"], 4
                def body(i):
                    for n in range(per):
                        for c in range(len(chunks)):
                            split_ahead(st, i, len(chunks) * per, len(chunks) * n + c)
                        k = per * i + n
                        act.wait_ge(s_evac, st["t0"] + k + 1)
                        act.wait_ge(s_sum, (2 * KD + 1) * st["n0"] + 1 + 2 * k)
                        act.activation(pair[:, 0, META:T], res[:, bass.ds(k, 1), META:T].rearrange("p a t -> p (a t)"),
                                       ACT.Square).then_inc(s_sq, 1)
                each(act, st, KD // per, body)

            def layer_norm(st):
                act.wait_ge(s_stat, 2 * st["n0"] + 1)
                act.activation(pair[:, 1, META:T], ps[:, 5, 0:S], ACT.Square).then_inc(s_var, 1)
                act.wait_ge(s_var, 5 * st["n0"] + 4)
                act.activation(rstd[:, META:T], rstd[:, META:T], ACT.Sqrt).then_inc(s_var, 1)
                gain, bias = f"ln_gain{st['l']}{st['j']}", f"ln_bias{st['l']}{st['j']}"
                for k in range(KD):
                    n = KD * st["n0"] + k + 1
                    act.wait_ge(s_nrm, n)
                    act.activation(res[:, k, META:T], res[:, k, META:T], ACT.Identity,
                                   bias=par_of(bias, k), scale=par_of(gain, k)).then_inc(s_aff, 1)
                    if not st["scaled"]:
                        continue
                    act.wait_ge(s_aff, n)
                    act.activation(x_hi[:, k, META:T], res[:, k, META:T], ACT.Copy).then_inc(s_xhi, 1)

            def pool_in(st):
                for n in range(KD):
                    split(st["u0"] + n + AHEAD, (st["u0"] + n + AHEAD) % RING)
                    act.wait_ge(s_unit, st["u0"] + n + 1)
                    if n < 2:
                        act.wait_ge(s_pad, 1)
                    else:
                        act.wait_ge(s_win, win_steps(n - 1))
                    act.activation(upad[:, n % 2, PAD:PAD + S], psv((st["t0"] + n) % RING), ACT.Copy)\
                        .then_inc(s_evac, 1)
                    if n >= 1:
                        high_mixed(n - 1)
                high_mixed(KD - 1)

            def high_mixed(n):
                act.wait_ge(s_win, win_steps(n + 1))
                act.activation(h_hi[:, n, META:T], pair[:, n % 2, META:T], ACT.Copy).then_inc(s_hhi, 1)

            def pool_group(st):
                for v in range(2):
                    split(st["u0"] + v + AHEAD, (st["u0"] + v + AHEAD) % RING)
                    act.wait_ge(s_unit, st["u0"] + v + 1)
                    for n in range(4 * v, 4 * v + 4):
                        act.wait_ge(s_hlo, st["h0"] + n - 1)
                        act.activation(pair[:, n % 2, META:T], psv((st["t0"] + n) % RING), ACT.Copy,
                                       scale=par_of("pool_scale", n)).then_inc(s_evac, 1)
                        act.wait_ge(s_evac, st["t0"] + n + 1)
                        act.activation(h_hi[:, KD + n, META:T], pair[:, n % 2, META:T], ACT.Copy).then_inc(s_hhi, 1)

            def values1(st):
                def value(v, j, permuted):
                    split(st["u0"] + v + AHEAD, (st["u0"] + j + AHEAD) % RING)
                    act.wait_ge(s_unit, st["u0"] + v + 1)
                    if not (isinstance(v, int) and v < 2):
                        act.wait_ge(s_vtr, v - 1)
                    dst, src = vT[:, j % 2, :], psv((st["t0"] + j) % RING)
                    if permuted:
                        dst, src = by_residue(dst), in_order(src)
                    act.activation(dst, src, ACT.Copy).then_inc(s_evac, 1)

                for v in range(KD):
                    value(v, v % 4, False)
                with act.Fori(KD // 4, 3 * KD // 4) as i:
                    for j in range(4):
                        value(4 * i + j, j, True)

            def attend1(st):
                def job(p, m, only_from=0):
                    a = 8 * p + m
                    if only_from < 2 and not (isinstance(a, int) and a < 1):
                        act.wait_ge(s_pT, a)
                        if not (isinstance(a, int) and a < 2):
                            act.wait_ge(s_pv, a - 1)
                        act.activation(probT[:, :], ps[:, 4:6, :].rearrange("p a b -> p (a b)")[:, 0:S + 2 * NI],
                                       ACT.Copy).then_inc(s_pTe, 1)
                    if only_from < 1:
                        act.wait_ge(s_max, a + 1)
                        act.activation(prob[:, :], prob[:, :], ACT.Exp, bias=stat[:, m % 2:m % 2 + 1],
                                       accum_out=stat[:, 2 + m % 2:3 + m % 2]).then_inc(s_exp, 1)

                def pair_step(p, q, buf, jobs):
                    for c in range(1, 25):
                        if c % 4 == 0:
                            j = c // 4 - 1
                            v = 6 * p + j
                            split(st["u0"] + v + AHEAD, (st["u0"] + 6 * q + j + AHEAD) % RING)
                            act.wait_ge(s_unit, st["u0"] + v + 1)
                            if not (isinstance(p, int) and p < 2):
                                act.wait_ge(s_score, 8 * p - 8)
                            dst, src = qk[:, buf, j, :], psv((st["t0"] + j) % 2)
                            if j != 1:
                                dst, src = by_residue(dst), in_order(src)
                            act.activation(dst, src, ACT.Copy, scale=1.0 if j % 2 else HD ** -0.5)\
                                .then_inc(s_evac, 1)
                        if c % 3 == 0 and jobs:
                            job(p - 1, c // 3 - 1)

                pair_step(0, 0, 0, False)
                pair_step(1, 1, 1, True)
                pair_step(2, 2, 0, True)
                with act.Fori(1, KD // 2 - 1) as i:
                    pair_step(2 * i + 1, 1, 1, True)
                    pair_step(2 * i + 2, 2, 0, True)
                pair_step(KD - 1, KD - 1, 1, True)
                for m in range(8):
                    job(KD - 1, m)
                job(KD, 0, only_from=1)
                act.wait_ge(s_unit, st["u0"] + 6 * KD)
                for k in range(KD):
                    act.wait_ge(s_oe, R4 * (k + 1))
                    act.activation(x_hi[:, k, META:T], att[:, k, :], ACT.Copy).then_inc(s_xhi, 1)

            def glu2(st):
                def body(i):
                    for f in range(2):
                        k = 2 * i + f
                        c = st["c0"] + k
                        slot = (st["t0"] + 2 * f) % RING
                        split_ahead(st, i, 4, 2 * f)
                        act.wait_ge(s_unit, st["u0"] + 4 * i + 2 * f + 1)
                        if not (isinstance(c, int) and c < 1):
                            act.wait_ge(s_cv, 6 * c - 3)
                        act.activation(sbv(upad2[:, 0, 2:], T), psv(slot, T), ACT.Copy).then_inc(s_evac, 1)
                        act.wait_ge(s_cv, 6 * c + 3)
                        act.activation(pair[:, 0, :], pair[:, 0, :], ACT.Silu).then_inc(s_gate, 1)
                        split_ahead(st, i, 4, 2 * f + 1)
                        act.wait_ge(s_unit, st["u0"] + 4 * i + 2 * f + 2)
                        past(act, s_cv, 6 * c)
                        act.activation(sbv(upad2[:, 1, 2:], T), psv((slot + 1) % RING, T), ACT.Copy).then_inc(s_evac, 1)
                        act.wait_ge(s_h, c + 1)
                        act.activation(h_hi[:, bass.ds(k, 1), :].rearrange("p a t -> p (a t)"), pair[:, 1, :],
                                       ACT.Copy).then_inc(s_hhi, 1)
                body(0)
                with act.Fori(1, KF // 2) as i:
                    body(i)

            def project2(st):
                chunks, per = st["chunks"], 4

                def body(i):
                    for n in range(per):
                        for c in range(len(chunks)):
                            split_ahead(st, i, len(chunks) * per, len(chunks) * n + c)
                        k = per * i + n
                        act.wait_ge(s_unit, st["u0"] + len(chunks) * (k + 1))
                        act.wait_ge(s_sum2, (KD + 1) * st["j0"] + 1 + k)
                        act.activation(sbv(pair[:, 0, :], T), psv((st["t0"] + n) % RING, T), ACT.Square)\
                            .then_inc(s_mixed, 1)
                        act.activation(sbv(mix[:, bass.ds(k, 1), :].rearrange("p a t -> p (a t)"), T),
                                       psv((st["t0"] + n) % RING, T), ACT.Copy).then_inc(s_evac, 1)
                each(act, st, KD // per, body)

            def renorm(st):
                v = 3 * st["v0"]
                if st["after"]:
                    act.wait_ge(s_rv, v + 2)
                    act.activation(rstd[:, :], rstd[:, :], ACT.Sqrt).then_inc(s_rv, 1)
                    v += 3
                if st["outs"]:
                    for k in range(KD):
                        if st["after"]:
                            act.wait_ge(s_add, st["a0"] + k + 1)
                        else:
                            act.wait_ge(s_aff, KD * st["n0"] - KD + k + 1)
                        past(act, s_sqp, st["s0"] + k - 1 if k > 1 else st["s0"])
                        act.activation(pair[:, k % 2, :], res[:, k, :], ACT.Square).then_inc(s_sqr, 1)
                    act.wait_ge(s_rv, v + 2)
                    act.activation(rstd[:, :], rstd[:, :], ACT.Sqrt).then_inc(s_rv, 1)
                for o, (_, to) in enumerate(st["outs"]):
                    for k in range(KD):
                        act.wait_ge(s_y, st["y0"] + KD * o + k + 1)
                        if to == "x":
                            act.activation(x_hi[:, k, :], mix[:, k, :], ACT.Copy).then_inc(s_xhi, 1)
                        else:
                            act.activation(h_hi[:, k, :], h_mix[:, k, :], ACT.Copy).then_inc(s_hhi, 1)

            def hgrn(st):
                def products(n, odd):
                    out = (
                        lambda p: (past(act, G["qin"], n), act.activation(sbv(g_q, T), p, ACT.Copy)),
                        lambda p: (past(act, G["c"], n), act.activation(sbv(g_b, T), p, ACT.Sigmoid)),
                        lambda p: (past(act, G["turn"], n), act.activation(sbv(g_v, T), p, ACT.Copy)),
                        lambda p: (past(act, G["og"], 2 * n - 2 if not isinstance(n, int) or n > 1 else 0),
                                   act.activation(sbv(g_gate[:, odd, :], T), p, ACT.Silu)),
                    )
                    return out

                def take(n, odd, j):
                    split(st["u0"] + 4 * n + j + AHEAD, (st["u0"] + j + AHEAD) % RING)
                    act.wait_ge(s_unit, st["u0"] + 4 * n + j + 1)
                    p = psv((st["t0"] + j) % 2, T)
                    products(n, odd)[j](p)[1].then_inc(s_evac, 1)

                def decays(n):
                    act.wait_ge(G["k"], n + 1)
                    act.activation(g_b[:, :], g_b[:, :], ACT.Ln).then_inc(G["ln"], 1)
                    act.wait_ge(G["c"], n + 1)
                    past(act, G["state"], NCH * n)
                    act.activation(g_eb[:, :], g_c[:, :], ACT.Exp).then_inc(G["eb"], 1)
                    past(act, G["score"], n)
                    act.activation(g_kin[:, :], g_c[:, :], ACT.Exp, scale=-1.0).then_inc(G["enb"], 1)
                    act.wait_ge(G["d"], n + 1)
                    act.activation(g_kout[:, :], g_kout[:, :], ACT.Exp).then_inc(G["ed"], 1)

                def copies(n):
                    act.wait_ge(G["turn"], n + 1)
                    act.activation(g_kt[:, :, :], ps[:, 4, :].rearrange("p (b n) -> p b n", n=P), ACT.Copy)\
                        .then_inc(G["kt"], 1)
                    past(act, G["o"], n)
                    act.activation(g_vt[:, :, :], ps[:, 5, :].rearrange("p (b n) -> p b n", n=P), ACT.Copy)\
                        .then_inc(G["vt"], 1)

                def squares(n):
                    act.wait_ge(G["oe"], 2 * n + 2)
                    past(act, G["ms"], n)
                    act.activation(pair[:, 0, :], g_o[:, :], ACT.Square).then_inc(G["sq"], 1)

                def root(n):
                    act.wait_ge(G["eps"], n + 1)
                    act.activation(g_rs[:, :], g_rs[:, :], ACT.Ln).then_inc(G["lnr"], 1)
                    act.wait_ge(G["lnr"], n + 1)
                    act.activation(g_rs[:, :], g_rs[:, :], ACT.Exp, scale=-0.5).then_inc(G["rs"], 1)

                def high(n):
                    act.wait_ge(G["og"], 2 * n + 2)
                    act.activation(h_hi[:, bass.ds(n, 1), :].rearrange("p a t -> p (a t)"), g_o[:, :], ACT.Copy)\
                        .then_inc(s_hhi, 1)

                def step(n, odd, before, before2):
                    if before:
                        decays(n - 1)
                    take(n, odd, 0)
                    if before2:
                        root(n - 2)
                        high(n - 2)
                    take(n, odd, 1)
                    if before:
                        copies(n - 1)
                    take(n, odd, 2)
                    take(n, odd, 3)
                    if before:
                        squares(n - 1)

                act.wait_ge(G["lb"], 3)
                act.activation(g_lb[:, 0:2, :], g_lb[:, 0:2, :], ACT.Exp).then_inc(G["lb"], 1)
                step(0, 0, False, False)
                step(1, 1, True, False)
                step(2, 0, True, True)
                step(3, 1, True, True)
                with act.Fori(2, KD // 2) as i:
                    step(2 * i, 0, True, True)
                    step(2 * i + 1, 1, True, True)
                decays(KD - 1)
                root(KD - 2)
                high(KD - 2)
                copies(KD - 1)
                squares(KD - 1)
                root(KD - 1)
                high(KD - 1)

            def fox_values(st):
                z = f_b[:, :, :]
                for n in range(1 + KD):
                    split(st["u0"] + n + AHEAD, (st["u0"] + n + AHEAD) % RING)
                    act.wait_ge(s_unit, st["u0"] + n + 1)
                    src = psv((st["t0"] + n) % 2, T)
                    if n == 0:
                        act.activation(sbv(z[:, 0, :], T), src, ACT.Identity,
                                       bias=par[:, PARAM["fg_b"]:PARAM["fg_b"] + 1]).then_inc(s_evac, 1)
                        continue
                    v = n - 1
                    if v >= 2:
                        act.wait_ge(FX["vtr"], v - 1)
                    act.activation(sbv(pair[:, v % 2, :], T), src, ACT.Copy).then_inc(s_evac, 1)
                    if n == 1:
                        act.wait_ge(FX["c"], 1)
                        act.activation(z[:, 1, :], z[:, 1, :], ACT.Exp, scale=-1.0).then_inc(FX["c"], 1)
                    if n == 2:
                        act.wait_ge(FX["c"], 3)
                        act.activation(z[:, 1, :], z[:, 1, :], ACT.Ln).then_inc(FX["c"], 1)

            def fox(st):
                def job(p, m, only_from=0):
                    if only_from < 2 and back(p, m, 1):
                        pp, mm = back(p, m, 1)
                        b = FOX_JOBS[mm][1]
                        act.wait_ge(FX["pT"], NJ * pp + mm + 1)
                        if back(pp, mm, 2):
                            act.wait_ge(FX["pv"], NJ * pp + mm - 1)
                        if b:
                            act.activation(f_probT[:, mm % 2, 1:1 + b, :],
                                           ps[:, 4, 0:P * b].rearrange("p (j n) -> p j n", n=P), ACT.Copy)
                        act.activation(f_probT[0:META, mm % 2, 0, :], ps[0:META, 5, 0:P], ACT.Copy)\
                            .then_inc(FX["pTe"], 1)
                    if only_from < 1:
                        a = NJ * p + m
                        nk = fox_block(FOX_JOBS[m][1])[1]
                        bank = 6 if m % 2 else 2
                        s = ps[:, bank:bank + 2, :].rearrange("p a n -> p (a n)")[:, 0:nk]
                        act.wait_ge(FX["max"], a + 1)
                        if back(p, m, 2):
                            act.wait_ge(FX["pT"], a - 1)
                            act.wait_ge(FX["rec"], a - 1)
                        act.activation(f_prob[:, m % 2, 0:nk], s, ACT.Exp, bias=stat[:, m % 2:m % 2 + 1],
                                       accum_out=stat[:, 2 + m % 2:3 + m % 2]).then_inc(FX["exp"], 1)

                def pair_step(p, q, buf, jobs):
                    for c in range(1, 2 * KD + 1):
                        if c % KD == 0:
                            j = c // KD - 1
                            v = 2 * p + j
                            split(st["u0"] + v + AHEAD, (st["u0"] + 2 * q + j + AHEAD) % RING)
                            act.wait_ge(s_unit, st["u0"] + v + 1)
                            if not (isinstance(p, int) and p < 2):
                                act.wait_ge(FX["score"], NJ * (p - 1))
                            act.activation(sbv(f_qk[:, buf, j, :], T), psv(0, T), ACT.Copy,
                                           scale=HD ** -0.5 if j else 1.0).then_inc(s_evac, 1)
                        if jobs and c in FOX_AT:
                            job(p - 1, FOX_AT[c])

                pair_step(0, 0, 0, False)
                pair_step(1, 1, 1, True)
                pair_step(2, 2, 0, True)
                with act.Fori(1, KD // 2 - 1) as i:
                    pair_step(2 * i + 1, 1, 1, True)
                    pair_step(2 * i + 2, 2, 0, True)
                pair_step(KD - 1, KD - 1, 1, True)
                for m in range(NJ):
                    job(KD - 1, m)
                job(KD, 0, only_from=1)
                act.wait_ge(s_unit, st["u0"] + 2 * KD)
                for k in range(KD):
                    act.wait_ge(FX["oe"], 5 * (k + 1))
                    act.activation(h_hi[:, k, :], f_o[:, k, :], ACT.Copy).then_inc(s_hhi, 1)

            run = dict(load=load, glu=glu, project=project, layer_norm=layer_norm, pool_in=pool_in,
                       pool_group=pool_group, values1=values1, attend1=attend1, glu2=glu2, project2=project2,
                       renorm=renorm, hgrn=hgrn, fox_values=fox_values, fox=fox)
            for st in STAGES:
                if st["kind"] in run:
                    run[st["kind"]](st)

        @block.vector
        def _(dve):
            def split(u, slot):
                if isinstance(u, int) and u >= UNITS:
                    return
                dve.wait_ge(s_hi, u + 1)
                if not (isinstance(u, int) and u < RING):
                    dve.wait_ge(s_unit, u - RING + 1)
                dve.tensor_tensor(w_lo[:, slot], raw[:, slot], w_hi[:, slot].bitcast(F32), ALU.subtract)\
                    .then_inc(s_lo, 1)

            def split_ahead(st, i, per, j):
                split(st["u0"] + per * i + j + AHEAD, (st["u0"] + j + AHEAD) % RING)

            def load(st):
                split(0, 0)
                split(1, 1)
                for k in range(KD):
                    dve.wait_ge(s_xhi, k + 1)
                    dve.tensor_tensor(x_lo[:, k, META:T], res[:, k, META:T], x_hi[:, k, META:T].bitcast(F32),
                                      ALU.subtract).then_inc(s_xlo, 1)

            def glu(st):
                def body(i):
                    for f in range(2):
                        k = 2 * i + f
                        slot = (st["t0"] + 2 * f + 1) % RING
                        split_ahead(st, i, 4, 2 * f)
                        dve.wait_ge(s_silu, st["g0"] + k + 1)
                        dve.wait_ge(s_unit, st["u0"] + 4 * i + 2 * f + 2)
                        dve.tensor_tensor(pair[:, f, META:T], pair[:, f, META:T], psv(slot), ALU.mult)\
                            .then_inc(s_evac, 2)
                        split_ahead(st, i, 4, 2 * f + 1)
                        dve.wait_ge(s_hhi, st["h0"] + k + 1)
                        h = bass.ds(k, 1)
                        dve.tensor_tensor(h_lo[:, h, META:T].rearrange("p a t -> p (a t)"), pair[:, f, META:T],
                                          h_hi[:, h, META:T].rearrange("p a t -> p (a t)").bitcast(F32),
                                          ALU.subtract).then_inc(s_hlo, 1)
                body(0)
                with dve.Fori(1, KF // 2) as i:
                    body(i)

            def project(st):
                chunks, per = st["chunks"], 4
                cleared = (2 * KD + 1) * st["n0"] + 1
                dve.memset(sums[:, :, :], 0.0).then_inc(s_sum, 1)
                dve.wait_ge(s_res, st["r0"])
                def body(i):
                    for n in range(per):
                        for c in range(len(chunks)):
                            split_ahead(st, i, len(chunks) * per, len(chunks) * n + c)
                        k = per * i + n
                        z = res[:, bass.ds(k, 1), META:T].rearrange("p a t -> p (a t)")
                        dve.wait_ge(s_unit, st["u0"] + len(chunks) * (k + 1))
                        dve.scalar_tensor_tensor(out=z, in0=psv((st["t0"] + n) % RING), scalar=st["coef"], in1=z,
                                                 op0=ALU.mult, op1=ALU.add).then_inc(s_evac, 1)
                        dve.wait_ge(s_evac, st["t0"] + k + 1)
                        dve.wait_ge(s_sum, cleared + 2 * k)
                        dve.tensor_tensor(sums[:, 0, META:T], sums[:, 0, META:T], z, ALU.add).then_inc(s_sum, 1)
                        dve.wait_ge(s_sq, st["p0"] + k + 1)
                        dve.tensor_tensor(sums[:, 1, META:T], sums[:, 1, META:T], pair[:, 0, META:T], ALU.add)\
                            .then_inc(s_sum, 1)
                each(dve, st, KD // per, body)

            def layer_norm(st):
                n0, v0 = KD * st["n0"], 5 * st["n0"]

                def centre(k):
                    dve.tensor_tensor(res[:, k, META:T], res[:, k, META:T], ps[:, 5, 0:S], ALU.subtract)\
                        .then_inc(s_cen, 1)

                def low(k):
                    dve.wait_ge(s_xhi, st["x0"] + k + 1)
                    dve.tensor_tensor(x_lo[:, k, META:T], res[:, k, META:T], x_hi[:, k, META:T].bitcast(F32),
                                      ALU.subtract).then_inc(s_xlo, 1)

                dve.wait_ge(s_var, v0 + 1)
                centre(0)
                dve.wait_ge(s_stat, 2 * st["n0"] + 2)
                dve.tensor_tensor(rstd[:, META:T], ps[:, 7, 0:S], pair[:, 1, META:T], ALU.subtract).then_inc(s_var, 1)
                dve.wait_ge(s_var, v0 + 2)
                dve.tensor_scalar(rstd[:, META:T], rstd[:, META:T], 0.0, LN_EPS, ALU.max, ALU.add).then_inc(s_var, 1)
                dve.wait_ge(s_var, v0 + 3)
                dve.reciprocal(rstd[:, META:T], rstd[:, META:T]).then_inc(s_var, 1)
                for k in range(1, 4):
                    centre(k)
                dve.wait_ge(s_var, v0 + 5)
                for k in range(KD):
                    dve.wait_ge(s_cen, n0 + k + 1)
                    dve.tensor_tensor(res[:, k, META:T], res[:, k, META:T], rstd[:, META:T], ALU.mult)\
                        .then_inc(s_nrm, 1)
                    if k + 4 < KD:
                        centre(k + 4)
                    if k >= 2 and st["scaled"]:
                        low(k - 2)
                if st["scaled"]:
                    low(KD - 2)
                    low(KD - 1)

            def pool_in(st):
                def mixed(n):
                    g = n // 2
                    w, done = POOL_WINDOWS[g], win_steps(n)
                    h = w // 2
                    dve.wait_ge(s_evac, st["t0"] + n + 1)
                    src, width, step = upad[:, n % 2, PAD - h:PAD - h + S + w - 1], S + w - 1, 1
                    while step < w:
                        width = S + w - 2 * step
                        dst = win[:, done % 2, 0:width]
                        if done:
                            dve.wait_ge(s_win, done)
                        dve.tensor_tensor(dst, src[:, 0:width], src[:, step:step + width], ALU.add).then_inc(s_win, 1)
                        src, step, done = dst, 2 * step, done + 1
                    dve.wait_ge(s_win, done)
                    dst = win[:, done % 2, 0:S]
                    dve.tensor_tensor(dst, src, invc[:, g, :], ALU.mult).then_inc(s_win, 1)
                    done += 1
                    dve.wait_ge(s_win, done)
                    dve.tensor_tensor(pair[:, n % 2, META:T], dst, upad[:, n % 2, PAD:PAD + S], ALU.subtract)\
                        .then_inc(s_win, 1)

                def low(n):
                    dve.wait_ge(s_hhi, st["h0"] + n + 1)
                    dve.tensor_tensor(h_lo[:, n, META:T], pair[:, n % 2, META:T], h_hi[:, n, META:T].bitcast(F32),
                                      ALU.subtract).then_inc(s_hlo, 1)

                dve.wait_ge(s_tab, 16)
                for n in range(KD):
                    split(st["u0"] + n + AHEAD, (st["u0"] + n + AHEAD) % RING)
                    mixed(n)
                    if n >= 1:
                        low(n - 1)
                low(KD - 1)

            def pool_group(st):
                for v in range(2):
                    split(st["u0"] + v + AHEAD, (st["u0"] + v + AHEAD) % RING)
                    for n in range(4 * v, 4 * v + 4):
                        dve.wait_ge(s_hhi, st["h0"] + n + 1)
                        dve.tensor_tensor(h_lo[:, KD + n, META:T], pair[:, n % 2, META:T],
                                          h_hi[:, KD + n, META:T].bitcast(F32), ALU.subtract).then_inc(s_hlo, 1)

            def values1(st):
                def store(v, j):
                    dve.wait_ge(s_vtr, v + 1)
                    dve.tensor_copy(val[:, :, bass.ds(v * P, P)],
                                    ps[:, 1 + 2 * (j % 2), :].rearrange("p (r n) -> p r n", r=R4)).then_inc(s_val, 1)

                def body(i):
                    for j in range(4):
                        split_ahead(st, i, 4, j)
                        if not (isinstance(i, int) and j == 0):
                            store(4 * i + j - 1, (j - 1) % 4)
                body(0)
                with dve.Fori(1, 3 * KD // 4) as i:
                    body(i)
                store(3 * KD - 1, 3)

            def attend1(st):
                def job(p, m, only_from=0):
                    a = 8 * p + m
                    r, half = m // 2, m % 2
                    if only_from < 1:
                        slope = slopes[:, bass.ds(2 * p + half, 1)]
                        dve.wait_ge(s_score, a + 1)
                        if not (isinstance(a, int) and a < 1):
                            dve.wait_ge(s_pT, a)
                        dve.scalar_tensor_tensor(out=prob[:, 0:S], in0=near[:, R4 - 1 - r:R4 - 1 - r + S], scalar=slope,
                                                 in1=ps[:, 1, :], op0=ALU.mult, op1=ALU.add)
                        dve.scalar_tensor_tensor(out=prob[:, S:S + 2 * NI], in0=far[:, :], scalar=slope,
                                                 in1=ps[:, 3, 0:2 * NI], op0=ALU.mult, op1=ALU.add).then_inc(s_bias, 1)
                        dve.wait_ge(s_bias, a + 1)
                        dve.tensor_reduce(stat[:, half:half + 1], prob[:, :], AX_X, ALU.max, negate=True)\
                            .then_inc(s_max, 1)
                    if only_from < 2 and not (isinstance(a, int) and a < 1):
                        dve.wait_ge(s_exp, a)
                        if not (isinstance(a, int) and a < 3):
                            dve.wait_ge(s_on, a - 2)
                        dve.reciprocal(stat[:, 5 - half:6 - half], stat[:, 3 - half:4 - half]).then_inc(s_rec, 1)
                    if only_from < 3 and not (isinstance(a, int) and a < 2):
                        if not (isinstance(a, int) and a < 6):
                            dve.wait_ge(s_oT, 4 * p + (m - 2) // 2 - 1)
                        dve.wait_ge(s_pv, a - 1)
                        dve.wait_ge(s_rec, a - 1)
                        dve.tensor_scalar(o_tok[:, (r - 1) % 2, half * HD:(half + 1) * HD],
                                          ps[:, 6, half * HD:(half + 1) * HD], stat[:, 4 + half:5 + half], None,
                                          ALU.mult).then_inc(s_on, 1)
                    if half == 0 and not (isinstance(a, int) and a < 4):
                        c = 4 * p + m // 2 - 2
                        rc = (m // 2 - 2) % R4
                        dve.wait_ge(s_oT, c + 1)
                        dst = att[:, bass.ds(p if m >= 4 else p - 1, 1), :].rearrange("p a (i r) -> p (a i) r", r=R4)
                        dve.tensor_copy(dst[:, :, rc], ps[:, 7, 0:P]).then_inc(s_oe, 1)

                def pair_step(p, q, jobs):
                    for c in range(1, 25):
                        if c % 4 == 0:
                            j = c // 4 - 1
                            split(st["u0"] + 6 * p + j + AHEAD, (st["u0"] + 6 * q + j + AHEAD) % RING)
                        if c % 3 == 0 and jobs:
                            job(p - 1, c // 3 - 1)

                dve.wait_ge(s_tab, 3 * 16)
                pair_step(0, 0, False)
                pair_step(1, 1, True)
                pair_step(2, 2, True)
                with dve.Fori(1, KD // 2 - 1) as i:
                    pair_step(2 * i + 1, 1, True)
                    pair_step(2 * i + 2, 2, True)
                pair_step(KD - 1, KD - 1, True)
                for m in range(8):
                    job(KD - 1, m)
                for m in range(3):
                    job(KD, m, only_from=m + 1)
                for k in range(KD):
                    dve.wait_ge(s_xhi, st["x0"] + k + 1)
                    dve.tensor_tensor(x_lo[:, k, META:T], att[:, k, :], x_hi[:, k, META:T].bitcast(F32),
                                      ALU.subtract).then_inc(s_xlo, 1)

            def glu2(st):
                taps = {part: [f"conv{st['l']}{part}{tap}" for tap in range(3)] for part in "gv"}

                def convolve(part, k, c):
                    q = "gv".index(part)
                    src, dst = upad2[:, q, :], pair[:, q, :]

                    def tap(n):
                        at_ = PARAM[taps[part][n]]
                        return par[:, bass.ds(k + at_, 1)]
                    done = 6 * c + 3 * q
                    dve.tensor_scalar(dst, src[:, 2:2 + T], tap(2), None, ALU.mult).then_inc(s_cv, 1)
                    for n in (1, 0):
                        dve.wait_ge(s_cv, done + 2 - n)
                        dve.scalar_tensor_tensor(out=dst, in0=src[:, n:n + T], scalar=tap(n), in1=dst,
                                                 op0=ALU.mult, op1=ALU.add).then_inc(s_cv, 1)

                def body(i):
                    for f in range(2):
                        k = 2 * i + f
                        c = st["c0"] + k
                        split_ahead(st, i, 4, 2 * f)
                        dve.wait_ge(s_evac, st["t0"] + 4 * i + 2 * f + 1)
                        past(dve, s_h, c)
                        convolve("g", k, c)
                        split_ahead(st, i, 4, 2 * f + 1)
                        dve.wait_ge(s_evac, st["t0"] + 4 * i + 2 * f + 2)
                        if not (isinstance(k, int) and k < 1):
                            dve.wait_ge(s_hlo, st["h0"] + k)
                        convolve("v", k, c)
                        dve.wait_ge(s_gate, c + 1)
                        dve.wait_ge(s_cv, 6 * c + 6)
                        dve.tensor_tensor(pair[:, 1, :], pair[:, 0, :], pair[:, 1, :], ALU.mult).then_inc(s_h, 1)
                        dve.wait_ge(s_hhi, st["h0"] + k + 1)
                        h = bass.ds(k, 1)
                        dve.tensor_tensor(h_lo[:, h, :].rearrange("p a t -> p (a t)"), pair[:, 1, :],
                                          h_hi[:, h, :].rearrange("p a t -> p (a t)").bitcast(F32),
                                          ALU.subtract).then_inc(s_hlo, 1)
                dve.wait_ge(s_zero, 1)
                body(0)
                with dve.Fori(1, KF // 2) as i:
                    body(i)

            def project2(st):
                chunks, per = st["chunks"], 4
                cleared = (KD + 1) * st["j0"] + 1
                dve.memset(sums[:, 1, :], 0.0).then_inc(s_sum2, 1)

                def body(i):
                    for n in range(per):
                        for c in range(len(chunks)):
                            split_ahead(st, i, len(chunks) * per, len(chunks) * n + c)
                        k = per * i + n
                        dve.wait_ge(s_mixed, cleared - st["j0"] - 1 + k + 1)
                        dve.wait_ge(s_sum2, cleared + k)
                        dve.tensor_tensor(sums[:, 1, :], sums[:, 1, :], pair[:, 0, :], ALU.add).then_inc(s_sum2, 1)
                each(dve, st, KD // per, body)

            def renorm(st):
                v = 3 * st["v0"]

                def root():
                    dve.tensor_scalar(sbv(rstd, T), psv(3, T), EPS, None, ALU.add).then_inc(s_rv, 1)
                    dve.wait_ge(s_rv, v + 1)
                    dve.reciprocal(rstd[:, :], rstd[:, :]).then_inc(s_rv, 1)
                    dve.wait_ge(s_rv, v + 3)

                if st["after"]:
                    dve.wait_ge(s_rst, st["a0"] // KD + 1)
                    root()
                    v += 3
                    for k in range(KD + 1):
                        if k < KD:
                            dve.scalar_tensor_tensor(out=mix[:, k, :], in0=mix[:, k, :], scalar=par_of(st["after"], k),
                                                     in1=rstd[:, :], op0=ALU.mult, op1=ALU.mult).then_inc(s_mx, 1)
                        if k:
                            dve.wait_ge(s_mx, st["a0"] + k)
                            dve.tensor_tensor(res[:, k - 1, :], res[:, k - 1, :], mix[:, k - 1, :], ALU.add)\
                                .then_inc(s_add, 1)
                if st["outs"]:
                    dve.wait_ge(s_sqp, st["s0"] + KD)
                    root()
                for o, (name, to) in enumerate(st["outs"]):
                    hi, lo, f32, s_h_, s_l_, base_ = ((x_hi, x_lo, mix, s_xhi, s_xlo, st["x0"]) if to == "x" else
                                                     (h_hi, h_lo, h_mix, s_hhi, s_hlo, st["h0"]))
                    for k in range(KD + 2):
                        if k < KD:
                            dve.scalar_tensor_tensor(out=f32[:, k, :], in0=res[:, k, :], scalar=par_of(name, k),
                                                     in1=rstd[:, :], op0=ALU.mult, op1=ALU.mult).then_inc(s_y, 1)
                        if k >= 2:
                            dve.wait_ge(s_h_, base_ + k - 1)
                            dve.tensor_tensor(lo[:, k - 2, :], f32[:, k - 2, :], hi[:, k - 2, :].bitcast(F32),
                                              ALU.subtract).then_inc(s_l_, 1)

            def hgrn(st):
                one_less = 3

                def bounds():
                    l = [par[:, PARAM[f"lb{q}"]:PARAM[f"lb{q}"] + KD] for q in range(2)]
                    dve.tensor_tensor(g_lb[:, 2, :], l[0], l[1], ALU.max).then_inc(G["lb"], 1)
                    dve.wait_ge(G["lb"], 1)
                    for q in range(2):
                        dve.tensor_tensor(g_lb[:, q, :], l[q], g_lb[:, 2, :], ALU.subtract).then_inc(G["lb"], 1)
                    dve.wait_ge(G["lb"], 4)
                    dve.tensor_tensor(g_lb[:, 2, :], g_lb[:, 0, :], g_lb[:, 1, :], ALU.add).then_inc(G["lb"], 1)
                    dve.wait_ge(G["lb"], 5)
                    dve.reciprocal(g_lb[:, 2, :], g_lb[:, 2, :]).then_inc(G["lb"], 1)
                    dve.wait_ge(G["lb"], 6)
                    dve.tensor_tensor(g_lb[:, 0, :], g_lb[:, 0, :], g_lb[:, 2, :], ALU.mult).then_inc(G["lb"], 1)
                    dve.wait_ge(G["lb"], 7)
                    dve.tensor_scalar(g_lb[:, one_less, :], g_lb[:, 0, :], -1.0, 1.0, ALU.mult, ALU.add)\
                        .then_inc(G["lb"], 1)
                    dve.wait_ge(G["lb"], 8)

                def forget(n):
                    dve.wait_ge(s_evac, st["t0"] + 4 * n + 2)
                    dve.tensor_scalar(g_b[:, :], g_b[:, :], g_lb[:, one_less, bass.ds(n, 1)], g_lb[:, 0, bass.ds(n, 1)],
                                      ALU.mult, ALU.add).then_inc(G["f"], 1)
                    dve.wait_ge(G["f"], n + 1)
                    past(dve, G["kout"], n)
                    dve.tensor_scalar(g_k[:, :], g_b[:, :], -1.0, 1.0, ALU.mult, ALU.add).then_inc(G["k"], 1)

                def decays(n):
                    dve.wait_ge(G["ln"], n + 1)
                    dve.tensor_tensor_scan(g_c[:, :], g_chunk[:, :], g_b[:, :], 0.0, ALU.mult, ALU.add)\
                        .then_inc(G["c"], 1)
                    dve.wait_ge(G["c"], n + 1)
                    past(dve, G["turn"], n)
                    dve.tensor_scalar(g_kout[:, 0:META], g_c[:, 0:META], g_c[:, META - 1:META], -1.0,
                                      ALU.subtract, ALU.mult)
                    c3 = g_c[:, META:T].rearrange("p (j t) -> p j t", t=CH)
                    dve.tensor_tensor(g_kout[:, META:T].rearrange("p (j t) -> p j t", t=CH),
                                      c3[:, :, CH - 1:CH].to_broadcast([P, NCH, CH]), c3, ALU.subtract)\
                        .then_inc(G["d"], 1)
                    dve.wait_ge(G["eb"], n + 1)
                    past(dve, G["o"], n)
                    dve.tensor_tensor(g_qin[:, :], g_q[:, :], g_eb[:, :], ALU.mult).then_inc(G["qin"], 1)
                    dve.wait_ge(G["enb"], n + 1)
                    dve.tensor_tensor(g_kin[:, :], g_kin[:, :], g_k[:, :], ALU.mult).then_inc(G["kin"], 1)
                    dve.wait_ge(G["ed"], n + 1)
                    dve.tensor_tensor(g_kout[:, :], g_kout[:, :], g_k[:, :], ALU.mult).then_inc(G["kout"], 1)

                def clip(n):
                    dve.wait_ge(G["score"], n + 1)
                    past(dve, G["o"], n)
                    dve.tensor_copy(g_mt[:, :, :], ps[0:META, 6, 0:2 * P].rearrange("p (b n) -> p b n", n=P))\
                        .then_inc(G["mt"], 1)
                    dve.tensor_tensor(g_at[:, :, :].rearrange("p a b -> p (a b)"), ps[:, 7, :], g_keep[:, 0, :], ALU.min)
                    dve.tensor_tensor(g_atm[:, :], ps[0:META, 6, 2 * P:2 * P + META], g_keep[0:META, 0, 0:META], ALU.min)\
                        .then_inc(G["clip"], 1)
                    dve.wait_ge(G["clip"], n + 1)
                    dve.tensor_tensor(g_at[:, :, :].rearrange("p a b -> p (a b)"),
                                      g_at[:, :, :].rearrange("p a b -> p (a b)"), g_keep[:, 1, :], ALU.max)
                    dve.tensor_tensor(g_atm[:, :], g_atm[:, :], g_keep[0:META, 1, 0:META], ALU.max).then_inc(G["at"], 1)

                def states(n):
                    dve.wait_ge(G["ds"], n + 1)
                    dve.tensor_copy(g_state[:, 0, :], ps[:, 6, 0:P]).then_inc(G["state"], 1)
                    for j in range(NCH - 1):
                        dve.wait_ge(G["state"], NCH * n + j + 1)
                        last = META + CH * j + CH - 1
                        dve.scalar_tensor_tensor(out=g_state[:, j + 1, :], in0=g_state[:, j, :],
                                                 scalar=g_eb[:, last:last + 1],
                                                 in1=ps[:, 4 + j % 2, P * (j // 2):P * (j // 2) + P],
                                                 op0=ALU.mult, op1=ALU.add).then_inc(G["state"], 1)

                def take(n):
                    dve.wait_ge(G["o"], n + 1)
                    if not (isinstance(n, int) and n < 1):
                        dve.wait_ge(s_hlo, st["h0"] + n)
                    dve.tensor_copy(g_o[:, 0:META], ps[:, 6, 0:META]).then_inc(G["oe"], 1)
                    dve.tensor_copy(g_o[:, META:T], ps[:, 7, :]).then_inc(G["oe"], 1)

                def finish(n, odd):
                    dve.wait_ge(G["rs"], n + 1)
                    dve.scalar_tensor_tensor(out=g_o[:, :], in0=g_o[:, :],
                                             scalar=par[:, bass.ds(n + PARAM["head_norm"], 1)], in1=g_rs[:, :],
                                             op0=ALU.mult, op1=ALU.mult).then_inc(G["og"], 1)
                    dve.wait_ge(G["og"], 2 * n + 1)
                    dve.tensor_tensor(g_o[:, :], g_o[:, :], g_gate[:, odd, :], ALU.mult).then_inc(G["og"], 1)
                    dve.wait_ge(s_hhi, st["h0"] + n + 1)
                    h = bass.ds(n, 1)
                    dve.tensor_tensor(h_lo[:, h, :].rearrange("p a t -> p (a t)"), g_o[:, :],
                                      h_hi[:, h, :].rearrange("p a t -> p (a t)").bitcast(F32),
                                      ALU.subtract).then_inc(s_hlo, 1)

                def with_eps(n):
                    dve.wait_ge(G["ms"], n + 1)
                    past(dve, G["og"], 2 * n)
                    dve.tensor_scalar(sbv(g_rs, T), psv(2, T), float(D // P), EPS, ALU.mult, ALU.add)\
                        .then_inc(G["eps"], 1)

                def step(n, odd, before, before2):
                    if before:
                        decays(n - 1)
                    split(st["u0"] + 4 * n + 0 + AHEAD, (st["u0"] + 0 + AHEAD) % RING)
                    if before2:
                        with_eps(n - 2)
                        finish(n - 2, odd)
                    split(st["u0"] + 4 * n + 1 + AHEAD, (st["u0"] + 1 + AHEAD) % RING)
                    forget(n)
                    if before:
                        clip(n - 1)
                    split(st["u0"] + 4 * n + 2 + AHEAD, (st["u0"] + 2 + AHEAD) % RING)
                    if before:
                        states(n - 1)
                    split(st["u0"] + 4 * n + 3 + AHEAD, (st["u0"] + 3 + AHEAD) % RING)
                    if before:
                        take(n - 1)

                bounds()
                dve.wait_ge(G["tab"], 32)
                dve.tensor_scalar(g_keep[:, 1, :], g_keep[:, 0, :], -1.0, None, ALU.mult).then_inc(G["neg"], 1)
                dve.wait_ge(G["neg"], 1)
                step(0, 0, False, False)
                step(1, 1, True, False)
                step(2, 0, True, True)
                step(3, 1, True, True)
                with dve.Fori(2, KD // 2) as i:
                    step(2 * i, 0, True, True)
                    step(2 * i + 1, 1, True, True)
                decays(KD - 1)
                with_eps(KD - 2)
                finish(KD - 2, 0)
                clip(KD - 1)
                states(KD - 1)
                take(KD - 1)
                with_eps(KD - 1)
                finish(KD - 1, 1)

            def fox_values(st):
                z = f_b[:, :, :]
                ones = sums[:, 0, :]
                dve.memset(ones, 1.0).then_inc(FX["one"], 1)

                def gates(step):
                    if step == 0:
                        dve.wait_ge(s_evac, st["t0"] + 1)
                        dve.scalar_tensor_tensor(out=z[:, 1, :], in0=z[:, 0, :], scalar=-1.0, in1=z[:, 0, :],
                                                 op0=ALU.mult, op1=ALU.max).then_inc(FX["c"], 1)
                    if step == 1:
                        dve.wait_ge(FX["c"], 2)
                        dve.tensor_scalar(z[:, 1, :], z[:, 1, :], 1.0, None, ALU.add).then_inc(FX["c"], 1)
                    if step == 2:
                        dve.wait_ge(FX["c"], 4)
                        dve.scalar_tensor_tensor(out=z[:, 1, :], in0=z[:, 0, :], scalar=0.0, in1=z[:, 1, :],
                                                 op0=ALU.min, op1=ALU.subtract).then_inc(FX["c"], 1)
                    if step == 3:
                        dve.wait_ge(FX["c"], 5)
                        dve.wait_ge(FX["one"], 1)
                        dve.tensor_tensor_scan(f_c[:, :], ones, z[:, 1, :], 0.0, ALU.mult, ALU.add)\
                            .then_inc(FX["c"], 1)
                        dve.wait_ge(FX["c"], 6)
                        dve.tensor_copy(f_a[:, :], f_c[:, :]).then_inc(FX["c"], 1)
                        dve.wait_ge(FX["c"], 7)
                        dve.memset(f_a[FG:2 * FG, :], -1.0).then_inc(FX["one"], 1)

                for n in range(1 + KD):
                    split(st["u0"] + n + AHEAD, (st["u0"] + n + AHEAD) % RING)
                    gates(n - 1)
                    if n >= 3:
                        store(n - 3)
                store(KD - 2)
                store(KD - 1)

            def store(v):
                dve.wait_ge(FX["vtr"], v + 1)
                dve.tensor_copy(f_val[:, :, P * v:P * v + P], ps[:, 4 + v % 2, :].rearrange("p (b n) -> p b n", n=P))
                dve.tensor_copy(f_vmeta[:, P * v:P * v + P], ps[0:META, 6 + v % 2, 0:P]).then_inc(FX["val"], 1)

            def fox(st):
                def key_side(p, half):
                    dve.tensor_scalar(f_b[:, half, :], f_c[:, :],
                                      ident[:, bass.ds(2 * p + (FG + half), 1)],
                                      ident[:, bass.ds(2 * p + half, 1)], ALU.mult, ALU.add)\
                        .then_inc(FX["b"], 1)

                def job(p, m, only_from=0):
                    a = NJ * p + m
                    if only_from < 1:
                        nk = fox_block(FOX_JOBS[m][1])[1]
                        bank = 6 if m % 2 else 2
                        s = ps[:, bank:bank + 2, :].rearrange("p a n -> p (a n)")[:, 0:nk]
                        if m == 2:
                            past(dve, FX["score"], NJ * p)
                            key_side(p, 1)
                        if m == 7 and not (isinstance(p, int) and p == KD - 1):
                            dve.wait_ge(FX["score"], NJ * p + 5)
                            key_side(p + 1, 0)
                        dve.wait_ge(FX["score"], a + 1)
                        if back(p, m, 2):
                            dve.wait_ge(FX["exp"], a - 1)
                        dve.tensor_reduce(stat[:, m % 2:m % 2 + 1], s, AX_X, ALU.max, negate=True)\
                            .then_inc(FX["max"], 1)
                    if only_from < 2 and back(p, m, 1):
                        mm = (m - 1) % NJ
                        dve.wait_ge(FX["exp"], a)
                        if back(p, m, 3):
                            dve.wait_ge(FX["on"], a - 2)
                        dve.reciprocal(stat[:, 4 + mm % 2:5 + mm % 2], stat[:, 2 + mm % 2:3 + mm % 2])\
                            .then_inc(FX["rec"], 1)
                    if only_from < 3 and back(p, m, 2):
                        mm = (m - 2) % NJ
                        half, b = FOX_JOBS[mm]
                        dve.wait_ge(FX["pv"], a - 1)
                        dve.wait_ge(FX["rec"], a - 1)
                        dve.tensor_scalar(f_otok[:, b, half * HD:(half + 1) * HD], ps[:, 7, 0:HD],
                                          stat[:, 4 + mm % 2:5 + mm % 2], None, ALU.mult).then_inc(FX["on"], 1)
                    if back(p, m, 3) and FOX_JOBS[(m - 3) % NJ][0]:
                        pp, mm = back(p, m, 3)
                        b = FOX_JOBS[mm][1]
                        q0, nq = fox_block(b)[0], P if b else META
                        dve.wait_ge(FX["oT"], out_count(pp, mm))
                        dve.tensor_copy(f_o[:, bass.ds(pp, 1), q0:q0 + nq].rearrange("p a n -> p (a n)"),
                                        ps[:, 7, P:P + nq]).then_inc(FX["oe"], 1)

                def pair_step(p, q, jobs):
                    for c in range(1, 2 * KD + 1):
                        if c % KD == 0:
                            j = c // KD - 1
                            split(st["u0"] + 2 * p + j + AHEAD, (st["u0"] + 2 * q + j + AHEAD) % RING)
                        if jobs and c in FOX_AT:
                            job(p - 1, FOX_AT[c])

                dve.wait_ge(FX["c"], 7)
                dve.wait_ge(FX["one"], 2)
                key_side(0, 0)
                pair_step(0, 0, False)
                pair_step(1, 1, True)
                pair_step(2, 2, True)
                with dve.Fori(1, KD // 2 - 1) as i:
                    pair_step(2 * i + 1, 1, True)
                    pair_step(2 * i + 2, 2, True)
                pair_step(KD - 1, KD - 1, True)
                for m in range(NJ):
                    job(KD - 1, m)
                for m in range(3):
                    job(KD, m, only_from=m + 1)
                for k in range(KD):
                    dve.wait_ge(s_hhi, st["h0"] + k + 1)
                    dve.tensor_tensor(h_lo[:, k, :], f_o[:, k, :], h_hi[:, k, :].bitcast(F32), ALU.subtract)\
                        .then_inc(s_hlo, 1)

            run = dict(load=load, glu=glu, project=project, layer_norm=layer_norm, pool_in=pool_in,
                       pool_group=pool_group, values1=values1, attend1=attend1, glu2=glu2, project2=project2,
                       renorm=renorm, hgrn=hgrn, fox_values=fox_values, fox=fox)
            for st in STAGES:
                if st["kind"] in run:
                    run[st["kind"]](st)

        @block.gpsimd
        def _(pool):
            def scale_residual(x0, r0):
                for k in range(KD):
                    pool.wait_ge(s_xlo, x0 + k + 1)
                    pool.tensor_scalar(res[:, k, META:T], res[:, k, META:T], ALPHA, None, ALU.mult).then_inc(s_res, 1)

            for st in STAGES:
                if st["kind"] == "load":
                    scale_residual(st["x0"], st["r0"])
                if st["kind"] == "layer_norm" and st["scaled"]:
                    scale_residual(st["x0"], st["r0"])
                if st["kind"] == "pool_in":
                    pool.memset(upad[:, :, :], 0.0).then_inc(s_pad, 1)
                    pool.dma_start(invc[:, :, :], consts[:, C_POOL:C_POOL + 4 * S].rearrange("p (g s) -> p g s", g=4))\
                        .then_inc(s_tab, 16)
                if st["kind"] == "hgrn":
                    pool.wait_ge(s_xlo, st["x0"])
                    pool.dma_start(g_chunk[:, :], consts[:, C_CHUNK:C_CHUNK + T]).then_inc(G["tab"], 16)
                    pool.dma_start(g_keep[:, 0, :], consts[:, C_KEEP:C_KEEP + S]).then_inc(G["tab"], 16)
                if st["kind"] == "fox_values":
                    pool.wait_ge(s_xlo, st["x0"])
                    pool.dma_start(f_mask[:, :], consts[:, C_CAUSAL:C_CAUSAL + P]).then_inc(FX["tab"], 16)
                if st["kind"] == "glu2" and not st["c0"]:
                    pool.memset(upad2[:, :, 0:2], 0.0).then_inc(s_zero, 1)
                if st["kind"] == "values1":
                    pool.dma_start(near[:, :], consts[:, C_NEAR:C_NEAR + N_NEAR]).then_inc(s_tab, 16)
                    pool.dma_start(far[:, :], consts[:, C_FAR:C_FAR + 2 * NI]).then_inc(s_tab, 16)


def win_steps(n):
    return sum(POOL_WINDOWS[k // 2].bit_length() - 1 + 2 for k in range(n))


def table(w):
    out = np.zeros((P, N_PARAM), np.float32)

    def put(name, v):
        n = -(-v.size // P)
        padded = np.zeros(n * P, np.float32)
        padded[:v.size] = v
        out[:, PARAM[name]:PARAM[name] + n] = padded.reshape(n, P).T

    for l in range(2):
        for j in range(3):
            put(f"ln_gain{l}{j}", w["ln_gain"][l, j])
            put(f"ln_bias{l}{j}", w["ln_bias"][l, j])
    put("pool_scale", w["pool_scale"][0])
    for l in range(2):
        for j in range(4):
            put(f"norm{l}{j}", w["norm_gains_2"][l, j])
        for tap in range(3):
            put(f"conv{l}g{tap}", w["ffn_conv_2"][l, tap, :FF2])
            put(f"conv{l}v{tap}", w["ffn_conv_2"][l, tap, FF2:])
        put(f"lb{l}", w["a_lb_logits_2"][l])
    put("head_norm", w["a_head_norm_2"][0])
    put("kv_norm", w["kv_norm_2"])
    for row in (0, FG):
        out[row:row + HEADS, PARAM["fg_b"]] = w["fg_b_2"]
    return out


def host_arrays(w):
    return dict(
        wstream=weight_stream(w),
        xT=np.ascontiguousarray(w["x"][0].T),
        metaT=np.ascontiguousarray(w["meta_tokens_2"].T),
        params=table(w),
        consts=constants(),
    )


def kernel(**inputs):
    import concourse.bacc as bacc
    from concourse.bass_utils import run_bass_kernel_spmd

    arrays = host_arrays({k: np.asarray(v) for k, v in inputs.items()})
    nc = bacc.Bacc("TRN2", target_bir_lowering=False, num_devices=1)
    args = [nc.dram_tensor(k, a.shape, F32, kind="ExternalInput").ap() for k, a in arrays.items()]
    out = nc.dram_tensor("out", (D, S), F32, kind="ExternalOutput").ap()
    build(nc, *args, out)
    r = run_bass_kernel_spmd(nc, [arrays], core_ids=[0])
    return np.ascontiguousarray(r.results[0]["out"].T)[None]
```

```python
from contextlib import ExitStack

import numpy as np

import concourse.bass as bass
from concourse import mybir

F32 = mybir.dt.float32
F32R = mybir.dt.float32r
ACT = mybir.ActivationFunctionType
ALU = mybir.AluOpType
AX_X = mybir.AxisListType.X

P = 128
D = 1024
KD = D // P
S = 512
META = 16
T = S + META
FF = 2816
KF = FF // P
FF2 = 2752
RING = 4
AHEAD = 2
ALPHA = 4.0 ** 0.25
LN_EPS = 1e-5
EPS = 1e-6
POOL_WINDOWS = (2, 4, 8, 16)
PAD = 8
ON_SCALAR = (3, 7)
LATE = {1: 4, 3: 1}
K_CHUNKS = (8, 8, 6)
HEADS = 16
HD = 64
DIL = ((64, 1), (64, 4), (64, 16))
R4 = 4
NI = S // R4
MASKED = -1e30
CH = 64
FG = 32
FOX_JOBS = tuple((0, b) for b in range(5)) + tuple((1, b) for b in (0, 1, 2, 4, 3))
FOX_AT = {-(-16 * (m + 1) // len(FOX_JOBS)): m for m in range(len(FOX_JOBS))}
NCH = S // CH


def param_columns():
    out = {}
    at = 0
    sizes = [(f"ln_{what}{l}{j}", KD) for l in range(2) for j in range(3) for what in ("gain", "bias")]
    sizes += [("pool_scale", KD)]
    sizes += [(f"norm{l}{j}", KD) for l in range(2) for j in range(4)]
    sizes += [(f"conv{l}{part}{tap}", KF) for l in range(2) for part in "gv" for tap in range(3)]
    sizes += [("lb0", KD), ("lb1", KD), ("head_norm", KD), ("kv_norm", KD), ("fg_b", 1)]
    for name, n in sizes:
        out[name] = at
        at += n
    return out, at


PARAM, N_PARAM = param_columns()

C_ID = 0
C_MEAN = C_ID + P
C_POOL = C_MEAN + P
C_NEAR = C_POOL + 4 * S
N_NEAR = S + R4 - 1
C_FAR = C_NEAR + N_NEAR
C_SLOPE = C_FAR + 2 * NI
C_CHUNK = C_SLOPE + HEADS
C_KEEP = C_CHUNK + T
C_CAUSAL = C_KEEP + S
N_CONST = C_CAUSAL + P


def constants():
    c = np.zeros((P, N_CONST), np.float32)
    c[:, C_ID:C_ID + P] = np.eye(P)
    c[:, C_MEAN:C_MEAN + P] = 1.0 / D
    t = np.arange(S)
    for g, w in enumerate(POOL_WINDOWS):
        count = np.minimum(t + w // 2, S) - np.maximum(t - w // 2, 0)
        c[:, C_POOL + g * S:C_POOL + (g + 1) * S] = 1.0 / count
    i = np.arange(P)[:, None]
    dist = np.abs(4 * i - (np.arange(N_NEAR)[None, :] - (R4 - 1)))
    c[:, C_NEAR:C_NEAR + N_NEAR] = np.where(dist <= DIL[0][0], -dist, MASKED)
    steps = np.abs(i - np.arange(NI)[None, :])
    n = 3 * HEADS
    slopes = 2.0 ** (-8.0 * np.arange(1, n + 1) / n)
    near = np.where(steps <= DIL[1][0], -4.0 * steps, MASKED)
    same = np.where(steps % 4 == 0, -4.0 * steps, MASKED)
    c[:, C_FAR:C_FAR + NI] = near * (slopes[HEADS] / slopes[0])
    c[:, C_FAR + NI:C_FAR + 2 * NI] = same * (slopes[2 * HEADS] / slopes[0])
    c[:, C_SLOPE:C_SLOPE + HEADS] = slopes[:HEADS]
    c[:, C_CHUNK:C_CHUNK + T] = 1.0
    c[:, [C_CHUNK] + [C_CHUNK + META + CH * j for j in range(S // CH)]] = 0.0
    q = np.arange(P)[None, :]
    keep = (i // CH == q // CH) & (i <= q)
    c[:, C_KEEP:C_KEEP + S] = np.tile(np.where(keep, np.finfo(np.float32).max, 0.0), (1, S // P))
    c[:, C_CAUSAL:C_CAUSAL + P] = np.where(i >= q, 0.0, MASKED)
    return c


def plan():
    stages = []
    at = dict(u0=0, t0=0, z0=0, e0=0, n0=0, g0=0, h0=0, q0=0, p0=0, x0=0,
              c0=0, j0=0, w0=0, v0=0, a0=0, i0=0, s0=0, y0=0)

    def add(kind, counts={}, **more):
        lead = stages[-1].get("lead", 0) if stages else 0
        held = [st["halved"] for st in stages if "halved" in st][-1:] or [0]
        stages.append(dict(kind=kind, led=max(0, lead - AHEAD), held=held[0], **at, **more))
        for key, n in counts.items():
            at[key + "0"] += n

    def down(kind, units, chunks, lead, **more):
        halved = LATE[len(chunks)]
        sums = dict(q=1 + 2 * (KD + halved), p=KD + halved) if kind == "project" else \
            dict(j=1 + KD + halved, w=KD + halved)
        add(kind, dict(u=units, t=KD, z=halved, e=halved * len(chunks), **sums, **more.pop("counts")),
            chunks=chunks, halved=halved, lead=lead, **more)

    def project(source, src0, chunks, coef, l, j, lead):
        scaled = (l, j) != (1, 2)
        down("project", len(chunks) * KD, chunks, lead, counts=dict(n=1, x=2 * KD * scaled), source=source,
             src0=src0, coef=coef, l=l, j=j, scaled=scaled)

    def inputs(*outs):
        return dict(i=1, s=2 * KD, y=KD * (1 + len(outs)), x=2 * KD, h=KD * (len(outs) - 1)) if outs else {}

    def project2(units, chunks, lead, after, *outs):
        down("project2", units, chunks, lead, counts=dict(v=1, a=2 * KD, **inputs(*outs)), after=after, outs=outs)

    def ffn2(l, lead, after, *outs):
        add("glu2", dict(u=2 * KF, t=2 * KF, c=KF, h=KF), l=l)
        project2(3 * KD, K_CHUNKS, lead, after, *outs)

    def ffn1(l, j, lead):
        add("glu", dict(u=2 * KF, t=2 * KF, g=KF, h=KF))
        project("h", 0, K_CHUNKS, 0.5, l, j, lead)

    add("load", dict(x=2 * KD), lead=4)
    ffn1(0, 0, lead=4)
    add("pool_in", dict(u=KD, t=KD, h=KD))
    add("pool_group", dict(u=2, t=KD, h=KD))
    project("h", KD, (KD,), 1.0, 0, 1, lead=4)
    ffn1(0, 2, lead=4)
    ffn1(1, 0, lead=4)
    add("values1", dict(u=3 * KD, t=3 * KD))
    add("attend1", dict(u=6 * KD, t=6 * KD, x=KD))
    project("x", 0, (KD,), 1.0, 1, 1, lead=4)
    ffn1(1, 2, lead=2)
    outs = (("norm00", "x"),)
    add("renorm", inputs(*outs), outs=outs)
    add("hgrn", dict(u=4 * KD, t=4 * KD, h=KD))
    project2(KD, (KD,), 4, "norm01", ("norm02", "x"))
    ffn2(0, 2, "norm03", ("kv_norm", "x"), ("norm10", "h"))
    add("fox_values", dict(u=1 + KD, t=1 + KD))
    add("fox", dict(u=2 * KD, t=2 * KD, h=KD))
    project2(KD, (KD,), 4, "norm11", ("norm12", "x"))
    ffn2(1, 0, "norm13")
    add("end")
    return stages, at["u0"]


STAGES, UNITS = plan()


def weight_stream(w):
    def tiles(m):
        k, n = m.shape
        return m.reshape(k // P, P, n // P, P).transpose(2, 1, 0, 3)

    units = np.zeros((UNITS, P, KD, P), np.float32)
    at = 0

    def put(u):
        nonlocal at
        units[at, :, :u.shape[1]] = u
        at += 1

    def ffn(gate, up, down):
        g, v, d = tiles(gate), tiles(up), tiles(down)
        for f in range(KF):
            put(g[f])
            put(v[f])
        for n in range(KD):
            k = 0
            for kn in K_CHUNKS:
                put(d[n][:, k:k + kn])
                k += kn

    def every(m):
        for u in tiles(m):
            put(u)

    def ffn1(l, which):
        ffn(w[f"ffn{which}_w_gate"][l], w[f"ffn{which}_w_up"][l], w[f"ffn{which}_w_down"][l])

    ffn1(0, 1)
    every(w["pool_w_in"][0])
    for v in range(2):
        two = [tiles(w["pool_w_group"][0][2 * v + g]) for g in range(2)]
        put(np.concatenate([two[g][e] for g in range(2) for e in range(2)], axis=1))
    every(w["pool_w_out"][0])
    ffn1(0, 2)
    ffn1(1, 1)
    qkv = tiles(w["attn_w_qkv"][0]).reshape(3, 3, KD, P, KD, P)
    for g in range(3):
        for n in range(KD):
            put(qkv[g, 2, n])
    for n in range(KD):
        for g in range(3):
            put(qkv[g, 0, n])
            put(qkv[g, 1, n])
    every(w["attn_w_out"][0])
    ffn1(1, 2)
    parts = tiles(w["a_w_in_2"][0]).reshape(4, KD, P, KD, P)
    for n in range(KD):
        for part in range(4):
            put(parts[part, n])
    every(w["a_w_out_2"][0])

    def ffn2(l):
        both, down = w["ffn_w_up_2"][l], w["ffn_w_down_2"][l]
        wide = [np.zeros((D, FF), np.float32) for _ in range(2)]
        wide[0][:, :FF2], wide[1][:, :FF2] = both[:, :FF2], both[:, FF2:]
        tall = np.zeros((FF, D), np.float32)
        tall[:FF2] = down
        ffn(wide[0], wide[1], tall)

    ffn2(0)
    kv, gates = w["kv_w_2"], np.zeros((D, P), np.float32)
    gates[:, :HEADS] = gates[:, FG:FG + HEADS] = kv[:, 2 * D:]
    put(tiles(gates)[0])
    every(kv[:, D:2 * D])
    k_tiles, q_tiles = tiles(kv[:, :D]), tiles(w["b_w_q_2"][0])
    for n in range(KD):
        put(k_tiles[n])
        put(q_tiles[n])
    every(w["b_w_out_2"][0])
    ffn2(1)
    assert at == UNITS
    return units


def build(nc, wstream, xT, metaT, params, consts, out):
    with ExitStack() as ctx:
        top = [0]

        def at(name, shape, dt=F32, offset=None):
            size = -(-int(np.prod(shape[1:])) * 4 // 64) * 64
            if offset is None:
                offset = top[0]
                top[0] += size
            assert base + offset + size <= nc.sbuf_usable_end, (name, offset, size)
            return nc.alloc_sbuf_tensor_at(name, shape, dt, offset=base + offset)

        def sem(name):
            return ctx.enter_context(nc.semaphore(name))

        base = -(-nc.sbuf_base // 64) * 64

        raw = at("raw", [P, RING, KD, P])
        w_hi = at("w_hi", [P, RING, KD, P], F32R)
        w_lo = at("w_lo", [P, RING, KD, P], F32R)
        res = at("res", [P, KD, T])
        x_hi = at("x_hi", [P, KD, T], F32R)
        x_lo_at = top[0]
        x_lo = at("x_lo", [P, KD, T], F32R)
        par = at("par", [P, N_PARAM])
        ident = at("ident", [P, P])
        mean_w = at("mean_w", [P, P])
        slopes = at("slopes", [P, HEADS])
        stat = at("stat", [P, 8])
        eps = at("eps", [P, 1])
        scaled = at("scaled", [P, 2 * 3 * 2 * KD])
        mixer0 = top[0]
        sums = at("sums", [P, 2, T])
        rstd = at("rstd", [P, T])
        pair = at("pair", [P, 2, T])
        upad2 = at("upad2", [P, 2, T + 2])
        hidden0 = top[0]
        h_hi = at("h_hi", [P, KF, T], F32R)
        h_lo = at("h_lo", [P, KF, T], F32R)
        top[0] = hidden0 + 2 * KD * T * 4
        invc = at("invc", [P, 4, S])
        upad = at("upad", [P, 2, PAD + S + PAD])
        assert top[0] <= hidden0 + KF * T * 4
        top[0] = hidden0 + (KF + 2 * KD) * T * 4
        win = at("win", [P, 2, PAD + S + PAD])
        top[0] = mixer0
        val = at("val", [P, R4, 3 * D])
        att = at("att", [P, KD, S])
        qk = at("qk", [P, 2, 6, S])
        prob = at("prob", [P, S + 2 * NI])
        probT = at("probT", [P, S + 2 * NI])
        near = at("near", [P, N_NEAR])
        far = at("far", [P, 2 * NI])
        o_tok = at("o_tok", [P, 2, P])
        vT = at("vT", [P, 2, S], offset=mixer0 + (R4 * 3 * D + KD * S + 2 * 6 * S) * 4)
        mix = at("mix", [P, KD, T], offset=x_lo_at)
        h_mix = at("h_mix", [P, KD, T], offset=hidden0 + KF * T * 4)
        top[0] = hidden0 + KD * T * 4
        g_q = at("g_q", [P, T])
        g_k = at("g_k", [P, T])
        g_b = at("g_b", [P, T])
        g_c = at("g_c", [P, T])
        g_eb = at("g_eb", [P, T])
        g_qin = at("g_qin", [P, T])
        g_kin = at("g_kin", [P, T])
        g_kout = at("g_kout", [P, T])
        g_v = at("g_v", [P, T])
        g_gate = at("g_gate", [P, 2, T])
        g_o = at("g_o", [P, T])
        g_rs = at("g_rs", [P, T])
        assert top[0] <= hidden0 + KF * T * 4
        top[0] = hidden0 + (KF + KD) * T * 4
        g_chunk = at("g_chunk", [P, T])
        g_keep = at("g_keep", [P, 2, S])
        g_kt = at("g_kt", [P, 4, P])
        g_vt = at("g_vt", [P, 4, P])
        g_mt = at("g_mt", [META, 2, P])
        g_at = at("g_at", [P, 4, P])
        g_atm = at("g_atm", [META, META])
        g_state = at("g_state", [P, NCH, P])
        g_lb = at("g_lb", [P, 4, KD])
        top[0] = hidden0 + KD * T * 4
        f_o = at("f_o", [P, KD, T])
        f_qk = at("f_qk", [P, 2, 2, T])
        f_b = at("f_b", [P, 2, T])
        assert top[0] <= hidden0 + KF * T * 4
        top[0] = hidden0 + (KF + KD) * T * 4
        f_val = at("f_val", [P, 4, D])
        f_vmeta = at("f_vmeta", [META, D])
        f_a = at("f_a", [P, T])
        f_c = at("f_c", [P, T])
        f_mask = at("f_mask", [P, P])
        f_otok = at("f_otok", [P, 5, P])
        f_probT = at("f_probT", [P, 2, 5, P], offset=mixer0)
        f_prob = pair
        ps = ctx.enter_context(nc.psum_tensor("ps", [P, 8, 512], F32))

        s_load = [sem(f"s_load{i}") for i in range(RING)]
        s_init = sem("s_init")
        s_x = [[sem(f"s_x{h}{k}") for k in range(KD // 2)] for h in range(2)]
        s_tab = sem("s_tab")
        s_hi = sem("s_hi")
        s_lo = sem("s_lo")
        s_unit = sem("s_unit")
        s_evac = sem("s_evac")
        s_silu = sem("s_silu")
        s_hhi = sem("s_hhi")
        s_hlo = sem("s_hlo")
        s_sq = sem("s_sq")
        s_sum = sem("s_sum")
        s_za = sem("s_za")
        s_ua = sem("s_ua")
        s_stat = sem("s_stat")
        s_var = sem("s_var")
        s_cen = sem("s_cen")
        s_nrm = sem("s_nrm")
        s_aff = sem("s_aff")
        s_affs = sem("s_affs")
        s_affv = sem("s_affv")
        s_xhi = sem("s_xhi")
        s_xlo = sem("s_xlo")
        s_res = sem("s_res")
        s_eps = sem("s_eps")
        s_pad = sem("s_pad")
        s_win = sem("s_win")
        s_vtr = sem("s_vtr")
        s_val = sem("s_val")
        s_score = sem("s_score")
        s_bias = sem("s_bias")
        s_max = sem("s_max")
        s_exp = sem("s_exp")
        s_pT = sem("s_pT")
        s_pTe = sem("s_pTe")
        s_pv = sem("s_pv")
        s_rec = sem("s_rec")
        s_on = sem("s_on")
        s_oT = sem("s_oT")
        s_oe = sem("s_oe")
        s_mixed = sem("s_mixed")
        s_sum2 = sem("s_sum2")
        s_rst = sem("s_rst")
        s_root1 = sem("s_root1")
        s_root2 = sem("s_root2")
        s_mx = sem("s_mx")
        s_add = sem("s_add")
        s_sqr = sem("s_sqr")
        s_sqp = sem("s_sqp")
        s_y = sem("s_y")
        s_u = sem("s_u")
        s_zero = sem("s_zero")
        s_cv = sem("s_cv")
        s_gate = sem("s_gate")
        s_h = sem("s_h")
        G = {name: sem("s_g_" + name) for name in (
            "tab", "neg", "lb", "sig", "f", "k", "ln", "c", "eb", "enb", "d", "ed", "qin", "kin", "kout", "turn", "kt",
            "vt", "mt", "score", "clip", "at", "ds", "state", "o", "oe", "sq", "ms", "eps", "lnr", "rs", "og", "oh")}
        FX = {name: sem("s_f_" + name) for name in (
            "tab", "one", "c", "vtr", "val", "b", "score", "max", "exp", "pT", "pTe", "rec", "pv", "on", "oT", "oe")}
        s_out = sem("s_out")

        def two_banks(tok):
            return tok == T

        def psv(slot, tok=S):
            if two_banks(tok):
                return ps[:, 2 * slot:2 * slot + 2, 0:T // 2]
            return ps[:, 2 * slot, 0:S]

        def sbv(ap, tok=S):
            if two_banks(tok):
                return ap.rearrange("p (a b) -> p a b", a=2)
            return ap[:, META:T]

        def halves(tok):
            return [(0, 0, T // 2), (1, T // 2, T // 2)] if two_banks(tok) else [(0, META, S)]

        def half_of(tok, h):
            return (h * (T // 2), T // 2) if two_banks(tok) else (META + h * (S // 2), S // 2)

        def half_cols(tok, h):
            c0, n = half_of(tok, h)
            return slice(c0, c0 + n)

        def half_bank(slot, tok, h):
            return ps[:, 2 * slot + h, 0:half_of(tok, h)[1]]

        def beside(st, k, tile=None, split=None):
            tiles, units = ({-1: (0, 1), 2: (2,), 5: (3,)}, {-1: (0, 1), 2: (2,), 5: (3,)}) \
                if len(st["chunks"]) == 1 else ({4: (0,)}, {0: (1,), 3: (2,), 5: (3,)})
            for q in tiles.get(k, ()) if tile else ():
                tile(q)
            for j in units.get(k, ()) if split else ():
                if j < st["lead"]:
                    u = st["u0"] + len(st["chunks"]) * KD + j
                    split(u, u % RING)

        def own_units(st):
            n = len(st["chunks"])
            return range(st["u0"] + n * (KD - st["halved"]) + AHEAD,
                         st["u0"] + n * KD + (st["lead"] > 0 and n * st["halved"] < RING))

        def par_of(name, k):
            return par[:, PARAM[name] + k:PARAM[name] + k + 1]

        def scaled_of(name, k):
            return scaled[:, PARAM[name] + k:PARAM[name] + k + 1]

        def by_residue(ap):
            return ap.rearrange("p (r i) -> p i r", r=R4)

        def in_order(ap):
            return ap.rearrange("p (i r) -> p i r", r=R4)

        def past(eng, s, n):
            if not (isinstance(n, int) and n < 1):
                eng.wait_ge(s, n)

        NJ = len(FOX_JOBS)

        def back(p, m, lag):
            if isinstance(p, int) and NJ * p + m < lag:
                return None
            return (p, m - lag) if m >= lag else (p - 1, m - lag + NJ)

        def fox_block(b):
            return (META + P * (b - 1), META + P * b) if b else (0, META)

        def out_count(p, m):
            return p * 5 + max(m - 4, 0)

        def by_bank(lo, hi):
            return [(c, min(hi, e) - c, b) for b, c, e in ((0, lo, 512), (1, max(lo, 512), hi)) if c < min(hi, e)]

        block = ctx.enter_context(nc.Block())

        @block.sync
        def _(sp):
            x_in = xT.rearrange("(k p) t -> p k t", p=P)
            sp.dma_start(raw[:, 0], wstream[0]).then_inc(s_load[0], 16)
            for h in range(2):
                for k in range(0, KD, 2):
                    sp.dma_start(res[:, k:k + 2, half_cols(S, h)], x_in[:, k:k + 2, h * (S // 2):(h + 1) * (S // 2)])\
                        .then_inc(s_x[h][k // 2], 16)
                for u in (1, 2) if h == 0 else (3,):
                    sp.dma_start(raw[:, u], wstream[u]).then_inc(s_load[u], 16)
            for dst, src in ((par[:, :], params), (ident[:, :], consts[:, C_ID:C_ID + P]),
                             (mean_w[:, :], consts[:, C_MEAN:C_MEAN + P]),
                             (slopes[:, :], consts[:, C_SLOPE:C_SLOPE + HEADS]),
                             (res[:, :, 0:META], metaT.rearrange("(k p) t -> p k t", p=P))):
                sp.dma_start(dst, src).then_inc(s_init, 16)
            whole = UNITS // RING
            with sp.Fori(1, whole) as i:
                for j in range(RING):
                    sp.wait_ge(s_lo, i * RING + (j - RING + 1))
                    sp.dma_start(raw[:, j], wstream[bass.ds(i * RING + j, 1)].rearrange("a p k n -> (a p) k n"))\
                        .then_inc(s_load[j], 16)
            for u in range(whole * RING, UNITS):
                sp.wait_ge(s_lo, u - RING + 1)
                sp.dma_start(raw[:, u % RING], wstream[u]).then_inc(s_load[u % RING], 16)
            for h in range(2):
                c0, n = half_of(T, h)
                skip = META if h == 0 else 0
                for k in range(0, KD, 2):
                    sp.wait_ge(s_add, STAGES[-1]["a0"] - 2 * KD + KD * h + k + 2)
                    sp.dma_start(out.rearrange("(k p) t -> p k t", p=P)[:, k:k + 2, c0 + skip - META:c0 + n - META],
                                 res[:, k:k + 2, c0 + skip:c0 + n]).then_inc(s_out, 16)
            sp.wait_ge(s_out, KD * 16)

        @block.tensor
        def _(pe):
            x_src = (x_hi, x_lo)
            h_src = (h_hi, h_lo)

            def products(bank, slot, wt, src, k, c0, n, first, last):
                hi, lo = src
                for q, (w, x) in enumerate(((w_hi, hi), (w_lo, hi), (w_hi, lo))):
                    m = pe.matmul(ps[:, bank, 0:n], w[:, slot, wt, :], x[:, k, c0:c0 + n],
                                  start=first and q == 0, stop=last and q == 2)
                return m

            def unit(u, slot, tile_slot, tok, src, k0, kn, first=True, last=True, ready=None, between=None):
                pe.wait_ge(s_lo, u + 1)
                for k in range(kn):
                    if ready is not None:
                        pe.wait_ge(ready[0], ready[1] + k)
                    for a, c0, n in halves(tok):
                        m = products(2 * tile_slot + a, slot, k, src, k0 + k, c0, n,
                                     first and k == 0, last and k == kn - 1)
                    if k == kn - 1:
                        m.then_inc(s_unit, 1)
                    if between is not None:
                        between(k)

            late = []

            def first_units(st, count, tok):
                if st["t0"]:
                    pe.wait_ge(s_evac, st["t0"] - st["held"])
                    pe.wait_ge(s_za, st["z0"])
                for h in range(2):
                    if h and st["t0"]:
                        pe.wait_ge(s_evac, st["t0"])
                    c0, n = half_of(tok, h)
                    for j in range(count):
                        if h == 0:
                            pe.wait_ge(s_lo, st["u0"] + j + 1)
                        for k in range(KD):
                            if j == 0:
                                pe.wait_ge(s_xlo, st["x0"] - 2 * KD + KD * h + k + 1)
                            dst = 2 * j + h if two_banks(tok) else 2 * j
                            hi, lo = x_src
                            at0 = 0 if two_banks(tok) else h * n
                            for q, (w, x) in enumerate(((w_hi, hi), (w_lo, hi), (w_hi, lo))):
                                m = pe.matmul(ps[:, dst, at0:at0 + n], w[:, (st["u0"] + j) % RING, k, :],
                                              x[:, k, c0:c0 + n], start=k == 0 and q == 0, stop=k == KD - 1 and q == 2)
                            if h == 0:
                                for f in late:
                                    f(j, k)
                        if h == 1:
                            m.then_inc(s_unit, 1)
                late.clear()


            def glu(st):
                tok = T if st["kind"] == "glu2" else S
                first_units(st, RING, tok)
                with pe.Fori(1, 2 * KF // 4) as i:
                    for j in range(4):
                        u, t = st["u0"] + 4 * i + j, st["t0"] + 4 * i + j
                        pe.wait_ge(s_evac, t - RING + 1)
                        unit(u, (st["u0"] + j) % RING, j, tok, x_src, 0, KD)

            def project(st):
                chunks, tok, halved = st["chunks"], T if st["kind"] == "project2" else S, st["halved"]
                src = x_src if st.get("source") == "x" else h_src
                s_in, in0 = (s_xlo, st["x0"]) if src is x_src else (s_hlo, st["h0"])
                in0 -= sum(chunks)
                full = KD - halved
                for n in range(full):
                    pe.wait_ge(s_evac, st["t0"] + n - RING + 1)
                    k0 = 0
                    for c, kn in enumerate(chunks):
                        u = st["u0"] + len(chunks) * n + c
                        unit(u, u % RING, n % RING, tok, src, k0 + st.get("src0", 0), kn, c == 0, c == len(chunks) - 1,
                             ready=(s_in, in0 + k0 + 1) if n == 0 else None)
                        k0 += kn
                for h in range(2):
                    c0, width = half_of(tok, h)
                    for n in range(full, KD):
                        if h == 0:
                            pe.wait_ge(s_evac, st["t0"] + n - RING + 1)
                        k0 = 0
                        for c, kn in enumerate(chunks):
                            u = st["u0"] + len(chunks) * n + c
                            if h == 0:
                                pe.wait_ge(s_lo, u + 1)
                            for k in range(kn):
                                m = products(2 * (n % RING) + h, u % RING, k, src, st.get("src0", 0) + k0 + k, c0, width,
                                             k0 + k == 0, k0 + k == sum(chunks) - 1)
                            m.then_inc(s_unit if h else s_ua, 1)
                            k0 += kn
                            v = len(chunks) * (n - full) + c
                            if h == 1 and v == 0:
                                sums_of(st, 0)
                            elif h == 1 and st.get("outs"):
                                squares_of(st, 0, range(2 * v - 2, 2 * v))
                if st.get("outs"):
                    squares_of(st, 0, range(2 * (halved * len(chunks) - 1), KD))
                if tok == S and st["scaled"]:
                    at1 = (0, 5) if halved == 1 else (0, 7)
                    late.append(lambda j, k: sums_of(st, 1) if (j, k) == at1 else None)
                else:
                    sums_of(st, 1)
                if st.get("outs"):
                    late.append(lambda j, k: squares_of(st, 1, [k]) if j == 1 else None)

            def sums_of(st, h):
                full = KD - st["halved"]
                if st["kind"] == "project":
                    if not st["n0"]:
                        pe.wait_ge(s_init, 5 * 16)
                    for q in range(2):
                        pe.wait_ge(s_sum, st["q0"] + 2 * full + 2 * st["halved"] * (h + 1) + q)
                        pe.matmul(ps[:, h + 2 * q, 0:S // 2], mean_w[:, :], sums[:, q, half_cols(S, h)],
                                  start=True, stop=True).then_inc(s_stat, 1)
                else:
                    if st["halved"] == 1:
                        pe.wait_ge(s_evac, st["t0"] + 6)
                    elif h == 0:
                        pe.wait_ge(s_za, st["z0"] + 2)
                    else:
                        pe.wait_ge(s_evac, st["t0"] + 6)
                    pe.wait_ge(s_sum2, st["j0"] + 1 + full + st["halved"] * (h + 1))
                    pe.matmul(ps[:, h, 0:T // 2], mean_w[:, :], sums[:, 1, half_cols(T, h)], start=True, stop=True)\
                        .then_inc(s_rst, 1)

            def squares_of(st, h, tiles):
                for k in tiles:
                    pe.wait_ge(s_sqr, st["s0"] + KD * h + k + 1)
                    pe.matmul(ps[:, 2 + h, 0:T // 2], mean_w[:, :], pair[:, k % 2, half_cols(T, h)],
                              start=k == 0, stop=k == KD - 1).then_inc(s_sqp, 1)

            def renorm(st):
                squares_of(st, 0, range(KD))
                late.append(lambda j, k: squares_of(st, 1, [k]) if j == 1 else None)

            def pool_in(st):
                first_units(st, RING, S)
                for n in range(RING, KD):
                    u, t = st["u0"] + n, st["t0"] + n
                    pe.wait_ge(s_evac, t - RING + 1)
                    unit(u, u % RING, n % RING, S, x_src, 0, KD)

            def pool_group(st):
                for v in range(2):
                    u = st["u0"] + v
                    pe.wait_ge(s_lo, u + 1)
                    for w in range(KD):
                        n, k = 4 * v + w // 2, 4 * v + 2 * (w // 4) + w % 2
                        t = st["t0"] + n
                        if k % 2 == 0:
                            pe.wait_ge(s_evac, t - RING + 1)
                        pe.wait_ge(s_hlo, st["h0"] - KD + k + 1)
                        m = products(2 * (n % RING), u % RING, w, h_src, k, META, S, k % 2 == 0, k % 2 == 1)
                    m.then_inc(s_unit, 1)

            def values1(st):
                def turn(v, j):
                    pe.wait_ge(s_evac, st["t0"] + v + 1)
                    if not (isinstance(v, int) and v < 2):
                        pe.wait_ge(s_val, v - 1)
                    for r in range(R4):
                        m = pe.transpose(ps[:, 1 + 2 * (j % 2), r * P:(r + 1) * P],
                                         vT[:, j % 2, r * P:(r + 1) * P], ident[:, :])
                    m.then_inc(s_vtr, 1)

                first_units(st, RING, S)
                for v in range(3):
                    turn(v, v)
                with pe.Fori(1, 3 * KD // 4) as i:
                    for j in range(4):
                        u, t = st["u0"] + 4 * i + j, st["t0"] + 4 * i + j
                        pe.wait_ge(s_evac, t - RING + 1)
                        unit(u, (st["u0"] + j) % RING, j, S, x_src, 0, KD)
                        turn(4 * i + j - 1, (j - 1) % 4)
                turn(3 * KD - 1, 3)

            def attend1(st):
                def head(half):
                    return slice(HD * half, HD * half + HD)

                def scores(a, m, buf, p):
                    r, hs = m // 2, head(m % 2)
                    if m == 0:
                        pe.wait_ge(s_evac, st["t0"] + 6 * p + 6)
                    if not (isinstance(a, int) and a < 1):
                        pe.wait_ge(s_bias, a)
                    q = [qk[hs, buf, 2 * g, r * NI:(r + 1) * NI] for g in range(3)]
                    pe.matmul(ps[:, 1, 0:S], q[0], qk[hs, buf, 1, :], start=True, stop=True)
                    for g in (1, 2):
                        mm = pe.matmul(ps[:, 3, (g - 1) * NI:g * NI], q[g],
                                       qk[hs, buf, 2 * g + 1, r * NI:(r + 1) * NI], start=True, stop=True)
                    mm.then_inc(s_score, 1)

                def turn(a):
                    pe.wait_ge(s_exp, a + 1)
                    if not (isinstance(a, int) and a < 1):
                        pe.wait_ge(s_pTe, a)
                    for b in range(6):
                        mm = pe.transpose(ps[:, 4 + b // 4, (b % 4) * P:(b % 4 + 1) * P],
                                          prob[:, b * P:(b + 1) * P], ident[:, :])
                    mm.then_inc(s_pT, 1)

                def weigh(a, m, p):
                    r, half = m // 2, m % 2
                    pe.wait_ge(s_pTe, a + 1)
                    if not (isinstance(a, int) and a < 1):
                        pe.wait_ge(s_on, a)
                    for b in range(6):
                        g, tile = (0, b) if b < 4 else (b - 3, r)
                        v = val[:, tile, bass.ds(g * D + P * p + HD * half, HD)]
                        mm = pe.matmul(ps[:, 6, half * HD:(half + 1) * HD], probT[:, b * P:(b + 1) * P], v,
                                       start=b == 0, stop=b == 5)
                    mm.then_inc(s_pv, 1)

                def turn_out(c, r):
                    pe.wait_ge(s_on, 2 * c + 2)
                    if not (isinstance(c, int) and c < 1):
                        pe.wait_ge(s_oe, c)
                    pe.transpose(ps[:, 7, 0:P], o_tok[:, r % 2, :], ident[:, :]).then_inc(s_oT, 1)

                def job(p, m, buf, only_from=0):
                    a = 8 * p + m
                    if only_from < 1:
                        scores(a, m, buf, p)
                    if only_from < 2 and not (isinstance(a, int) and a < 1):
                        turn(a - 1)
                    if only_from < 3 and not (isinstance(a, int) and a < 2):
                        weigh(a - 2, (m - 2) % 8, p if m >= 2 else p - 1)
                    if m % 2 == 0 and not (isinstance(a, int) and a < 4):
                        turn_out(4 * p + m // 2 - 2, (m // 2 - 2) % R4)

                def pair_step(p, q, buf, jobs):
                    count = [0]
                    for j in range(6):
                        u, t = st["u0"] + 6 * p + j, st["t0"] + 6 * p + j
                        pe.wait_ge(s_evac, t - 1)

                        def between(k):
                            if k % 2:
                                count[0] += 1
                                if count[0] % 3 == 0 and jobs:
                                    job(p - 1, count[0] // 3 - 1, 1 - buf)
                        unit(u, (st["u0"] + 6 * q + j) % RING, j % 2, S, x_src, 0, KD, between=between)

                pe.wait_ge(s_val, 3 * KD)
                pair_step(0, 0, 0, False)
                pair_step(1, 1, 1, True)
                pair_step(2, 2, 0, True)
                with pe.Fori(1, KD // 2 - 1) as i:
                    pair_step(2 * i + 1, 1, 1, True)
                    pair_step(2 * i + 2, 2, 0, True)
                pair_step(KD - 1, KD - 1, 1, True)
                for m in range(8):
                    job(KD - 1, m, 1)
                for m in range(3):
                    job(KD, m, 0, only_from=m + 1)

            def hgrn(st):
                real = slice(META, T)

                def cols(b):
                    return slice(META + P * b, META + P * b + P)

                def turn_and_score(n):
                    pe.wait_ge(G["kout"], n + 1)
                    past(pe, G["kt"], n)
                    past(pe, G["vt"], n)
                    past(pe, G["mt"], n)
                    if not (isinstance(n, int) and n < 1):
                        pe.wait_ge(G["state"], NCH * n)
                        pe.wait_ge(G["eps"], n)
                        pe.wait_ge(G["oe"], 2 * n)
                    for b in range(4):
                        pe.transpose(ps[:, 4, P * b:P * b + P], g_kout[:, cols(b)], ident[:, :])
                    for b in range(4):
                        pe.transpose(ps[:, 5, P * b:P * b + P], g_v[:, cols(b)], ident[:, :])
                    pe.transpose(ps[0:META, 6, 0:P], g_kout[:, 0:META], ident[:, :])
                    pe.transpose(ps[0:META, 6, P:2 * P], g_v[:, 0:META], ident[:, :]).then_inc(G["turn"], 1)
                    for b in range(4):
                        pe.matmul(ps[:, 7, P * b:P * b + P], g_kin[:, cols(b)], g_qin[:, cols(b)],
                                  start=True, stop=True)
                    pe.matmul(ps[0:META, 6, 2 * P:2 * P + META], g_kin[:, 0:META], g_qin[:, 0:META],
                              start=True, stop=True).then_inc(G["score"], 1)

                def state_steps(n):
                    pe.wait_ge(G["kt"], n + 1)
                    pe.wait_ge(G["vt"], n + 1)
                    pe.wait_ge(G["mt"], n + 1)
                    pe.wait_ge(G["at"], n + 1)
                    pe.matmul(ps[:, 6, 0:P], g_mt[:, 0, :], g_mt[:, 1, :], start=True, stop=True)
                    for j in range(NCH - 1):
                        rows = slice(CH * (j % 2), CH * (j % 2) + CH)
                        m = pe.matmul(ps[:, 4 + j % 2, P * (j // 2):P * (j // 2) + P], g_kt[rows, j // 2, :],
                                      g_vt[rows, j // 2, :], start=True, stop=True)
                    m.then_inc(G["ds"], 1)

                def outputs(n):
                    pe.wait_ge(G["state"], NCH * (n + 1))
                    pe.matmul(ps[:, 6, 0:META], g_mt[:, 1, :], g_atm[:, :], start=True, stop=True)
                    for b in range(4):
                        pe.matmul(ps[:, 7, P * b:P * b + P], g_vt[:, b, :], g_at[:, b, :], start=True, stop=False)
                        for j in (2 * b, 2 * b + 1):
                            m = pe.matmul(ps[:, 7, CH * j:CH * j + CH], g_state[:, j, :],
                                          g_qin[:, META + CH * j:META + CH * j + CH], start=False, stop=j == 2 * b + 1)
                    m.then_inc(G["o"], 1)

                def mean_square(n):
                    pe.wait_ge(G["sq"], n + 1)
                    for a, c0, w in halves(T):
                        m = pe.matmul(ps[:, 4 + a, 0:w], mean_w[:, :], pair[:, 0, c0:c0 + w], start=True, stop=True)
                    m.then_inc(G["ms"], 1)

                def step(n, odd, before, before2):
                    start = isinstance(n, int) and n == 0
                    if start:
                        first_units(st, 2, T)
                    for j in range(2 if start else 0, 4):
                        u, t = st["u0"] + 4 * n + j, st["t0"] + 4 * n + j
                        pe.wait_ge(s_evac, t - 1)
                        unit(u, (st["u0"] + j) % RING, j % 2, T, x_src, 0, KD)
                        if j == 0 and before2:
                            mean_square(n - 2)
                        if j >= 1 and before:
                            (turn_and_score, state_steps, outputs)[j - 1](n - 1)

                step(0, 0, False, False)
                step(1, 1, True, False)
                step(2, 0, True, True)
                step(3, 1, True, True)
                with pe.Fori(2, KD // 2) as i:
                    step(2 * i, 0, True, True)
                    step(2 * i + 1, 1, True, True)
                mean_square(KD - 2)
                turn_and_score(KD - 1)
                state_steps(KD - 1)
                outputs(KD - 1)
                mean_square(KD - 1)

            def fox_values(st):
                def turn(v):
                    pe.wait_ge(s_evac, st["t0"] + v + 2)
                    if v >= 2:
                        pe.wait_ge(FX["val"], v - 1)
                    for b in range(4):
                        pe.transpose(ps[:, 4 + v % 2, P * b:P * b + P],
                                     pair[:, v % 2, META + P * b:META + P * b + P], ident[:, :])
                    pe.transpose(ps[0:META, 6 + v % 2, 0:P], pair[:, v % 2, 0:META], ident[:, :])\
                        .then_inc(FX["vtr"], 1)

                first_units(st, 2, T)
                for n in range(2, 1 + KD):
                    u, t = st["u0"] + n, st["t0"] + n
                    pe.wait_ge(s_evac, t - 1)
                    unit(u, u % RING, n % 2, T, x_src, 0, KD)
                    turn(n - 2)
                turn(KD - 1)

            def fox(st):
                def head(half):
                    return slice(HD * half, HD * half + HD)

                def scores(p, m, buf):
                    half, b = FOX_JOBS[m]
                    q0, nk = fox_block(b)
                    own = P if b else META
                    a, hs, bank = NJ * p + m, head(half), 6 if m % 2 else 2
                    if m == 0:
                        pe.wait_ge(s_evac, st["t0"] + 2 * p + 2)
                    if m % 5 == 0:
                        pe.wait_ge(FX["b"], 2 * p + half + 1)
                    if back(p, m, 2):
                        pe.wait_ge(FX["exp"], a - 1)
                    def at_bank(rows, c, n, k):
                        return ps[0:rows, bank + k, c - 512 * k:c - 512 * k + n]
                    for c, n, k in by_bank(0, nk):
                        pe.matmul(at_bank(P, c, n, k), f_a[:, q0:q0 + P], f_b[:, half, c:c + n],
                                  start=True, stop=False)
                    for c, n, k in by_bank(nk - own, nk):
                        pe.matmul(at_bank(own, c, n, k), ident[0:own, 0:own],
                                  f_mask[0:own, c - nk + own:c - nk + own + n], start=False, stop=False)
                    for c, n, k in by_bank(0, nk):
                        mm = pe.matmul(at_bank(P, c, n, k), f_qk[hs, buf, 1, q0:q0 + P], f_qk[hs, buf, 0, c:c + n],
                                       start=False, stop=True)
                    mm.then_inc(FX["score"], 1)

                def turn(p, m):
                    pe.wait_ge(FX["exp"], NJ * p + m + 1)
                    past(pe, FX["pTe"], NJ * p + m)
                    mm = pe.transpose(ps[0:META, 5, 0:P], f_prob[:, m % 2, 0:META], ident[:, :])
                    for j in range(FOX_JOBS[m][1]):
                        mm = pe.transpose(ps[:, 4, P * j:P * j + P],
                                          f_prob[:, m % 2, META + P * j:META + P * j + P], ident[:, :])
                    mm.then_inc(FX["pT"], 1)

                def turn_out(p, m):
                    pe.transpose(ps[:, 7, P:2 * P], f_otok[:, FOX_JOBS[m][1], :], ident[:, :]).then_inc(FX["oT"], 1)

                def weigh(p, m):
                    half, b = FOX_JOBS[m]
                    cols = bass.ds(P * p + HD * half, HD)
                    mm = pe.matmul(ps[:, 7, 0:HD], f_probT[0:META, m % 2, 0, :], f_vmeta[:, cols],
                                   start=True, stop=b == 0)
                    for j in range(b):
                        mm = pe.matmul(ps[:, 7, 0:HD], f_probT[:, m % 2, 1 + j, :], f_val[:, j, cols],
                                       start=False, stop=j == b - 1)
                    mm.then_inc(FX["pv"], 1)

                def job(p, m, buf, only_from=0):
                    if only_from < 1:
                        scores(p, m, buf)
                    if only_from < 3 and back(p, m, 2):
                        pe.wait_ge(FX["pTe"], NJ * p + m - 1)
                    if back(p, m, 3):
                        pe.wait_ge(FX["on"], NJ * p + m - 2)
                    if back(p, m, 4):
                        past(pe, FX["oe"], out_count(*back(p, m, 4)))
                    if only_from < 2 and back(p, m, 1):
                        turn(*back(p, m, 1))
                    if back(p, m, 3) and FOX_JOBS[(m - 3) % NJ][0]:
                        turn_out(*back(p, m, 3))
                    if only_from < 3 and back(p, m, 2):
                        weigh(*back(p, m, 2))

                def pair_step(p, q, buf, jobs):
                    for j in range(2):
                        u, t = st["u0"] + 2 * p + j, st["t0"] + 2 * p + j
                        pe.wait_ge(s_evac, t)

                        def between(k):
                            c = KD * j + k + 1
                            if jobs and c in FOX_AT:
                                job(p - 1, FOX_AT[c], 1 - buf)
                        unit(u, (st["u0"] + 2 * q + j) % RING, 0, T, (x_src, h_src)[j], 0, KD, between=between)

                pe.wait_ge(FX["val"], KD)
                pe.wait_ge(FX["tab"], 16)
                pe.wait_ge(s_hlo, st["h0"])
                pair_step(0, 0, 0, False)
                pair_step(1, 1, 1, True)
                pair_step(2, 2, 0, True)
                with pe.Fori(1, KD // 2 - 1) as i:
                    pair_step(2 * i + 1, 1, 1, True)
                    pair_step(2 * i + 2, 2, 0, True)
                pair_step(KD - 1, KD - 1, 1, True)
                for m in range(NJ):
                    job(KD - 1, m, 1)
                for m in range(3):
                    job(KD, m, 0, only_from=m + 1)

            run = dict(glu=glu, project=project, pool_in=pool_in, pool_group=pool_group,
                       values1=values1, attend1=attend1, glu2=glu, project2=project, renorm=renorm, hgrn=hgrn,
                       fox_values=fox_values, fox=fox)
            for st in STAGES:
                if st["kind"] in run:
                    run[st["kind"]](st)

        @block.scalar
        def _(act):
            def split(u, slot):
                if isinstance(u, int) and u >= UNITS:
                    return
                act.wait_ge(s_load[slot], (u // RING + 1) * 16 if isinstance(u, int) else (u - slot) * 4 + 16)
                if not (isinstance(u, int) and u < RING):
                    act.wait_ge(s_unit, u - RING + 1)
                act.activation(w_hi[:, slot], raw[:, slot], ACT.Copy).then_inc(s_hi, 1)

            def split_ahead(st, i, per, j):
                if isinstance(i, int) and i == 0 and j < st.get("led", 0):
                    return
                u = st["u0"] + per * i + j + AHEAD
                split(u, u % RING if isinstance(u, int) else (st["u0"] + j + AHEAD) % RING)

            def load(st):
                split(0, 0)
                for h in range(2):
                    for k in range(KD):
                        if k % 2 == 0:
                            act.wait_ge(s_x[h][k // 2], 16)
                        act.activation(x_hi[:, k, half_cols(S, h)], res[:, k, half_cols(S, h)], ACT.Copy)\
                            .then_inc(s_xhi, 1)
                    for u in (1, 2) if h == 0 else (3,):
                        split(u, u)

            def glu(st):
                def body(i):
                    for f in range(2):
                        h = st["h0"] + 2 * i + f
                        g = st["g0"] + 2 * i + f
                        slot = (2 * f) % RING
                        split_ahead(st, i, 4, 2 * f)
                        act.wait_ge(s_unit, st["u0"] + 4 * i + 2 * f + 1)
                        if not (isinstance(h, int) and h < 2):
                            act.wait_ge(s_hlo, h - 1)
                        act.activation(pair[:, f, META:T], psv(slot), ACT.Silu).then_inc(s_silu, 1)
                        split_ahead(st, i, 4, 2 * f + 1)
                        act.wait_ge(s_evac, st["t0"] + 4 * i + 2 * f + 2)
                        k = 2 * i + f
                        act.activation(h_hi[:, bass.ds(k, 1), META:T].rearrange("p a t -> p (a t)"),
                                       pair[:, f, META:T], ACT.Copy).then_inc(s_hhi, 1)
                body(0)
                with act.Fori(1, KF // 2) as i:
                    body(i)

            def project(st):
                chunks, full, m = st["chunks"], KD - st["halved"], st["halved"]

                def square(k, h, before):
                    act.wait_ge(s_sum, st["q0"] + 1 + 2 * before)
                    c = slice(META, T) if h is None else half_cols(S, h)
                    act.activation(pair[:, 0, c], res[:, k, c], ACT.Square).then_inc(s_sq, 1)

                def root(h):
                    v = 10 * st["n0"] + 5 * h
                    act.wait_ge(s_stat, 4 * st["n0"] + 2 * h + 1)
                    act.activation(sums[:, 0, half_cols(S, h)], ps[:, h, 0:S // 2], ACT.Copy)
                    act.activation(pair[:, 1, half_cols(S, h)], ps[:, h, 0:S // 2], ACT.Square).then_inc(s_var, 1)
                    act.wait_ge(s_var, v + 3)
                    r = rstd[:, half_cols(S, h)]
                    act.activation(r, r, ACT.Ln).then_inc(s_var, 1)
                    act.wait_ge(s_var, v + 4)
                    act.activation(r, r, ACT.Exp, scale=-0.5).then_inc(s_var, 1)

                def affine(h, k):
                    n = 2 * KD * st["n0"] + KD * h + k + 1
                    r = res[:, k, half_cols(S, h)]
                    gain, bias = f"ln_gain{st['l']}{st['j']}", f"ln_bias{st['l']}{st['j']}"
                    act.wait_ge(s_nrm, n)
                    if not st["scaled"]:
                        act.activation(r, r, ACT.Identity, bias=par_of(bias, k), scale=par_of(gain, k))\
                            .then_inc(s_aff, 1)
                        return
                    act.activation(x_hi[:, k, half_cols(S, h)], r, ACT.Identity, bias=par_of(bias, k),
                                   scale=par_of(gain, k)).then_inc(s_xhi, 1)
                    if k not in ON_SCALAR:
                        return
                    act.wait_ge(s_xhi, st["x0"] + KD * h + k + 1)
                    act.activation(r, r, ACT.Identity, bias=scaled_of(bias, k), scale=scaled_of(gain, k))\
                        .then_inc(s_affs, 1)

                def late_tile(q):
                    act.wait_ge(s_evac, st["t0"] + full + q + 1)
                    square(full + q, 1, full + m + q)

                if not st["n0"]:
                    act.wait_ge(s_res, KD + 1)

                for k in range(full):
                    for c in range(len(chunks)):
                        split_ahead(st, k, len(chunks), c)
                    act.wait_ge(s_evac, st["t0"] + k + 1)
                    square(k, None, k)
                for u in own_units(st):
                    split(u, u % RING)
                for q in range(m):
                    act.wait_ge(s_za, st["z0"] + q + 1)
                    square(full + q, 0, full + q)
                root(0)
                beside(st, -1, late_tile, split)
                for k in range(KD):
                    affine(0, k)
                    beside(st, k, late_tile, split)
                root(1)
                for k in range(KD):
                    affine(1, k)

            def pool_in(st):
                for n in range(KD):
                    split_ahead(st, 0, 1, n)
                    act.wait_ge(s_unit, st["u0"] + n + 1)
                    if n < 2:
                        act.wait_ge(s_pad, 1)
                    else:
                        act.wait_ge(s_win, win_steps(n - 1))
                    act.activation(upad[:, n % 2, PAD:PAD + S], psv(n % RING), ACT.Copy)\
                        .then_inc(s_evac, 1)
                    if n >= 1:
                        high_mixed(n - 1)
                high_mixed(KD - 1)

            def high_mixed(n):
                act.wait_ge(s_win, win_steps(n + 1))
                act.activation(h_hi[:, n, META:T], pair[:, n % 2, META:T], ACT.Copy).then_inc(s_hhi, 1)

            def pool_group(st):
                for v in range(2):
                    split(st["u0"] + v + AHEAD, (st["u0"] + v + AHEAD) % RING)
                    act.wait_ge(s_unit, st["u0"] + v + 1)
                    for n in range(4 * v, 4 * v + 4):
                        act.wait_ge(s_hlo, st["h0"] + n - 1)
                        act.activation(pair[:, n % 2, META:T], psv(n % RING), ACT.Copy,
                                       scale=par_of("pool_scale", n)).then_inc(s_evac, 1)
                        act.wait_ge(s_evac, st["t0"] + n + 1)
                        act.activation(h_hi[:, KD + n, META:T], pair[:, n % 2, META:T], ACT.Copy).then_inc(s_hhi, 1)

            def values1(st):
                def value(v, j, permuted):
                    if not isinstance(v, int):
                        split(st["u0"] + v + AHEAD, (st["u0"] + j + AHEAD) % RING)
                    else:
                        split_ahead(st, 0, 1, v)
                    act.wait_ge(s_unit, st["u0"] + v + 1)
                    if not (isinstance(v, int) and v < 2):
                        act.wait_ge(s_vtr, v - 1)
                    dst, src = vT[:, j % 2, :], psv(j % RING)
                    if permuted:
                        dst, src = by_residue(dst), in_order(src)
                    act.activation(dst, src, ACT.Copy).then_inc(s_evac, 1)

                for v in range(KD):
                    value(v, v % 4, False)
                with act.Fori(KD // 4, 3 * KD // 4) as i:
                    for j in range(4):
                        value(4 * i + j, j, True)

            def attend1(st):
                def job(p, m, only_from=0):
                    a = 8 * p + m
                    if only_from < 2 and not (isinstance(a, int) and a < 1):
                        act.wait_ge(s_pT, a)
                        if not (isinstance(a, int) and a < 2):
                            act.wait_ge(s_pv, a - 1)
                        act.activation(probT[:, :], ps[:, 4:6, :].rearrange("p a b -> p (a b)")[:, 0:S + 2 * NI],
                                       ACT.Copy).then_inc(s_pTe, 1)
                    if only_from < 1:
                        act.wait_ge(s_max, a + 1)
                        act.activation(prob[:, :], prob[:, :], ACT.Exp, bias=stat[:, m % 2:m % 2 + 1],
                                       accum_out=stat[:, 2 + m % 2:3 + m % 2]).then_inc(s_exp, 1)

                def pair_step(p, q, buf, jobs):
                    for c in range(1, 25):
                        if c % 4 == 0:
                            j = c // 4 - 1
                            v = 6 * p + j
                            split(st["u0"] + v + AHEAD, (st["u0"] + 6 * q + j + AHEAD) % RING)
                            act.wait_ge(s_unit, st["u0"] + v + 1)
                            if not (isinstance(p, int) and p < 2):
                                act.wait_ge(s_score, 8 * p - 8)
                            dst, src = qk[:, buf, j, :], psv(j % 2)
                            if j != 1:
                                dst, src = by_residue(dst), in_order(src)
                            act.activation(dst, src, ACT.Copy, scale=1.0 if j % 2 else HD ** -0.5)\
                                .then_inc(s_evac, 1)
                        if c % 3 == 0 and jobs:
                            job(p - 1, c // 3 - 1)

                pair_step(0, 0, 0, False)
                pair_step(1, 1, 1, True)
                pair_step(2, 2, 0, True)
                with act.Fori(1, KD // 2 - 1) as i:
                    pair_step(2 * i + 1, 1, 1, True)
                    pair_step(2 * i + 2, 2, 0, True)
                pair_step(KD - 1, KD - 1, 1, True)
                for m in range(8):
                    job(KD - 1, m)
                job(KD, 0, only_from=1)
                act.wait_ge(s_unit, st["u0"] + 6 * KD)
                for k in range(KD):
                    act.wait_ge(s_oe, R4 * (k + 1))
                    act.activation(x_hi[:, k, META:T], att[:, k, :], ACT.Copy).then_inc(s_xhi, 1)

            def glu2(st):
                def high(k, h):
                    act.wait_ge(s_h, h + 1)
                    act.activation(h_hi[:, bass.ds(k, 1), :].rearrange("p a t -> p (a t)"), pair[:, 1, :],
                                   ACT.Copy).then_inc(s_hhi, 1)

                def body(i):
                    for f in range(2):
                        k = 2 * i + f
                        c = st["c0"] + k
                        slot = 2 * f
                        split_ahead(st, i, 4, 2 * f)
                        act.wait_ge(s_unit, st["u0"] + 4 * i + 2 * f + 1)
                        if not (isinstance(c, int) and c < 1):
                            act.wait_ge(s_cv, 6 * c - 3)
                        act.activation(sbv(upad2[:, 0, 2:], T), psv(slot, T), ACT.Copy).then_inc(s_evac, 1)
                        if not (isinstance(k, int) and k < 1):
                            high(k - 1, c - 1)
                        split_ahead(st, i, 4, 2 * f + 1)
                        act.wait_ge(s_unit, st["u0"] + 4 * i + 2 * f + 2)
                        past(act, s_cv, 6 * c)
                        act.activation(sbv(upad2[:, 1, 2:], T), psv(slot + 1, T), ACT.Copy).then_inc(s_evac, 1)
                        act.wait_ge(s_cv, 6 * c + 3)
                        act.activation(pair[:, 0, :], pair[:, 0, :], ACT.Silu).then_inc(s_gate, 1)
                body(0)
                with act.Fori(1, KF // 2) as i:
                    body(i)
                high(KF - 1, st["c0"] + KF - 1)

            def project2(st):
                chunks, full, m = st["chunks"], KD - st["halved"], st["halved"]

                def take(k, h, before):
                    act.wait_ge(s_sum2, st["j0"] + 1 + before)
                    if h is None:
                        src, c = psv(k % RING, T), slice(0, T)
                        dst, sq = sbv(mix[:, k, :], T), sbv(pair[:, 0, :], T)
                    else:
                        src, c = half_bank(k % RING, T, h), half_cols(T, h)
                        dst, sq = mix[:, k, c], pair[:, 0, c]
                    act.activation(sq, src, ACT.Square).then_inc(s_mixed, 1)
                    act.activation(dst, src, ACT.Copy).then_inc(s_za if h == 0 else s_evac, 1)

                def late_tile(q):
                    act.wait_ge(s_unit, st["u0"] + len(chunks) * (full + q + 1))
                    take(full + q, 1, full + m + q)

                for k in range(full):
                    for c in range(len(chunks)):
                        split_ahead(st, k, len(chunks), c)
                    act.wait_ge(s_unit, st["u0"] + len(chunks) * (k + 1))
                    take(k, None, k)
                for u in own_units(st):
                    split(u, u % RING)
                for q in range(m):
                    act.wait_ge(s_ua, st["e0"] + len(chunks) * (q + 1))
                    take(full + q, 0, full + q)
                root(0, s_rst, 2 * st["v0"] + 1, 0, s_root1, 4 * st["v0"])
                beside(st, -1, late_tile, split)
                for k in range(KD):
                    if st["outs"]:
                        square(st, 0, k)
                    beside(st, k, late_tile, split)
                root(1, s_rst, 2 * st["v0"] + 2, 1, s_root1, 4 * st["v0"] + 2)
                if st["outs"]:
                    next_input(st)

            def root(h, s_ms, ready, bank, s_step, done):
                r = rstd[:, half_cols(T, h)]
                act.wait_ge(s_ms, ready)
                if done < 2 and s_step is s_root2:
                    act.wait_ge(s_eps, 1)
                act.activation(r, ps[:, bank, 0:T // 2], ACT.Ln, bias=eps[:, 0:1]).then_inc(s_step, 1)
                act.wait_ge(s_step, done + 1)
                act.activation(r, r, ACT.Exp, scale=-0.5).then_inc(s_step, 1)

            def square(st, h, k):
                n = KD * h + k
                if st["kind"] == "renorm":
                    act.wait_ge(s_aff, n + 1)
                else:
                    act.wait_ge(s_add, st["a0"] + n + 1)
                past(act, s_sqp, st["s0"] + n - 1 if k > 1 else st["s0"] + KD * h)
                act.activation(pair[:, k % 2, half_cols(T, h)], res[:, k, half_cols(T, h)], ACT.Square)\
                    .then_inc(s_sqr, 1)

            def next_input(st):
                def high(h, k):
                    act.wait_ge(s_y, st["y0"] + KD * h + k + 1)
                    act.activation(x_hi[:, k, half_cols(T, h)], mix[:, k, half_cols(T, h)], ACT.Copy)\
                        .then_inc(s_xhi, 1)
                root(0, s_sqp, st["s0"] + KD, 2, s_root2, 4 * st["i0"])
                for k in range(KD):
                    high(0, k)
                for k in range(KD):
                    square(st, 1, k)
                root(1, s_sqp, st["s0"] + 2 * KD, 3, s_root2, 4 * st["i0"] + 2)
                for k in range(KD):
                    high(1, k)
                if len(st["outs"]) > 1:
                    for k in range(KD):
                        act.wait_ge(s_y, st["y0"] + 2 * KD + k + 1)
                        act.activation(h_hi[:, k, :], h_mix[:, k, :], ACT.Copy).then_inc(s_hhi, 1)

            def renorm(st):
                for k in range(KD):
                    square(st, 0, k)
                next_input(st)

            def hgrn(st):
                def products(n, odd):
                    out = (
                        lambda p: (past(act, G["qin"], n), act.activation(sbv(g_q, T), p, ACT.Copy)),
                        lambda p: (past(act, G["c"], n), act.activation(sbv(g_b, T), p, ACT.Sigmoid)),
                        lambda p: (past(act, G["turn"], n), act.activation(sbv(g_v, T), p, ACT.Copy)),
                        lambda p: (past(act, G["og"], 2 * n - 2 if not isinstance(n, int) or n > 1 else 0),
                                   act.activation(sbv(g_gate[:, odd, :], T), p, ACT.Silu)),
                    )
                    return out

                def take(n, odd, j):
                    split(st["u0"] + 4 * n + j + AHEAD, (st["u0"] + j + AHEAD) % RING)
                    act.wait_ge(s_unit, st["u0"] + 4 * n + j + 1)
                    p = psv(j % 2, T)
                    products(n, odd)[j](p)[1].then_inc(s_evac, 1)

                def decays(n):
                    act.wait_ge(G["k"], n + 1)
                    act.activation(g_b[:, :], g_b[:, :], ACT.Ln).then_inc(G["ln"], 1)
                    act.wait_ge(G["c"], n + 1)
                    past(act, G["state"], NCH * n)
                    act.activation(g_eb[:, :], g_c[:, :], ACT.Exp).then_inc(G["eb"], 1)
                    past(act, G["score"], n)
                    act.activation(g_kin[:, :], g_c[:, :], ACT.Exp, scale=-1.0).then_inc(G["enb"], 1)
                    act.wait_ge(G["d"], n + 1)
                    act.activation(g_kout[:, :], g_kout[:, :], ACT.Exp).then_inc(G["ed"], 1)

                def copies(n):
                    act.wait_ge(G["turn"], n + 1)
                    act.activation(g_kt[:, :, :], ps[:, 4, :].rearrange("p (b n) -> p b n", n=P), ACT.Copy)\
                        .then_inc(G["kt"], 1)
                    past(act, G["o"], n)
                    act.activation(g_vt[:, :, :], ps[:, 5, :].rearrange("p (b n) -> p b n", n=P), ACT.Copy)\
                        .then_inc(G["vt"], 1)

                def squares(n):
                    act.wait_ge(G["oe"], 2 * n + 2)
                    past(act, G["ms"], n)
                    act.activation(pair[:, 0, :], g_o[:, :], ACT.Square).then_inc(G["sq"], 1)

                def root(n):
                    act.wait_ge(G["eps"], n + 1)
                    act.activation(g_rs[:, :], g_rs[:, :], ACT.Ln).then_inc(G["lnr"], 1)
                    act.wait_ge(G["lnr"], n + 1)
                    act.activation(g_rs[:, :], g_rs[:, :], ACT.Exp, scale=-0.5).then_inc(G["rs"], 1)

                def high(n):
                    act.wait_ge(G["og"], 2 * n + 2)
                    act.activation(h_hi[:, bass.ds(n, 1), :].rearrange("p a t -> p (a t)"), g_o[:, :], ACT.Copy)\
                        .then_inc(s_hhi, 1)

                def step(n, odd, before, before2):
                    if before:
                        decays(n - 1)
                    take(n, odd, 0)
                    if before2:
                        root(n - 2)
                        high(n - 2)
                    take(n, odd, 1)
                    if before:
                        copies(n - 1)
                    take(n, odd, 2)
                    take(n, odd, 3)
                    if before:
                        squares(n - 1)

                act.wait_ge(G["lb"], 3)
                act.activation(g_lb[:, 0:2, :], g_lb[:, 0:2, :], ACT.Exp).then_inc(G["lb"], 1)
                step(0, 0, False, False)
                step(1, 1, True, False)
                step(2, 0, True, True)
                step(3, 1, True, True)
                with act.Fori(2, KD // 2) as i:
                    step(2 * i, 0, True, True)
                    step(2 * i + 1, 1, True, True)
                decays(KD - 1)
                root(KD - 2)
                high(KD - 2)
                copies(KD - 1)
                squares(KD - 1)
                root(KD - 1)
                high(KD - 1)

            def fox_values(st):
                z = f_b[:, :, :]
                for n in range(1 + KD):
                    split(st["u0"] + n + AHEAD, (st["u0"] + n + AHEAD) % RING)
                    act.wait_ge(s_unit, st["u0"] + n + 1)
                    src = psv(n % 2, T)
                    if n == 0:
                        act.activation(sbv(z[:, 0, :], T), src, ACT.Identity,
                                       bias=par[:, PARAM["fg_b"]:PARAM["fg_b"] + 1]).then_inc(s_evac, 1)
                        continue
                    v = n - 1
                    if v >= 2:
                        act.wait_ge(FX["vtr"], v - 1)
                    act.activation(sbv(pair[:, v % 2, :], T), src, ACT.Copy).then_inc(s_evac, 1)
                    if n == 1:
                        act.wait_ge(FX["c"], 1)
                        act.activation(z[:, 1, :], z[:, 1, :], ACT.Exp, scale=-1.0).then_inc(FX["c"], 1)
                    if n == 2:
                        act.wait_ge(FX["c"], 3)
                        act.activation(z[:, 1, :], z[:, 1, :], ACT.Ln).then_inc(FX["c"], 1)

            def fox(st):
                def job(p, m, only_from=0):
                    if only_from < 2 and back(p, m, 1):
                        pp, mm = back(p, m, 1)
                        b = FOX_JOBS[mm][1]
                        act.wait_ge(FX["pT"], NJ * pp + mm + 1)
                        if back(pp, mm, 2):
                            act.wait_ge(FX["pv"], NJ * pp + mm - 1)
                        if b:
                            act.activation(f_probT[:, mm % 2, 1:1 + b, :],
                                           ps[:, 4, 0:P * b].rearrange("p (j n) -> p j n", n=P), ACT.Copy)
                        act.activation(f_probT[0:META, mm % 2, 0, :], ps[0:META, 5, 0:P], ACT.Copy)\
                            .then_inc(FX["pTe"], 1)
                    if only_from < 1:
                        a = NJ * p + m
                        nk = fox_block(FOX_JOBS[m][1])[1]
                        bank = 6 if m % 2 else 2
                        s = ps[:, bank:bank + 2, :].rearrange("p a n -> p (a n)")[:, 0:nk]
                        act.wait_ge(FX["max"], a + 1)
                        if back(p, m, 2):
                            act.wait_ge(FX["pT"], a - 1)
                            act.wait_ge(FX["rec"], a - 1)
                        act.activation(f_prob[:, m % 2, 0:nk], s, ACT.Exp, bias=stat[:, m % 2:m % 2 + 1],
                                       accum_out=stat[:, 2 + m % 2:3 + m % 2]).then_inc(FX["exp"], 1)

                def pair_step(p, q, buf, jobs):
                    for c in range(1, 2 * KD + 1):
                        if c % KD == 0:
                            j = c // KD - 1
                            v = 2 * p + j
                            split(st["u0"] + v + AHEAD, (st["u0"] + 2 * q + j + AHEAD) % RING)
                            act.wait_ge(s_unit, st["u0"] + v + 1)
                            if not (isinstance(p, int) and p < 2):
                                act.wait_ge(FX["score"], NJ * (p - 1))
                            act.activation(sbv(f_qk[:, buf, j, :], T), psv(0, T), ACT.Copy,
                                           scale=HD ** -0.5 if j else 1.0).then_inc(s_evac, 1)
                        if jobs and c in FOX_AT:
                            job(p - 1, FOX_AT[c])

                pair_step(0, 0, 0, False)
                pair_step(1, 1, 1, True)
                pair_step(2, 2, 0, True)
                with act.Fori(1, KD // 2 - 1) as i:
                    pair_step(2 * i + 1, 1, 1, True)
                    pair_step(2 * i + 2, 2, 0, True)
                pair_step(KD - 1, KD - 1, 1, True)
                for m in range(NJ):
                    job(KD - 1, m)
                job(KD, 0, only_from=1)
                act.wait_ge(s_unit, st["u0"] + 2 * KD)
                for k in range(KD):
                    act.wait_ge(FX["oe"], 5 * (k + 1))
                    act.activation(h_hi[:, k, :], f_o[:, k, :], ACT.Copy).then_inc(s_hhi, 1)

            run = dict(load=load, glu=glu, project=project, pool_in=pool_in,
                       pool_group=pool_group, values1=values1, attend1=attend1, glu2=glu2, project2=project2,
                       renorm=renorm, hgrn=hgrn, fox_values=fox_values, fox=fox)
            for st in STAGES:
                if st["kind"] in run:
                    run[st["kind"]](st)

        @block.vector
        def _(dve):
            def split(u, slot):
                if isinstance(u, int) and u >= UNITS:
                    return
                dve.wait_ge(s_hi, u + 1)
                if not (isinstance(u, int) and u < RING):
                    dve.wait_ge(s_unit, u - RING + 1)
                dve.tensor_tensor(w_lo[:, slot], raw[:, slot], w_hi[:, slot].bitcast(F32), ALU.subtract)\
                    .then_inc(s_lo, 1)

            def split_ahead(st, i, per, j):
                if isinstance(i, int) and i == 0 and j < st.get("led", 0):
                    return
                u = st["u0"] + per * i + j + AHEAD
                split(u, u % RING if isinstance(u, int) else (st["u0"] + j + AHEAD) % RING)

            def load(st):
                dve.memset(eps[:, :], EPS).then_inc(s_eps, 1)
                split(0, 0)
                for h in range(2):
                    for k in range(KD):
                        dve.wait_ge(s_xhi, KD * h + k + 1)
                        c = half_cols(S, h)
                        dve.tensor_tensor(x_lo[:, k, c], res[:, k, c], x_hi[:, k, c].bitcast(F32), ALU.subtract)\
                            .then_inc(s_xlo, 1)
                    for u in (1, 2) if h == 0 else (3,):
                        split(u, u)

            def glu(st):
                def body(i):
                    for f in range(2):
                        k = 2 * i + f
                        slot = (2 * f + 1) % RING
                        split_ahead(st, i, 4, 2 * f)
                        dve.wait_ge(s_silu, st["g0"] + k + 1)
                        dve.wait_ge(s_unit, st["u0"] + 4 * i + 2 * f + 2)
                        dve.tensor_tensor(pair[:, f, META:T], pair[:, f, META:T], psv(slot), ALU.mult)\
                            .then_inc(s_evac, 2)
                        split_ahead(st, i, 4, 2 * f + 1)
                        dve.wait_ge(s_hhi, st["h0"] + k + 1)
                        h = bass.ds(k, 1)
                        dve.tensor_tensor(h_lo[:, h, META:T].rearrange("p a t -> p (a t)"), pair[:, f, META:T],
                                          h_hi[:, h, META:T].rearrange("p a t -> p (a t)").bitcast(F32),
                                          ALU.subtract).then_inc(s_hlo, 1)
                body(0)
                with dve.Fori(1, KF // 2) as i:
                    body(i)

            def project(st):
                chunks, full, m = st["chunks"], KD - st["halved"], st["halved"]
                cleared = st["q0"] + 1
                dve.memset(sums[:, :, :], 0.0).then_inc(s_sum, 1)
                if not st["n0"]:
                    dve.wait_ge(s_res, KD + 1)

                def take(k, h, before, taken, count):
                    c = slice(META, T) if h is None else half_cols(S, h)
                    src = psv(k % RING) if h is None else half_bank(k % RING, S, h)
                    z = res[:, k, c]
                    dve.scalar_tensor_tensor(out=z, in0=src, scalar=st["coef"], in1=z, op0=ALU.mult, op1=ALU.add)\
                        .then_inc(taken, 1)
                    dve.wait_ge(taken, count)
                    dve.wait_ge(s_sum, cleared + 2 * before)
                    dve.tensor_tensor(sums[:, 0, c], sums[:, 0, c], z, ALU.add).then_inc(s_sum, 1)
                    dve.wait_ge(s_sq, st["p0"] + before + 1)
                    dve.tensor_tensor(sums[:, 1, c], sums[:, 1, c], pair[:, 0, c], ALU.add).then_inc(s_sum, 1)

                def late_tile(q):
                    dve.wait_ge(s_unit, st["u0"] + len(chunks) * (full + q + 1))
                    take(full + q, 1, full + m + q, s_evac, st["t0"] + full + q + 1)

                def variance(h):
                    v, r = 10 * st["n0"] + 5 * h, rstd[:, half_cols(S, h)]
                    dve.wait_ge(s_var, v + 1)
                    dve.wait_ge(s_stat, 4 * st["n0"] + 2 * h + 2)
                    dve.tensor_tensor(r, ps[:, 2 + h, 0:S // 2], pair[:, 1, half_cols(S, h)], ALU.subtract)\
                        .then_inc(s_var, 1)
                    dve.wait_ge(s_var, v + 2)
                    dve.tensor_scalar(r, r, 0.0, LN_EPS, ALU.max, ALU.add).then_inc(s_var, 1)

                def normalise(h, k):
                    n, c = 2 * KD * st["n0"] + KD * h + k + 1, half_cols(S, h)
                    if k == 0:
                        dve.wait_ge(s_var, 10 * st["n0"] + 5 * h + 5)
                    dve.wait_ge(s_cen, n)
                    dve.tensor_tensor(res[:, k, c], res[:, k, c], rstd[:, c], ALU.mult).then_inc(s_nrm, 1)

                def affine(h, k):
                    if not 0 <= k < KD or not st["scaled"] or k in ON_SCALAR:
                        return
                    c, gain, bias = half_cols(S, h), f"ln_gain{st['l']}{st['j']}", f"ln_bias{st['l']}{st['j']}"
                    dve.wait_ge(s_xhi, st["x0"] + KD * h + k + 1)
                    dve.tensor_scalar(res[:, k, c], res[:, k, c], scaled_of(gain, k), scaled_of(bias, k),
                                      ALU.mult, ALU.add).then_inc(s_affv, 1)

                def low(h, k):
                    if k < 0 or not st["scaled"]:
                        return
                    c = half_cols(S, h)
                    if k in ON_SCALAR:
                        dve.wait_ge(s_affs, len(ON_SCALAR) * (2 * st["n0"] + h) + ON_SCALAR.index(k) + 1)
                    else:
                        dve.wait_ge(s_affv, (KD - len(ON_SCALAR)) * (2 * st["n0"] + h) +
                                    sum(i not in ON_SCALAR for i in range(k + 1)))
                    dve.scalar_tensor_tensor(out=x_lo[:, k, c], in0=res[:, k, c], scalar=1.0 / ALPHA,
                                             in1=x_hi[:, k, c].bitcast(F32), op0=ALU.mult, op1=ALU.subtract)\
                        .then_inc(s_xlo, 1)

                def step(h, k):
                    if k < KD:
                        normalise(h, k)
                    affine(h, k - 1)
                    low(h, k - 2)

                for k in range(full):
                    for c in range(len(chunks)):
                        split_ahead(st, k, len(chunks), c)
                    dve.wait_ge(s_unit, st["u0"] + len(chunks) * (k + 1))
                    take(k, None, k, s_evac, st["t0"] + k + 1)
                for u in own_units(st):
                    split(u, u % RING)
                for q in range(m):
                    dve.wait_ge(s_ua, st["e0"] + len(chunks) * (q + 1))
                    take(full + q, 0, full + q, s_za, st["z0"] + q + 1)
                variance(0)
                beside(st, -1, late_tile)
                for k in range(KD):
                    step(0, k)
                    beside(st, k - 1, split=split)
                    beside(st, k, late_tile)
                step(0, KD)
                step(0, KD + 1)
                variance(1)
                for k in range(KD + 2):
                    step(1, k)

            def pool_in(st):
                def mixed(n):
                    g = n // 2
                    w, done = POOL_WINDOWS[g], win_steps(n)
                    h = w // 2
                    dve.wait_ge(s_evac, st["t0"] + n + 1)
                    src, width, step = upad[:, n % 2, PAD - h:PAD - h + S + w - 1], S + w - 1, 1
                    while step < w:
                        width = S + w - 2 * step
                        dst = win[:, done % 2, 0:width]
                        if done:
                            dve.wait_ge(s_win, done)
                        dve.tensor_tensor(dst, src[:, 0:width], src[:, step:step + width], ALU.add).then_inc(s_win, 1)
                        src, step, done = dst, 2 * step, done + 1
                    dve.wait_ge(s_win, done)
                    dst = win[:, done % 2, 0:S]
                    dve.tensor_tensor(dst, src, invc[:, g, :], ALU.mult).then_inc(s_win, 1)
                    done += 1
                    dve.wait_ge(s_win, done)
                    dve.tensor_tensor(pair[:, n % 2, META:T], dst, upad[:, n % 2, PAD:PAD + S], ALU.subtract)\
                        .then_inc(s_win, 1)

                def low(n):
                    dve.wait_ge(s_hhi, st["h0"] + n + 1)
                    dve.tensor_tensor(h_lo[:, n, META:T], pair[:, n % 2, META:T], h_hi[:, n, META:T].bitcast(F32),
                                      ALU.subtract).then_inc(s_hlo, 1)

                dve.wait_ge(s_tab, 16)
                for n in range(KD):
                    split_ahead(st, 0, 1, n)
                    mixed(n)
                    if n >= 1:
                        low(n - 1)
                low(KD - 1)

            def pool_group(st):
                for v in range(2):
                    split(st["u0"] + v + AHEAD, (st["u0"] + v + AHEAD) % RING)
                    for n in range(4 * v, 4 * v + 4):
                        dve.wait_ge(s_hhi, st["h0"] + n + 1)
                        dve.tensor_tensor(h_lo[:, KD + n, META:T], pair[:, n % 2, META:T],
                                          h_hi[:, KD + n, META:T].bitcast(F32), ALU.subtract).then_inc(s_hlo, 1)

            def values1(st):
                def store(v, j):
                    dve.wait_ge(s_vtr, v + 1)
                    dve.tensor_copy(val[:, :, bass.ds(v * P, P)],
                                    ps[:, 1 + 2 * (j % 2), :].rearrange("p (r n) -> p r n", r=R4)).then_inc(s_val, 1)

                def body(i):
                    for j in range(4):
                        split_ahead(st, i, 4, j)
                        if not (isinstance(i, int) and j == 0):
                            store(4 * i + j - 1, (j - 1) % 4)
                body(0)
                with dve.Fori(1, 3 * KD // 4) as i:
                    body(i)
                store(3 * KD - 1, 3)

            def attend1(st):
                def job(p, m, only_from=0):
                    a = 8 * p + m
                    r, half = m // 2, m % 2
                    if only_from < 1:
                        slope = slopes[:, bass.ds(2 * p + half, 1)]
                        dve.wait_ge(s_score, a + 1)
                        if not (isinstance(a, int) and a < 1):
                            dve.wait_ge(s_pT, a)
                        dve.scalar_tensor_tensor(out=prob[:, 0:S], in0=near[:, R4 - 1 - r:R4 - 1 - r + S], scalar=slope,
                                                 in1=ps[:, 1, :], op0=ALU.mult, op1=ALU.add)
                        dve.scalar_tensor_tensor(out=prob[:, S:S + 2 * NI], in0=far[:, :], scalar=slope,
                                                 in1=ps[:, 3, 0:2 * NI], op0=ALU.mult, op1=ALU.add).then_inc(s_bias, 1)
                        dve.wait_ge(s_bias, a + 1)
                        dve.tensor_reduce(stat[:, half:half + 1], prob[:, :], AX_X, ALU.max, negate=True)\
                            .then_inc(s_max, 1)
                    if only_from < 2 and not (isinstance(a, int) and a < 1):
                        dve.wait_ge(s_exp, a)
                        if not (isinstance(a, int) and a < 3):
                            dve.wait_ge(s_on, a - 2)
                        dve.reciprocal(stat[:, 5 - half:6 - half], stat[:, 3 - half:4 - half]).then_inc(s_rec, 1)
                    if only_from < 3 and not (isinstance(a, int) and a < 2):
                        if not (isinstance(a, int) and a < 6):
                            dve.wait_ge(s_oT, 4 * p + (m - 2) // 2 - 1)
                        dve.wait_ge(s_pv, a - 1)
                        dve.wait_ge(s_rec, a - 1)
                        dve.tensor_scalar(o_tok[:, (r - 1) % 2, half * HD:(half + 1) * HD],
                                          ps[:, 6, half * HD:(half + 1) * HD], stat[:, 4 + half:5 + half], None,
                                          ALU.mult).then_inc(s_on, 1)
                    if half == 0 and not (isinstance(a, int) and a < 4):
                        c = 4 * p + m // 2 - 2
                        rc = (m // 2 - 2) % R4
                        dve.wait_ge(s_oT, c + 1)
                        dst = att[:, bass.ds(p if m >= 4 else p - 1, 1), :].rearrange("p a (i r) -> p (a i) r", r=R4)
                        dve.tensor_copy(dst[:, :, rc], ps[:, 7, 0:P]).then_inc(s_oe, 1)

                def pair_step(p, q, jobs):
                    for c in range(1, 25):
                        if c % 4 == 0:
                            j = c // 4 - 1
                            split(st["u0"] + 6 * p + j + AHEAD, (st["u0"] + 6 * q + j + AHEAD) % RING)
                        if c % 3 == 0 and jobs:
                            job(p - 1, c // 3 - 1)

                dve.wait_ge(s_tab, 3 * 16)
                pair_step(0, 0, False)
                pair_step(1, 1, True)
                pair_step(2, 2, True)
                with dve.Fori(1, KD // 2 - 1) as i:
                    pair_step(2 * i + 1, 1, True)
                    pair_step(2 * i + 2, 2, True)
                pair_step(KD - 1, KD - 1, True)
                for m in range(8):
                    job(KD - 1, m)
                for m in range(3):
                    job(KD, m, only_from=m + 1)
                for k in range(KD):
                    dve.wait_ge(s_xhi, st["x0"] + k + 1)
                    dve.tensor_tensor(x_lo[:, k, META:T], att[:, k, :], x_hi[:, k, META:T].bitcast(F32),
                                      ALU.subtract).then_inc(s_xlo, 1)

            def glu2(st):
                taps = {part: [f"conv{st['l']}{part}{tap}" for tap in range(3)] for part in "gv"}

                def convolve(part, k, c):
                    q = "gv".index(part)
                    src, dst = upad2[:, q, :], pair[:, q, :]

                    def tap(n):
                        at_ = PARAM[taps[part][n]]
                        return par[:, bass.ds(k + at_, 1)]
                    done = 6 * c + 3 * q
                    dve.tensor_scalar(dst, src[:, 2:2 + T], tap(2), None, ALU.mult).then_inc(s_cv, 1)
                    for n in (1, 0):
                        dve.wait_ge(s_cv, done + 2 - n)
                        dve.scalar_tensor_tensor(out=dst, in0=src[:, n:n + T], scalar=tap(n), in1=dst,
                                                 op0=ALU.mult, op1=ALU.add).then_inc(s_cv, 1)

                def low(k):
                    dve.wait_ge(s_hhi, st["h0"] + k + 1)
                    h = bass.ds(k, 1)
                    dve.tensor_tensor(h_lo[:, h, :].rearrange("p a t -> p (a t)"), pair[:, 1, :],
                                      h_hi[:, h, :].rearrange("p a t -> p (a t)").bitcast(F32),
                                      ALU.subtract).then_inc(s_hlo, 1)

                def body(i):
                    for f in range(2):
                        k = 2 * i + f
                        c = st["c0"] + k
                        split_ahead(st, i, 4, 2 * f)
                        dve.wait_ge(s_evac, st["t0"] + 4 * i + 2 * f + 1)
                        past(dve, s_h, c)
                        convolve("g", k, c)
                        if not (isinstance(k, int) and k < 1):
                            low(k - 1)
                        split_ahead(st, i, 4, 2 * f + 1)
                        dve.wait_ge(s_evac, st["t0"] + 4 * i + 2 * f + 2)
                        if not (isinstance(k, int) and k < 1):
                            dve.wait_ge(s_hlo, st["h0"] + k)
                        convolve("v", k, c)
                        dve.wait_ge(s_gate, c + 1)
                        dve.wait_ge(s_cv, 6 * c + 6)
                        dve.tensor_tensor(pair[:, 1, :], pair[:, 0, :], pair[:, 1, :], ALU.mult).then_inc(s_h, 1)
                dve.wait_ge(s_zero, 1)
                body(0)
                with dve.Fori(1, KF // 2) as i:
                    body(i)
                low(KF - 1)

            def project2(st):
                chunks, full, m = st["chunks"], KD - st["halved"], st["halved"]
                dve.memset(sums[:, 1, :], 0.0).then_inc(s_sum2, 1)

                def add_square(h, before):
                    c = slice(0, T) if h is None else half_cols(T, h)
                    dve.wait_ge(s_mixed, st["w0"] + before + 1)
                    dve.wait_ge(s_sum2, st["j0"] + 1 + before)
                    dve.tensor_tensor(sums[:, 1, c], sums[:, 1, c], pair[:, 0, c], ALU.add).then_inc(s_sum2, 1)

                def late_tile(q):
                    add_square(1, full + m + q)

                def normalise(h, k):
                    c = half_cols(T, h)
                    if k == 0:
                        dve.wait_ge(s_root1, 4 * st["v0"] + 2 * h + 2)
                    dve.scalar_tensor_tensor(out=mix[:, k, c], in0=mix[:, k, c], scalar=par_of(st["after"], k),
                                             in1=rstd[:, c], op0=ALU.mult, op1=ALU.mult).then_inc(s_mx, 1)

                for k in range(full):
                    for c in range(len(chunks)):
                        split_ahead(st, k, len(chunks), c)
                    add_square(None, k)
                for u in own_units(st):
                    split(u, u % RING)
                for q in range(m):
                    add_square(0, full + q)
                beside(st, -1, late_tile)
                for k in range(KD):
                    normalise(0, k)
                    beside(st, k - 1, split=split)
                    beside(st, k, late_tile)
                if st["outs"]:
                    next_input(st, lambda k: normalise(1, k))
                else:
                    for k in range(KD):
                        normalise(1, k)

            def next_input(st, other=None):
                name = st["outs"][0][0]
                for h in range(2):
                    c = half_cols(T, h)
                    if h == 0 and other:
                        other(0)
                    dve.wait_ge(s_root2, 4 * st["i0"] + 2 * h + 2)
                    for k in range(KD + 1):
                        if k < KD:
                            dve.scalar_tensor_tensor(out=mix[:, k, c], in0=res[:, k, c], scalar=par_of(name, k),
                                                     in1=rstd[:, c], op0=ALU.mult, op1=ALU.mult).then_inc(s_y, 1)
                        if k:
                            dve.wait_ge(s_xhi, st["x0"] + KD * h + k)
                            dve.tensor_tensor(x_lo[:, k - 1, c], mix[:, k - 1, c], x_hi[:, k - 1, c].bitcast(F32),
                                              ALU.subtract).then_inc(s_xlo, 1)
                        if h == 0 and other and k + 1 < KD:
                            other(k + 1)
                if len(st["outs"]) > 1:
                    name = st["outs"][1][0]
                    for k in range(KD + 2):
                        if k < KD:
                            dve.scalar_tensor_tensor(out=h_mix[:, k, :], in0=res[:, k, :], scalar=par_of(name, k),
                                                     in1=rstd[:, :], op0=ALU.mult, op1=ALU.mult).then_inc(s_y, 1)
                        if k >= 2:
                            dve.wait_ge(s_hhi, st["h0"] + k - 1)
                            dve.tensor_tensor(h_lo[:, k - 2, :], h_mix[:, k - 2, :], h_hi[:, k - 2, :].bitcast(F32),
                                              ALU.subtract).then_inc(s_hlo, 1)

            def renorm(st):
                next_input(st)

            def hgrn(st):
                one_less = 3

                def bounds():
                    l = [par[:, PARAM[f"lb{q}"]:PARAM[f"lb{q}"] + KD] for q in range(2)]
                    dve.tensor_tensor(g_lb[:, 2, :], l[0], l[1], ALU.max).then_inc(G["lb"], 1)
                    dve.wait_ge(G["lb"], 1)
                    for q in range(2):
                        dve.tensor_tensor(g_lb[:, q, :], l[q], g_lb[:, 2, :], ALU.subtract).then_inc(G["lb"], 1)
                    dve.wait_ge(G["lb"], 4)
                    dve.tensor_tensor(g_lb[:, 2, :], g_lb[:, 0, :], g_lb[:, 1, :], ALU.add).then_inc(G["lb"], 1)
                    dve.wait_ge(G["lb"], 5)
                    dve.reciprocal(g_lb[:, 2, :], g_lb[:, 2, :]).then_inc(G["lb"], 1)
                    dve.wait_ge(G["lb"], 6)
                    dve.tensor_tensor(g_lb[:, 0, :], g_lb[:, 0, :], g_lb[:, 2, :], ALU.mult).then_inc(G["lb"], 1)
                    dve.wait_ge(G["lb"], 7)
                    dve.tensor_scalar(g_lb[:, one_less, :], g_lb[:, 0, :], -1.0, 1.0, ALU.mult, ALU.add)\
                        .then_inc(G["lb"], 1)
                    dve.wait_ge(G["lb"], 8)

                def forget(n):
                    dve.wait_ge(s_evac, st["t0"] + 4 * n + 2)
                    dve.tensor_scalar(g_b[:, :], g_b[:, :], g_lb[:, one_less, bass.ds(n, 1)], g_lb[:, 0, bass.ds(n, 1)],
                                      ALU.mult, ALU.add).then_inc(G["f"], 1)
                    dve.wait_ge(G["f"], n + 1)
                    past(dve, G["kout"], n)
                    dve.tensor_scalar(g_k[:, :], g_b[:, :], -1.0, 1.0, ALU.mult, ALU.add).then_inc(G["k"], 1)

                def decays(n):
                    dve.wait_ge(G["ln"], n + 1)
                    dve.tensor_tensor_scan(g_c[:, :], g_chunk[:, :], g_b[:, :], 0.0, ALU.mult, ALU.add)\
                        .then_inc(G["c"], 1)
                    dve.wait_ge(G["c"], n + 1)
                    past(dve, G["turn"], n)
                    dve.tensor_scalar(g_kout[:, 0:META], g_c[:, 0:META], g_c[:, META - 1:META], -1.0,
                                      ALU.subtract, ALU.mult)
                    c3 = g_c[:, META:T].rearrange("p (j t) -> p j t", t=CH)
                    dve.tensor_tensor(g_kout[:, META:T].rearrange("p (j t) -> p j t", t=CH),
                                      c3[:, :, CH - 1:CH].to_broadcast([P, NCH, CH]), c3, ALU.subtract)\
                        .then_inc(G["d"], 1)
                    dve.wait_ge(G["eb"], n + 1)
                    past(dve, G["o"], n)
                    dve.tensor_tensor(g_qin[:, :], g_q[:, :], g_eb[:, :], ALU.mult).then_inc(G["qin"], 1)
                    dve.wait_ge(G["enb"], n + 1)
                    dve.tensor_tensor(g_kin[:, :], g_kin[:, :], g_k[:, :], ALU.mult).then_inc(G["kin"], 1)
                    dve.wait_ge(G["ed"], n + 1)
                    dve.tensor_tensor(g_kout[:, :], g_kout[:, :], g_k[:, :], ALU.mult).then_inc(G["kout"], 1)

                def clip(n):
                    dve.wait_ge(G["score"], n + 1)
                    past(dve, G["o"], n)
                    dve.tensor_copy(g_mt[:, :, :], ps[0:META, 6, 0:2 * P].rearrange("p (b n) -> p b n", n=P))\
                        .then_inc(G["mt"], 1)
                    dve.tensor_tensor(g_at[:, :, :].rearrange("p a b -> p (a b)"), ps[:, 7, :], g_keep[:, 0, :], ALU.min)
                    dve.tensor_tensor(g_atm[:, :], ps[0:META, 6, 2 * P:2 * P + META], g_keep[0:META, 0, 0:META], ALU.min)\
                        .then_inc(G["clip"], 1)
                    dve.wait_ge(G["clip"], n + 1)
                    dve.tensor_tensor(g_at[:, :, :].rearrange("p a b -> p (a b)"),
                                      g_at[:, :, :].rearrange("p a b -> p (a b)"), g_keep[:, 1, :], ALU.max)
                    dve.tensor_tensor(g_atm[:, :], g_atm[:, :], g_keep[0:META, 1, 0:META], ALU.max).then_inc(G["at"], 1)

                def states(n):
                    dve.wait_ge(G["ds"], n + 1)
                    dve.tensor_copy(g_state[:, 0, :], ps[:, 6, 0:P]).then_inc(G["state"], 1)
                    for j in range(NCH - 1):
                        dve.wait_ge(G["state"], NCH * n + j + 1)
                        last = META + CH * j + CH - 1
                        dve.scalar_tensor_tensor(out=g_state[:, j + 1, :], in0=g_state[:, j, :],
                                                 scalar=g_eb[:, last:last + 1],
                                                 in1=ps[:, 4 + j % 2, P * (j // 2):P * (j // 2) + P],
                                                 op0=ALU.mult, op1=ALU.add).then_inc(G["state"], 1)

                def take(n):
                    dve.wait_ge(G["o"], n + 1)
                    if not (isinstance(n, int) and n < 1):
                        dve.wait_ge(s_hlo, st["h0"] + n)
                    dve.tensor_copy(g_o[:, 0:META], ps[:, 6, 0:META]).then_inc(G["oe"], 1)
                    dve.tensor_copy(g_o[:, META:T], ps[:, 7, :]).then_inc(G["oe"], 1)

                def finish(n, odd):
                    dve.wait_ge(G["rs"], n + 1)
                    dve.scalar_tensor_tensor(out=g_o[:, :], in0=g_o[:, :],
                                             scalar=par[:, bass.ds(n + PARAM["head_norm"], 1)], in1=g_rs[:, :],
                                             op0=ALU.mult, op1=ALU.mult).then_inc(G["og"], 1)
                    dve.wait_ge(G["og"], 2 * n + 1)
                    dve.tensor_tensor(g_o[:, :], g_o[:, :], g_gate[:, odd, :], ALU.mult).then_inc(G["og"], 1)
                    dve.wait_ge(s_hhi, st["h0"] + n + 1)
                    h = bass.ds(n, 1)
                    dve.tensor_tensor(h_lo[:, h, :].rearrange("p a t -> p (a t)"), g_o[:, :],
                                      h_hi[:, h, :].rearrange("p a t -> p (a t)").bitcast(F32),
                                      ALU.subtract).then_inc(s_hlo, 1)

                def with_eps(n):
                    dve.wait_ge(G["ms"], n + 1)
                    past(dve, G["og"], 2 * n)
                    dve.tensor_scalar(sbv(g_rs, T), psv(2, T), float(D // P), EPS, ALU.mult, ALU.add)\
                        .then_inc(G["eps"], 1)

                def step(n, odd, before, before2):
                    if before:
                        decays(n - 1)
                    split(st["u0"] + 4 * n + 0 + AHEAD, (st["u0"] + 0 + AHEAD) % RING)
                    if before2:
                        with_eps(n - 2)
                        finish(n - 2, odd)
                    split(st["u0"] + 4 * n + 1 + AHEAD, (st["u0"] + 1 + AHEAD) % RING)
                    forget(n)
                    if before:
                        clip(n - 1)
                    split(st["u0"] + 4 * n + 2 + AHEAD, (st["u0"] + 2 + AHEAD) % RING)
                    if before:
                        states(n - 1)
                    split(st["u0"] + 4 * n + 3 + AHEAD, (st["u0"] + 3 + AHEAD) % RING)
                    if before:
                        take(n - 1)

                bounds()
                dve.wait_ge(G["tab"], 32)
                dve.tensor_scalar(g_keep[:, 1, :], g_keep[:, 0, :], -1.0, None, ALU.mult).then_inc(G["neg"], 1)
                dve.wait_ge(G["neg"], 1)
                step(0, 0, False, False)
                step(1, 1, True, False)
                step(2, 0, True, True)
                step(3, 1, True, True)
                with dve.Fori(2, KD // 2) as i:
                    step(2 * i, 0, True, True)
                    step(2 * i + 1, 1, True, True)
                decays(KD - 1)
                with_eps(KD - 2)
                finish(KD - 2, 0)
                clip(KD - 1)
                states(KD - 1)
                take(KD - 1)
                with_eps(KD - 1)
                finish(KD - 1, 1)

            def fox_values(st):
                z = f_b[:, :, :]
                ones = sums[:, 0, :]
                dve.memset(ones, 1.0).then_inc(FX["one"], 1)

                def gates(step):
                    if step == 0:
                        dve.wait_ge(s_evac, st["t0"] + 1)
                        dve.scalar_tensor_tensor(out=z[:, 1, :], in0=z[:, 0, :], scalar=-1.0, in1=z[:, 0, :],
                                                 op0=ALU.mult, op1=ALU.max).then_inc(FX["c"], 1)
                    if step == 1:
                        dve.wait_ge(FX["c"], 2)
                        dve.tensor_scalar(z[:, 1, :], z[:, 1, :], 1.0, None, ALU.add).then_inc(FX["c"], 1)
                    if step == 2:
                        dve.wait_ge(FX["c"], 4)
                        dve.scalar_tensor_tensor(out=z[:, 1, :], in0=z[:, 0, :], scalar=0.0, in1=z[:, 1, :],
                                                 op0=ALU.min, op1=ALU.subtract).then_inc(FX["c"], 1)
                    if step == 3:
                        dve.wait_ge(FX["c"], 5)
                        dve.wait_ge(FX["one"], 1)
                        dve.tensor_tensor_scan(f_c[:, :], ones, z[:, 1, :], 0.0, ALU.mult, ALU.add)\
                            .then_inc(FX["c"], 1)
                        dve.wait_ge(FX["c"], 6)
                        dve.tensor_copy(f_a[:, :], f_c[:, :]).then_inc(FX["c"], 1)
                        dve.wait_ge(FX["c"], 7)
                        dve.memset(f_a[FG:2 * FG, :], -1.0).then_inc(FX["one"], 1)

                for n in range(1 + KD):
                    split(st["u0"] + n + AHEAD, (st["u0"] + n + AHEAD) % RING)
                    gates(n - 1)
                    if n >= 3:
                        store(n - 3)
                store(KD - 2)
                store(KD - 1)

            def store(v):
                dve.wait_ge(FX["vtr"], v + 1)
                dve.tensor_copy(f_val[:, :, P * v:P * v + P], ps[:, 4 + v % 2, :].rearrange("p (b n) -> p b n", n=P))
                dve.tensor_copy(f_vmeta[:, P * v:P * v + P], ps[0:META, 6 + v % 2, 0:P]).then_inc(FX["val"], 1)

            def fox(st):
                def key_side(p, half):
                    dve.tensor_scalar(f_b[:, half, :], f_c[:, :],
                                      ident[:, bass.ds(2 * p + (FG + half), 1)],
                                      ident[:, bass.ds(2 * p + half, 1)], ALU.mult, ALU.add)\
                        .then_inc(FX["b"], 1)

                def job(p, m, only_from=0):
                    a = NJ * p + m
                    if only_from < 1:
                        nk = fox_block(FOX_JOBS[m][1])[1]
                        bank = 6 if m % 2 else 2
                        s = ps[:, bank:bank + 2, :].rearrange("p a n -> p (a n)")[:, 0:nk]
                        if m == 2:
                            past(dve, FX["score"], NJ * p)
                            key_side(p, 1)
                        if m == 7 and not (isinstance(p, int) and p == KD - 1):
                            dve.wait_ge(FX["score"], NJ * p + 5)
                            key_side(p + 1, 0)
                        dve.wait_ge(FX["score"], a + 1)
                        if back(p, m, 2):
                            dve.wait_ge(FX["exp"], a - 1)
                        dve.tensor_reduce(stat[:, m % 2:m % 2 + 1], s, AX_X, ALU.max, negate=True)\
                            .then_inc(FX["max"], 1)
                    if only_from < 2 and back(p, m, 1):
                        mm = (m - 1) % NJ
                        dve.wait_ge(FX["exp"], a)
                        if back(p, m, 3):
                            dve.wait_ge(FX["on"], a - 2)
                        dve.reciprocal(stat[:, 4 + mm % 2:5 + mm % 2], stat[:, 2 + mm % 2:3 + mm % 2])\
                            .then_inc(FX["rec"], 1)
                    if only_from < 3 and back(p, m, 2):
                        mm = (m - 2) % NJ
                        half, b = FOX_JOBS[mm]
                        dve.wait_ge(FX["pv"], a - 1)
                        dve.wait_ge(FX["rec"], a - 1)
                        dve.tensor_scalar(f_otok[:, b, half * HD:(half + 1) * HD], ps[:, 7, 0:HD],
                                          stat[:, 4 + mm % 2:5 + mm % 2], None, ALU.mult).then_inc(FX["on"], 1)
                    if back(p, m, 3) and FOX_JOBS[(m - 3) % NJ][0]:
                        pp, mm = back(p, m, 3)
                        b = FOX_JOBS[mm][1]
                        q0, nq = fox_block(b)[0], P if b else META
                        dve.wait_ge(FX["oT"], out_count(pp, mm))
                        dve.tensor_copy(f_o[:, bass.ds(pp, 1), q0:q0 + nq].rearrange("p a n -> p (a n)"),
                                        ps[:, 7, P:P + nq]).then_inc(FX["oe"], 1)

                def pair_step(p, q, jobs):
                    for c in range(1, 2 * KD + 1):
                        if c % KD == 0:
                            j = c // KD - 1
                            split(st["u0"] + 2 * p + j + AHEAD, (st["u0"] + 2 * q + j + AHEAD) % RING)
                        if jobs and c in FOX_AT:
                            job(p - 1, FOX_AT[c])

                dve.wait_ge(FX["c"], 7)
                dve.wait_ge(FX["one"], 2)
                key_side(0, 0)
                pair_step(0, 0, False)
                pair_step(1, 1, True)
                pair_step(2, 2, True)
                with dve.Fori(1, KD // 2 - 1) as i:
                    pair_step(2 * i + 1, 1, True)
                    pair_step(2 * i + 2, 2, True)
                pair_step(KD - 1, KD - 1, True)
                for m in range(NJ):
                    job(KD - 1, m)
                for m in range(3):
                    job(KD, m, only_from=m + 1)
                for k in range(KD):
                    dve.wait_ge(s_hhi, st["h0"] + k + 1)
                    dve.tensor_tensor(h_lo[:, k, :], f_o[:, k, :], h_hi[:, k, :].bitcast(F32), ALU.subtract)\
                        .then_inc(s_hlo, 1)

            run = dict(load=load, glu=glu, project=project, pool_in=pool_in,
                       pool_group=pool_group, values1=values1, attend1=attend1, glu2=glu2, project2=project2,
                       renorm=renorm, hgrn=hgrn, fox_values=fox_values, fox=fox)
            for st in STAGES:
                if st["kind"] in run:
                    run[st["kind"]](st)

        @block.gpsimd
        def _(pool):
            def load(st):
                for k in range(KD):
                    pool.wait_ge(s_xlo, KD + k + 1)
                    pool.tensor_scalar(res[:, k, META:T], res[:, k, META:T], ALPHA, None, ALU.mult).then_inc(s_res, 1)
                pool.wait_ge(s_init, 5 * 16)
                pool.tensor_scalar(scaled[:, :], par[:, 0:2 * 3 * 2 * KD], ALPHA, None, ALU.mult).then_inc(s_res, 1)

            def centre(st):
                for h in range(2):
                    c = half_cols(S, h)
                    pool.wait_ge(s_var, 10 * st["n0"] + 5 * h + 1)
                    for k in range(KD):
                        pool.tensor_tensor(res[:, k, c], res[:, k, c], sums[:, 0, c], ALU.subtract).then_inc(s_cen, 1)

            def add_mixed(st):
                for h in range(2):
                    c = half_cols(T, h)
                    for k in range(KD):
                        pool.wait_ge(s_mx, st["a0"] + KD * h + k + 1)
                        pool.tensor_tensor(res[:, k, c], res[:, k, c], mix[:, k, c], ALU.add).then_inc(s_add, 1)

            for st in STAGES:
                if st["kind"] == "load":
                    load(st)
                if st["kind"] == "project":
                    centre(st)
                if st["kind"] == "project2":
                    add_mixed(st)
                if st["kind"] == "pool_in":
                    pool.memset(upad[:, :, :], 0.0).then_inc(s_pad, 1)
                    pool.dma_start(invc[:, :, :], consts[:, C_POOL:C_POOL + 4 * S].rearrange("p (g s) -> p g s", g=4))\
                        .then_inc(s_tab, 16)
                if st["kind"] == "hgrn":
                    pool.wait_ge(s_xlo, st["x0"])
                    pool.dma_start(g_chunk[:, :], consts[:, C_CHUNK:C_CHUNK + T]).then_inc(G["tab"], 16)
                    pool.dma_start(g_keep[:, 0, :], consts[:, C_KEEP:C_KEEP + S]).then_inc(G["tab"], 16)
                if st["kind"] == "fox_values":
                    pool.wait_ge(s_xlo, st["x0"])
                    pool.dma_start(f_mask[:, :], consts[:, C_CAUSAL:C_CAUSAL + P]).then_inc(FX["tab"], 16)
                if st["kind"] == "glu2" and not st["c0"]:
                    pool.memset(upad2[:, :, 0:2], 0.0).then_inc(s_zero, 1)
                if st["kind"] == "values1":
                    pool.dma_start(near[:, :], consts[:, C_NEAR:C_NEAR + N_NEAR]).then_inc(s_tab, 16)
                    pool.dma_start(far[:, :], consts[:, C_FAR:C_FAR + 2 * NI]).then_inc(s_tab, 16)


def win_steps(n):
    return sum(POOL_WINDOWS[k // 2].bit_length() - 1 + 2 for k in range(n))


def table(w):
    out = np.zeros((P, N_PARAM), np.float32)

    def put(name, v):
        n = -(-v.size // P)
        padded = np.zeros(n * P, np.float32)
        padded[:v.size] = v
        out[:, PARAM[name]:PARAM[name] + n] = padded.reshape(n, P).T

    for l in range(2):
        for j in range(3):
            put(f"ln_gain{l}{j}", w["ln_gain"][l, j])
            put(f"ln_bias{l}{j}", w["ln_bias"][l, j])
    put("pool_scale", w["pool_scale"][0])
    for l in range(2):
        for j in range(4):
            put(f"norm{l}{j}", w["norm_gains_2"][l, j])
        for tap in range(3):
            put(f"conv{l}g{tap}", w["ffn_conv_2"][l, tap, :FF2])
            put(f"conv{l}v{tap}", w["ffn_conv_2"][l, tap, FF2:])
        put(f"lb{l}", w["a_lb_logits_2"][l])
    put("head_norm", w["a_head_norm_2"][0])
    put("kv_norm", w["kv_norm_2"])
    for row in (0, FG):
        out[row:row + HEADS, PARAM["fg_b"]] = w["fg_b_2"]
    return out


def host_arrays(w):
    return dict(
        wstream=weight_stream(w),
        xT=np.ascontiguousarray(w["x"][0].T),
        metaT=np.ascontiguousarray(w["meta_tokens_2"].T),
        params=table(w),
        consts=constants(),
    )


def kernel(**inputs):
    import concourse.bacc as bacc
    from concourse.bass_utils import run_bass_kernel_spmd

    arrays = host_arrays({k: np.asarray(v) for k, v in inputs.items()})
    nc = bacc.Bacc("TRN2", target_bir_lowering=False, num_devices=1)
    args = [nc.dram_tensor(k, a.shape, F32, kind="ExternalInput").ap() for k, a in arrays.items()]
    out = nc.dram_tensor("out", (D, S), F32, kind="ExternalOutput").ap()
    build(nc, *args, out)
    r = run_bass_kernel_spmd(nc, [arrays], core_ids=[0])
    return np.ascontiguousarray(r.results[0]["out"].T)[None]
```
